# Optimizing a Trainium2 kernel written in Bass

```python
import math
import jax
import jax.numpy as jnp
from jax import lax
import numpy as np

D_MODEL = 1024
BATCH = 1
SEQ = 256
DEPTH = 2

GRID_W = 64
CTX_LEN = 256
EPS = 1e-6

POOL_WINDOWS = (2, 4, 8, 16)
POOL_GROUP = 64
POOL_WIDTH = POOL_GROUP * len(POOL_WINDOWS)

MLA_HEADS = 8
MLA_NOPE = 64
MLA_ROPE = 32
MLA_QK = MLA_NOPE + MLA_ROPE
MLA_V = 64
MLA_Q_RANK = 384
MLA_KV_RANK = 256
MLA_WIDTH = MLA_HEADS * MLA_V
MLA_SCALE = MLA_QK ** -0.5
ROPE_BASE = 10000.0
Q_BLOCK = 128

ML_HEADS = 4
ML_DK = 64
ML_DV = 64
ML_WIDTH = ML_HEADS * ML_DV
ML_CHUNK = 64
NEG_INIT = -1e30

MIX_WIDTH = POOL_WIDTH + MLA_WIDTH + ML_WIDTH

IN_SIZES = (POOL_WIDTH, MLA_Q_RANK, MLA_KV_RANK, MLA_ROPE, ML_WIDTH, ML_WIDTH, ML_WIDTH, ML_WIDTH, 4 * ML_HEADS)
IN_WIDTH = 1968

PEER_HEADS = 8
PEER_KEYS = 128
PEER_EXPERTS = PEER_KEYS * PEER_KEYS
PEER_DKEY = 256
PEER_TOPK = 16
PEER_BLOCK = 128

kernel_name = "hybrid_pool_mla_mlstm_peer_dit"

def rms_norm(x, gain):
    xf = x.astype(jnp.float32)
    y = xf * lax.rsqrt(jnp.mean(xf * xf, axis=-1, keepdims=True) + EPS)
    return (y * gain.astype(jnp.float32)).astype(x.dtype)

def modulate(x, gain, shift, scale):
    return rms_norm(x, gain) * (1 + scale) + shift

def ada_mod(cond, w, b):
    m = jax.nn.silu(cond) @ w + b
    return [t[:, None, :] for t in jnp.split(m, 6, axis=-1)]

def split_columns(z):
    parts, start = [], 0
    for size in IN_SIZES:
        parts.append(z[..., start:start + size])
        start += size
    return parts

def axial_rope_tables(n):
    n_rows = n // GRID_W
    row = jnp.repeat(jnp.arange(n_rows), GRID_W, total_repeat_length=n).astype(jnp.float32)
    col = (jnp.arange(n) % GRID_W).astype(jnp.float32)
    per_axis = MLA_ROPE // 2
    freqs = ROPE_BASE ** (-jnp.arange(0, per_axis, 2, dtype=jnp.float32) / per_axis)
    ang = jnp.concatenate([row[:, None] * freqs, col[:, None] * freqs], axis=-1)
    return jnp.cos(ang), jnp.sin(ang)

def apply_rope(x, cos, sin):
    half = MLA_ROPE // 2
    c = cos[None, :, None, :]
    s = sin[None, :, None, :]
    x1, x2 = x[..., :half], x[..., half:]
    return jnp.concatenate([x1 * c - x2 * s, x2 * c + x1 * s], axis=-1).astype(x.dtype)

def centred_pool_minus_self(u):
    L = u.shape[1]
    uf = u.astype(jnp.float32)
    cs = jnp.concatenate([jnp.zeros_like(uf[:, :1]), jnp.cumsum(uf, axis=1)], axis=1)
    t = jnp.arange(L)
    outs = []
    for g, w in enumerate(POOL_WINDOWS):
        lo_c, hi_c = g * POOL_GROUP, (g + 1) * POOL_GROUP
        csg = cs[..., lo_c:hi_c]
        lo = jnp.clip(t - w // 2, 0, L)
        hi = jnp.clip(t + w // 2, 0, L)
        win_sum = jnp.take(csg, hi, axis=1) - jnp.take(csg, lo, axis=1)
        cnt = (hi - lo).astype(jnp.float32)[None, :, None]
        outs.append(win_sum / cnt - uf[..., lo_c:hi_c])
    return jnp.concatenate(outs, axis=-1).astype(u.dtype)

def pool_mixer(u, w_pool, scale):
    B, L, _ = u.shape
    d = centred_pool_minus_self(u).reshape(B, L, len(POOL_WINDOWS), POOL_GROUP)
    y = jnp.einsum('blgc,gce->blge', d, w_pool).reshape(B, L, POOL_WIDTH)
    return y * scale

def mla_qkv(zq, zkv, zkr, q_a_norm, kv_a_norm, w_uq, w_ukv, q_gain, k_gain, rope):
    B, L, _ = zq.shape
    q = (rms_norm(zq, q_a_norm) @ w_uq).reshape(B, L, MLA_HEADS, MLA_QK)
    kv = (rms_norm(zkv, kv_a_norm) @ w_ukv).reshape(B, L, MLA_HEADS, MLA_NOPE + MLA_V)
    k_rope = jnp.broadcast_to(zkr[:, :, None, :], (B, L, MLA_HEADS, MLA_ROPE))
    k = jnp.concatenate([kv[..., :MLA_NOPE], k_rope], axis=-1)
    v = kv[..., MLA_NOPE:]
    q = rms_norm(q, q_gain)
    k = rms_norm(k, k_gain)
    if rope is not None:
        cos, sin = rope
        q = jnp.concatenate([q[..., :MLA_NOPE], apply_rope(q[..., MLA_NOPE:], cos, sin)], axis=-1)
        k = jnp.concatenate([k[..., :MLA_NOPE], apply_rope(k[..., MLA_NOPE:], cos, sin)], axis=-1)
    return q, k, v

def attend(q, k, v):
    s = jnp.einsum('bqhd,bkhd->bhqk', q, k).astype(jnp.float32) * MLA_SCALE
    p = jax.nn.softmax(s, axis=-1).astype(v.dtype)
    return jnp.einsum('bhqk,bkhd->bqhd', p, v)

def blocked_attention(q, k, v):
    B, L, H, D = q.shape
    nb = L // Q_BLOCK
    qb = q.reshape(B, nb, Q_BLOCK, H, D).swapaxes(0, 1)
    out = lax.map(lambda qq: attend(qq, k, v), qb)
    return out.swapaxes(0, 1).reshape(B, L, H, v.shape[-1])

def zero_state(B):
    return (jnp.zeros((B, ML_HEADS, ML_DV, ML_DK), jnp.float32),
            jnp.zeros((B, ML_HEADS, ML_DK), jnp.float32),
            jnp.full((B, ML_HEADS), NEG_INIT, jnp.float32))

def mlstm_scan(q, k, v, log_i, log_f, state):
    B, L, H, _ = q.shape
    nc = L // ML_CHUNK

    def chunks(a):
        a = a.astype(jnp.float32)
        return a.reshape((B, nc, ML_CHUNK) + a.shape[2:]).swapaxes(0, 1)

    causal = jnp.tril(jnp.ones((ML_CHUNK, ML_CHUNK), dtype=bool))

    def step(carry, inp):
        C, n, m = carry
        qc, kc, vc, ic, fc = inp
        b = jnp.cumsum(fc, axis=1).swapaxes(1, 2)
        ih = ic.swapaxes(1, 2)
        dmat = b[..., :, None] - b[..., None, :] + ih[..., None, :]
        dmat = jnp.where(causal, dmat, -jnp.inf)
        inter = b + m[..., None]
        m_j = jnp.maximum(inter, dmat.max(axis=-1))
        w_inter = jnp.exp(inter - m_j)
        qk = jnp.einsum('bjhd,bshd->bhjs', qc, kc) * jnp.exp(dmat - m_j[..., None])
        num = (jnp.einsum('bhjs,bshv->bjhv', qk, vc)
               + jnp.einsum('bhvd,bjhd->bjhv', C, qc) * w_inter.swapaxes(1, 2)[..., None])
        den = qk.sum(axis=-1) + w_inter * jnp.einsum('bhd,bjhd->bhj', n, qc)
        denom = jnp.maximum(jnp.abs(den), jnp.exp(-m_j)).swapaxes(1, 2)[..., None]
        h = num / denom
        b_last = b[..., -1]
        dec = b_last[..., None] - b + ih
        m_new = jnp.maximum(b_last + m, dec.max(axis=-1))
        w_prev = jnp.exp(b_last + m - m_new)
        w_s = jnp.exp(dec - m_new[..., None])
        C_new = w_prev[..., None, None] * C + jnp.einsum('bhs,bshv,bshd->bhvd', w_s, vc, kc)
        n_new = w_prev[..., None] * n + jnp.einsum('bhs,bshd->bhd', w_s, kc)
        return (C_new, n_new, m_new), h

    final, hs = lax.scan(step, state, (chunks(q), chunks(k), chunks(v), chunks(log_i), chunks(log_f)))
    return hs.swapaxes(0, 1).reshape(B, L, H, v.shape[-1]), final

def mlstm_inputs(zq, zk, zv, zg, gate_bias):
    B, L, _ = zq.shape
    q = zq.reshape(B, L, ML_HEADS, ML_DK) * (ML_DK ** -0.5)
    k = zk.reshape(B, L, ML_HEADS, ML_DK)
    v = zv.reshape(B, L, ML_HEADS, ML_DV)
    g = (zg + gate_bias).astype(jnp.float32)
    i_f, f_f, i_b, f_b = jnp.split(g, 4, axis=-1)
    return q, k, v, (i_f, jax.nn.log_sigmoid(f_f)), (i_b, jax.nn.log_sigmoid(f_b))

def mlstm_bidir(q, k, v, gates_f, gates_b, st_f, st_b):
    h_f, st_f = mlstm_scan(q, k, v, gates_f[0], gates_f[1], st_f)
    flip = lambda a: jnp.flip(a, axis=1)
    h_b, st_b = mlstm_scan(flip(q), flip(k), flip(v), flip(gates_b[0]), flip(gates_b[1]), st_b)
    return (h_f + flip(h_b)).astype(q.dtype), st_f, st_b

def mlstm_out(h, o_pre, gain):
    B, L = h.shape[:2]
    o = jax.nn.sigmoid(o_pre).reshape(B, L, ML_HEADS, ML_DV)
    return (rms_norm(h, gain) * o).reshape(B, L, ML_WIDTH)

def peer_ffn(h, w_q, subkeys, u_tab, v_tab):
    B, L, D = h.shape
    hb_all = h.reshape((B * L) // PEER_BLOCK, PEER_BLOCK, D)

    def block(hb):
        P = hb.shape[0]
        q = (hb @ w_q).reshape(P, PEER_HEADS, 2, PEER_DKEY // 2)
        s = jnp.einsum('phcd,hcnd->phcn', q, subkeys).astype(jnp.float32)
        top_v, top_i = lax.top_k(s, PEER_TOPK)
        cand = top_v[:, :, 0, :, None] + top_v[:, :, 1, None, :]
        best, flat = lax.top_k(cand.reshape(P, PEER_HEADS, PEER_TOPK * PEER_TOPK), PEER_TOPK)
        i1 = jnp.take_along_axis(top_i[:, :, 0, :], flat // PEER_TOPK, axis=-1)
        i2 = jnp.take_along_axis(top_i[:, :, 1, :], flat % PEER_TOPK, axis=-1)
        expert = i1 * PEER_KEYS + i2
        g = jax.nn.softmax(best, axis=-1)
        a = jax.nn.gelu(jnp.einsum('pd,phkd->phk', hb, u_tab[expert]).astype(jnp.float32), approximate=False)
        w = (g * a).astype(hb.dtype)
        return jnp.einsum('phk,phkd->pd', w, v_tab[expert])

    return lax.map(block, hb_all).reshape(B, L, D)

def setup_inputs(seed: int = 0) -> dict:
    key = jax.random.key(seed)
    ks = jax.random.split(key, 32)
    nrm = lambda k, shape, s: jax.random.normal(k, shape, jnp.float32) * s
    D = D_MODEL
    i_bias = nrm(ks[20], (DEPTH, 2, ML_HEADS), 0.1)
    f_bias = 3.0 + nrm(ks[21], (DEPTH, 2, ML_HEADS), 0.5)
    gate_bias = jnp.stack([i_bias[:, 0], f_bias[:, 0], i_bias[:, 1], f_bias[:, 1]], axis=1).reshape(DEPTH, 4 * ML_HEADS)
    return {
        "x": nrm(ks[0], (BATCH, SEQ, D), 1.0),
        "c": nrm(ks[1], (BATCH, D), 1.0),
        "ctx": nrm(ks[2], (BATCH, CTX_LEN, D), 1.0),
        "c_ctx": nrm(ks[3], (D,), 1.0),
        "norm1_gain": 1.0 + nrm(ks[4], (DEPTH, D), 0.1),
        "norm2_gain": 1.0 + nrm(ks[5], (DEPTH, D), 0.1),
        "w_ada": nrm(ks[6], (DEPTH, D, 6 * D), 0.5 * D ** -0.5),
        "b_ada": nrm(ks[7], (DEPTH, 6 * D), 0.02),
        "w_in": nrm(ks[8], (DEPTH, D, IN_WIDTH), D ** -0.5),
        "pool_w": nrm(ks[9], (DEPTH, len(POOL_WINDOWS), POOL_GROUP, POOL_GROUP), POOL_GROUP ** -0.5),
        "pool_scale": 1.0 + nrm(ks[10], (DEPTH, POOL_WIDTH), 0.1),
        "mla_q_norm": 1.0 + nrm(ks[11], (DEPTH, MLA_Q_RANK), 0.1),
        "mla_kv_norm": 1.0 + nrm(ks[12], (DEPTH, MLA_KV_RANK), 0.1),
        "w_uq": nrm(ks[13], (DEPTH, MLA_Q_RANK, MLA_HEADS * MLA_QK), MLA_Q_RANK ** -0.5),
        "w_ukv": nrm(ks[14], (DEPTH, MLA_KV_RANK, MLA_HEADS * (MLA_NOPE + MLA_V)), MLA_KV_RANK ** -0.5),
        "q_norm": 1.0 + nrm(ks[15], (DEPTH, MLA_QK), 0.1),
        "k_norm": 1.0 + nrm(ks[16], (DEPTH, MLA_QK), 0.1),
        "ml_gate_bias": gate_bias,
        "ml_out_norm": 1.0 + nrm(ks[17], (DEPTH, ML_HEADS, ML_DV), 0.1),
        "w_out": nrm(ks[18], (DEPTH, MIX_WIDTH, D), MIX_WIDTH ** -0.5),
        "peer_wq": nrm(ks[19], (DEPTH, D, PEER_HEADS * PEER_DKEY), D ** -0.5),
        "peer_subkeys": nrm(ks[22], (DEPTH, PEER_HEADS, 2, PEER_KEYS, PEER_DKEY // 2), (PEER_DKEY // 2) ** -0.5),
        "peer_u": nrm(ks[23], (DEPTH, PEER_EXPERTS, D), D ** -0.5),
        "peer_v": nrm(ks[24], (DEPTH, PEER_EXPERTS, D), 1.0),
    }

def reference(x, c, ctx, c_ctx, norm1_gain, norm2_gain, w_ada, b_ada, w_in, pool_w, pool_scale,
              mla_q_norm, mla_kv_norm, w_uq, w_ukv, q_norm, k_norm, ml_gate_bias, ml_out_norm, w_out,
              peer_wq, peer_subkeys, peer_u, peer_v):
    B, S, _ = x.shape
    rope = axial_rope_tables(S)
    x_ctx = ctx
    for l in range(DEPTH):
        last = l == DEPTH - 1
        sh_a, sc_a, g_a, sh_f, sc_f, g_f = ada_mod(c, w_ada[l], b_ada[l])
        csh_a, csc_a, cg_a, csh_f, csc_f, cg_f = ada_mod(c_ctx[None], w_ada[l], b_ada[l])

        zc = split_columns(modulate(x_ctx, norm1_gain[l], csh_a, csc_a) @ w_in[l])
        qc, kc, vc = mla_qkv(zc[1], zc[2], zc[3], mla_q_norm[l], mla_kv_norm[l], w_uq[l], w_ukv[l],
                             q_norm[l], k_norm[l], None)
        mq, mk, mv, gf, gb = mlstm_inputs(zc[4], zc[5], zc[6], zc[8], ml_gate_bias[l])
        h_mc, st_f, st_b = mlstm_bidir(mq, mk, mv, gf, gb, zero_state(B), zero_state(B))
        if not last:
            pool_c = pool_mixer(zc[0], pool_w[l], pool_scale[l])
            attn_c = attend(qc, kc, vc).reshape(B, CTX_LEN, MLA_WIDTH)
            ml_c = mlstm_out(h_mc, zc[7], ml_out_norm[l])
            mix_c = jnp.concatenate([pool_c, attn_c, ml_c], axis=-1) @ w_out[l]
            x_ctx_new = x_ctx + cg_a * mix_c
            x_ctx_new = x_ctx_new + cg_f * peer_ffn(modulate(x_ctx_new, norm2_gain[l], csh_f, csc_f),
                                                    peer_wq[l], peer_subkeys[l], peer_u[l], peer_v[l])

        z = split_columns(modulate(x, norm1_gain[l], sh_a, sc_a) @ w_in[l])
        pool_x = pool_mixer(z[0], pool_w[l], pool_scale[l])
        q, k, v = mla_qkv(z[1], z[2], z[3], mla_q_norm[l], mla_kv_norm[l], w_uq[l], w_ukv[l],
                          q_norm[l], k_norm[l], rope)
        k_all = jnp.concatenate([k, kc], axis=1)
        v_all = jnp.concatenate([v, vc], axis=1)
        attn_x = blocked_attention(q, k_all, v_all).reshape(B, S, MLA_WIDTH)
        mq, mk, mv, gf, gb = mlstm_inputs(z[4], z[5], z[6], z[8], ml_gate_bias[l])
        h_m, _, _ = mlstm_bidir(mq, mk, mv, gf, gb, st_f, st_b)
        ml_x = mlstm_out(h_m, z[7], ml_out_norm[l])
        mix = jnp.concatenate([pool_x, attn_x, ml_x], axis=-1) @ w_out[l]
        x = x + g_a * mix
        x = x + g_f * peer_ffn(modulate(x, norm2_gain[l], sh_f, sc_f),
                               peer_wq[l], peer_subkeys[l], peer_u[l], peer_v[l])
        if not last:
            x_ctx = x_ctx_new
    return x


_drawn_inputs = setup_inputs


def setup_inputs(seed=0):
    import zlib

    import numpy as np

    out = dict(_drawn_inputs(seed))
    spreads = {}
    factors = {'mla_q_norm': 3.724, 'q_norm': 3.897, 'k_norm': 3.409}
    for name, (base, spread) in spreads.items():
        noise = np.random.default_rng([zlib.crc32(name.encode()), seed]).standard_normal(out[name].shape)
        drawn = base * np.exp(spread * noise) if base else spread * noise
        out[name] = jnp.asarray(drawn.astype(out[name].dtype))
    for name, factor in factors.items():
        out[name] = (out[name] * factor).astype(out[name].dtype)
    return out
```

```python
from contextlib import ExitStack

import numpy as np

import concourse.bass as bass
from concourse import mybir

ALU = mybir.AluOpType
ACT = mybir.ActivationFunctionType
AX = mybir.AxisListType
F32 = mybir.dt.float32
I32 = mybir.dt.int32
U32 = mybir.dt.uint32

P = 128
D = 1024
KC = D // P
SEQ = 256
CTX = 256
COLS = SEQ + CTX
DEPTH = 2
EPS = 1e-6
NEG = -1e30
GRID_W = 64

WINDOWS = (2, 4, 8, 16)
PGROUP = 64
PAD = max(WINDOWS) // 2
PLEN = SEQ + 2 * PAD

HEADS, NOPE, ROPE, QK, VD = 8, 64, 32, 96, 64
QRANK, KVRANK = 384, 256
SCALE = QK ** -0.5
ROPE_BASE = 10000.0

MH, MD = 4, 64
DIRS = 2

PH, PTOP, PKEYS, PDK = 8, 16, 128, 128
HC = 2 * PH
SLOTS = PH * PTOP

WT = 256
WSLOTS = 4
ADA_TILES = 6 * D // WT
IN_TILES = 8
OUT_TILES = D // WT
PQ_TILES = HC * PDK // WT
LAYER_TILES = ADA_TILES + IN_TILES + OUT_TILES + PQ_TILES

RING = 16
HALF = RING // 2
ITERS = SLOTS // RING
DIAGS = 4

PB_ADA, PB_G1, PB_G2, PB_PS, PB_QN, PB_KVN, PB_GI, PB_GF = 0, 48, 56, 64, 66, 69, 71, 72
PB_QG, PB_KG, PB_ML = 73, 73 + QK, 73 + 2 * QK
PB = PB_ML + MH * MD
C_ID, C_ONE = 0, 128
C_MASK = 256
C_INV = C_MASK + DIRS * 2 * 256
C_COS = C_INV + 2 * 256
C_SIN = C_COS + 32
C_DIR = C_SIN + 32
C_IOTA = C_DIR + 2
CB = C_IOTA + 16


class Signal:

    def __init__(self, ctx, nc, name, first, second):
        self.sem = ctx.enter_context(nc.semaphore(name))
        self.start = (0, first)
        self.each = (first, second)

    def at(self, layer, n):
        assert 0 < n <= self.each[layer]
        return self.start[layer] + n


def build(nc, x_in, c_in, par_in, con_in, w_in, uq_in, ukv_in, pw_in, sk_in, u_tabs, v_tabs, out):
    with ExitStack() as ctx:
        def sb(name, shape, dt=F32):
            return ctx.enter_context(nc.sbuf_tensor(name, shape, dt))

        def sem(name):
            return ctx.enter_context(nc.semaphore(name))

        def signal(name, first, second=None):
            return Signal(ctx, nc, name, first, first if second is None else second)

        ps = [ctx.enter_context(nc.psum_tensor(f"bank{i}", [P, 512], F32)) for i in range(6)]
        acc = ctx.enter_context(nc.psum_tensor("bank67", [P, 1024], F32))
        ps += [acc[:, 0:512], acc[:, 512:1024]]

        xT = sb("xT", [P, KC, COLS])
        hT = sb("hT", [P, KC, COLS])
        wring = sb("wring", [P, WSLOTS, KC, WT])
        regA = sb("regA", [P, RING * D])
        regB = sb("regB", [P, 8336])
        mlaw = sb("mlaw", [P, 3 * 768 + 2 * 1024])
        subk = sb("subk", [P, HC, PKEYS])
        poolw = sb("poolw", [P, 2, PGROUP])
        con = sb("con", [P, CB])
        par = sb("par", [P, DEPTH, PB])
        cT = sb("cT", [P, KC, 2])
        cS = sb("cS", [P, KC, 2])
        modT = sb("modT", [P, 48, 2])
        A1 = sb("A1", [P, KC, 2])
        A2 = sb("A2", [P, KC, 2])
        sqreg = sb("sqreg", [P, 2 * COLS])
        rms = sb("rms", [P, COLS])
        zrow = sb("zrow", [1, P])
        idx = sb("idx", [P, 2, SLOTS], I32)
        stage = sb("stage", [P, RING], I32)
        esum = sb("esum", [P, 2, PH])

        def shaped(reg, off, a, b=None, c=None):
            if b is None:
                return reg[:, off:off + a]
            if c is None:
                return reg[:, off:off + a * b].rearrange("p (a b) -> p a b", a=a)
            return reg[:, off:off + a * b * c].rearrange("p (a b c) -> p a b c", a=a, b=b)

        ring = shaped(regA, 0, RING, D)
        pu = shaped(regA, 0, 2, 2, PLEN)
        pa_ = shaped(regA, 1088, 2, 2, PLEN)
        pb_ = shaped(regA, 2176, 2, 2, PLEN)
        rows = shaped(regA, 4096, 12, COLS)[0:8]
        gi, gf, gt, lf, BF, BB, cF, cB, MF, MB, ones8, gu = (rows[:, i, :] for i in range(12))
        qT = shaped(regA, 0, HEADS, COLS)
        kT = shaped(regA, 4096, HEADS, COLS)
        vrow = shaped(regA, 8192, 4, HEADS * VD)
        rowbuf = regA[:, 10240:13312].rearrange("p (b g h d) -> p b g h d", b=2, g=2, h=HEADS)
        rowsq = regA[:, 13312:14848]
        pt = shaped(regA, 10240, 2, 4, P)
        prob = shaped(regA, 14848, 2, COLS)
        marg = shaped(regA, 10752, DIRS, 3, 256)
        mE = shaped(regA, 12288, DIRS, 4, 256)
        mP = shaped(regA, 14336, DIRS, 4, 256)
        hn = regA[:, 0:1024].rearrange("p (q e h d) -> p q e h d", q=2, e=2, h=MH)
        hs = shaped(regA, 1024, 2, MH, MD)
        hq = shaped(regA, 1536, 2, MH, MD)
        zqT = shaped(regB, 0, 3, COLS)
        zkvT = shaped(regB, 1536, 2, COLS)
        mqT = shaped(regB, 2560, 2, COLS)
        mkT = shaped(regB, 3584, 2, COLS)
        v1 = shaped(regB, 4608, 4, MH, MD + 1)
        osig = shaped(regB, 5648, 4, MH * MD)
        zkr = shaped(regB, 6672, 4, ROPE)
        gcm = shaped(regB, 6800, 3, COLS)[0:8]
        numS = regB[:, 0:1040].rearrange("p (q e h d) -> p q e h d", q=2, e=2, h=MH)
        hrow = shaped(regB, 0, 4, D)
        topv = shaped(regB, 4096, 4, HC, PTOP)
        topi = shaped(regB, 5120, 4, HC, PTOP)
        cand = regB[:, 6144:8192]
        uqw = shaped(mlaw, 0, 3, 768)
        ukvw = shaped(mlaw, 2304, 2, 1024)
        yrow = mlaw[:, 0:1024]
        pq = shaped(mlaw, 1024, 2, COLS)
        topiu = mlaw[:, 2048:3072].bitcast(U32).rearrange("p (t c k) -> p t c k", t=4, c=HC)
        s2 = mlaw[:, 3072:3328]
        bi = mlaw[:, 3328:3456].bitcast(U32)
        bf, r1, r2, araw, gact = (mlaw[:, 3456 + i * SLOTS:3456 + (i + 1) * SLOTS] for i in range(5))
        sq = shaped(sqreg, 0, 2, COLS)
        diag = shaped(sqreg, 0, DIAGS, P)
        bv = shaped(sqreg, 512, 2, SLOTS)
        wts = shaped(sqreg, 768, 2, SLOTS)
        rtmp = shaped(regA, 14848, 4, 16, 16)
        ident = con[:, C_ID:C_ID + P]
        ones = con[:, C_ONE:C_ONE + P]
        mask = con[:, C_MASK:C_MASK + 1024].rearrange("p (e k j) -> p e k j", e=2, k=2)
        inv = con[:, C_INV:C_INV + 512].rearrange("p (c j) -> p c j", c=2)
        cos = con[:, C_COS:C_COS + 32].rearrange("p (t f) -> p t f", t=2)
        sin = con[:, C_SIN:C_SIN + 32].rearrange("p (t f) -> p t f", t=2)
        iota16 = con[:, C_IOTA:C_IOTA + 16]
        gcol = sb("gcol", [P, 2, 4, 8])
        rowss = sb("rowss", [P, 3, 16])
        mden = sb("mden", [P, 3, 16])
        asm = sb("asm", [P, 2, 4])
        gate_f = sb("gate_f", [P, KC, 2])

        full = [(0, COLS), (0, SEQ)]
        tiles = [[0, 1, 2, 3], [0, 1]]
        streams = [[0, 1], [0]]

        loaded = sem("loaded")
        w_landed = [sem(f"w_landed{i}") for i in range(WSLOTS)]
        w_free = sem("w_free")
        mixw = sem("mixw")
        skw = sem("skw")
        cs_ready = sem("cs_ready")
        init_done = sem("init_done")
        pad_done = sem("pad_done")
        ada_mm = signal("ada_mm", 1)
        mod_ready = signal("mod_ready", 1)
        sq_ready = signal("sq_ready", 21)
        sq_used = signal("sq_used", 21)
        ss_ready = signal("ss_ready", 4)
        ms_ready = signal("ms_ready", 4)
        rt_ready = signal("rt_ready", 4)
        hx_ready = signal("hx_ready", 16)
        h_ready = signal("h_ready", 16)
        in_mm = signal("in_mm", 21, 19)
        in_evac = signal("in_evac", 21, 19)
        lnf_ready = signal("lnf_ready", 1)
        gm_ready = signal("gm_ready", 1)
        em_ready = signal("em_ready", 1)
        gt_mm = signal("gt_mm", 1)
        gc_ready = signal("gc_ready", 1)
        pool_ready = signal("pool_ready", 1)
        pool_mm = signal("pool_mm", 2)
        pool_out = signal("pool_out", 2)
        zn_ready = signal("zn_ready", 5)
        qk_mm = signal("qk_mm", 4)
        row_ready = signal("row_ready", 4)
        rss_ready = signal("rss_ready", 4)
        rsq_ready = signal("rsq_ready", 4)
        rown_ready = signal("rown_ready", 4)
        tr_mm = signal("tr_mm", 16, 12)
        tr_evac = signal("tr_evac", 16, 12)
        NU = [32, 16]
        sc_mm = signal("sc_mm", *NU)
        smax = signal("smax", *NU)
        e_done = signal("e_done", *NU)
        p_ready = signal("p_ready", *NU)
        pt_mm = signal("pt_mm", *NU)
        pt_ready = signal("pt_ready", *NU)
        pv_mm = signal("pv_mm", 16, 8)
        attn_out = signal("attn_out", 16, 8)
        st_mm = signal("st_mm", 8, 4)
        marg_ready = signal("marg_ready", 16, 8)
        mE_ready = signal("mE_ready", 16, 8)
        mP_ready = signal("mP_ready", 16, 8)
        num_mm = signal("num_mm", 8, 4)
        num_evac = signal("num_evac", 8, 4)
        hq_ready = signal("hq_ready", 2, 1)
        hsq_ready = signal("hsq_ready", 2, 1)
        hss_ready = signal("hss_ready", 2, 1)
        hrt_ready = signal("hrt_ready", 2, 1)
        ml_ready = signal("ml_ready", 2, 1)
        mt_mm = signal("mt_mm", 2, 1)
        mt_evac = signal("mt_evac", 2, 1)
        out_mm = signal("out_mm", 8)
        x_mid = signal("x_mid", 8)
        hr_mm = signal("hr_mm", 8, 4)
        hr_ready = signal("hr_ready", 8, 4)
        pq_mm = signal("pq_mm", 16)
        pq_ready = signal("pq_ready", 16)
        psc_mm = signal("psc_mm", 16)
        top_done = signal("top_done", 16)
        idx_ready = signal("idx_ready", 4, 2)
        sub_ready = signal("sub_ready", 4, 2)
        ex_ready = signal("ex_ready", 4, 2)
        u_done = signal("u_done", 4, 2)
        gelu_ready = signal("gelu_ready", 4, 2)
        w_ready = signal("w_ready", 4, 2)
        acc_done = signal("acc_done", 4, 2)
        y_ready = signal("y_ready", 4, 2)
        yt_mm = signal("yt_mm", 8, 4)
        x_done = signal("x_done", 4, 2)
        landed = [sem(f"landed{i}") for i in range(RING)]
        staged = sem("staged")
        pool_turn = sem("pool_turn")
        u_used = sem("u_used")
        v_used = sem("v_used")
        diag_ready = sem("diag_ready")
        s_out = sem("s_out")
        dve_step = sem("dve_step")
        act_step = sem("act_step")
        gp_step = sem("gp_step")

        def mixer_units(l):
            return [(t, h) for t in tiles[l] for h in range(HEADS)]

        def ml_units(l):
            return [(s, h) for s in streams[l] for h in range(MH)]

        block = ctx.enter_context(nc.Block())

        @block.sync
        def _(sp):
            sp.dma_start(cT[:, :, :], c_in).then_inc(loaded, 16)
            sp.dma_start(par[:, :, :], par_in).then_inc(loaded, 16)
            sp.dma_start(con[:, :], con_in).then_inc(loaded, 16)
            sp.dma_start(xT[:, :, :], x_in).then_inc(loaded, 16)
            with sp.Fori(0, DEPTH * LAYER_TILES // WSLOTS) as i:
                for s in range(WSLOTS):
                    sp.wait_ge(w_free, i * WSLOTS + s + 1)
                    sp.dma_start(wring[:, s, :, :], w_in[bass.ds(i * WSLOTS + s, 1), :, :]
                                 .rearrange("o p (k c) -> p (o k) c", k=KC)).then_inc(w_landed[s], 16)
            sp.wait_ge(x_done.sem, x_done.at(1, 2))
            sp.dma_start(out, xT[:, :, 0:SEQ]).then_inc(s_out, 16)
            sp.wait_ge(s_out, 16)

        @block.gpsimd
        def _(g):
            steps = [0]

            def link(ins):
                steps[0] += 1
                ins.then_inc(gp_step, 1)
                g.wait_ge(gp_step, steps[0])

            def pool_windows(l):
                ns = len(streams[l])
                g.wait_ge(pad_done, l + 1)
                g.wait_ge(in_evac.sem, in_evac.at(l, 2))

                def lo(t, c, n0, n1, shift, part=slice(0, P)):
                    return t[part, c, 0:ns, PAD + n0 + shift:PAD + n1 + shift]

                for c in range(2):
                    link(g.tensor_tensor(lo(pa_, c, -7, 263, 0), lo(pu, c, -7, 263, -1), lo(pu, c, -7, 263, 0), ALU.add))
                    link(g.tensor_tensor(lo(pb_, c, -6, 262, 0), lo(pa_, c, -6, 262, -1), lo(pa_, c, -6, 262, 1), ALU.add))
                    if c == 1:
                        link(g.tensor_tensor(lo(pa_, c, -4, 260, 0), lo(pb_, c, -4, 260, -2), lo(pb_, c, -4, 260, 2), ALU.add))
                        link(g.tensor_tensor(lo(pb_, c, 0, 256, 0, slice(64, P)), lo(pa_, c, 0, 256, -4, slice(64, P)),
                                             lo(pa_, c, 0, 256, 4, slice(64, P)), ALU.add))
                    iv = inv[:, c, :].unsqueeze(1).to_broadcast([P, ns, SEQ])
                    link(g.tensor_tensor(lo(pa_, c, 0, 256, 0, slice(0, 64)), lo(pa_, c, 0, 256, 0, slice(0, 64)), iv[0:64], ALU.mult))
                    link(g.tensor_tensor(lo(pa_, c, 0, 256, 0, slice(64, P)), lo(pb_, c, 0, 256, 0, slice(64, P)), iv[64:P], ALU.mult))
                    g.tensor_tensor(lo(pa_, c, 0, 256, 0), lo(pa_, c, 0, 256, 0), lo(pu, c, 0, 256, 0), ALU.subtract).then_inc(gp_step, 1)
                    steps[0] += 1
                g.wait_ge(gp_step, steps[0])
                g.sem_inc(pool_ready.sem, 1)

            def gathers(l, n):
                tile = n if l == 0 else 4 + n
                for tab, base in ((u_tabs[l], 0), (v_tabs[l], ITERS)):
                    is_u = base == 0
                    with g.Fori(0, ITERS) as it:
                        for h in range(2):
                            g.wait_ge(u_used, it * RING + (tile * SLOTS + HALF * h + HALF) if is_u
                                      else (tile + 1) * SLOTS + HALF * h + HALF)
                            g.wait_ge(v_used, tile * SLOTS + HALF * h + HALF if is_u
                                      else it * RING + (tile * SLOTS + HALF * h + HALF))
                            g.sem_inc(pool_turn, 1)
                            g.tensor_copy(stage[:, h * HALF:(h + 1) * HALF],
                                          idx[:, tile % 2, bass.ds(it * RING + h * HALF, HALF)]).then_inc(staged, 1)
                            g.wait_ge(staged, it * 2 + ((tile * 2 * ITERS + base) * 2 + h + 1))
                            g.sem_inc(pool_turn, 1)
                            for s in range(HALF * h, HALF * h + HALF):
                                g.indirect_dma_start(ring[:, s, :], None, tab,
                                                     bass.IndirectOffsetOnAxis(stage[:, s:s + 1], 0)).then_inc(landed[s], 16)

            g.sem_inc(u_used, RING)
            g.sem_inc(v_used, RING)
            for l in range(DEPTH):
                pool_windows(l)
                for n in range(len(tiles[l])):
                    g.wait_ge(idx_ready.sem, idx_ready.at(l, n + 1))
                    gathers(l, n)

        @block.scalar
        def _(a):
            steps = [0]

            def link(ins):
                steps[0] += 1
                ins.then_inc(act_step, 1)
                a.wait_ge(act_step, steps[0])

            sqn = [0, 0]

            def squares(l, src, n):
                for k in range(n):
                    sqn[l] += 1
                    i = sqn[l] + 21 * l
                    if i > 2:
                        a.wait_ge(sq_used.sem, i - 2)
                    a.activation(sq[:, i % 2, :], src[:, k, :], ACT.Square).then_inc(sq_ready.sem, 1)

            def root(l, i):
                a.wait_ge(ms_ready.sem, ms_ready.at(l, i))
                a.activation(rms[:, :], rms[:, :], ACT.Sqrt).then_inc(rt_ready.sem, 1)

            def modulate(l, which):
                A, shift = (A1, 0) if which == 0 else (A2, 24)
                a.wait_ge(mod_ready.sem, mod_ready.at(l, 1))
                for k in range(KC):
                    a.wait_ge(hx_ready.sem, hx_ready.at(l, which * KC + k + 1))
                    for s in range(2):
                        ins = a.activation(hT[:, k, s * SEQ:(s + 1) * SEQ], hT[:, k, s * SEQ:(s + 1) * SEQ], ACT.Identity,
                                           scale=A[:, k, s:s + 1], bias=modT[:, shift + k, s:s + 1])
                    ins.then_inc(h_ready.sem, 1)

            a.wait_ge(loaded, 64)
            link(a.activation(cS[:, :, :], cT[:, :, :], ACT.Silu))
            a.sem_inc(cs_ready, 1)

            for l in range(DEPTH):
                c1 = full[l][1]
                if l == 0:
                    a.dma_start(uqw, uq_in[l]).then_inc(mixw, 16)
                    a.dma_start(ukvw, ukv_in[l]).then_inc(mixw, 16)
                    a.dma_start(poolw[:, :, :], pw_in[l]).then_inc(mixw, 16)
                else:
                    a.wait_ge(x_done.sem, x_done.at(0, 4))
                    a.wait_ge(yt_mm.sem, yt_mm.at(0, 8))
                    a.dma_start(uqw, uq_in[l]).then_inc(mixw, 16)
                    a.dma_start(ukvw, ukv_in[l]).then_inc(mixw, 16)
                    a.dma_start(poolw[:, :, :], pw_in[l]).then_inc(mixw, 16)
                squares(l, xT, KC)
                root(l, 1)
                modulate(l, 0)

                g = [0]

                def group():
                    g[0] += 1
                    a.wait_ge(in_mm.sem, in_mm.at(l, g[0]))
                    return ps[2 + g[0] % 2]

                for b in range(12):
                    src = group()
                    if b < 2:
                        if b == 0:
                            a.wait_ge(pad_done, l + 1)
                        ns = len(streams[l])
                        ins = a.activation(pu[:, b, 0:ns, PAD:PAD + SEQ],
                                           src[:, 0:c1].rearrange("p (s j) -> p s j", s=ns), ACT.Copy)
                    elif b < 5:
                        ins = a.activation(zqT[:, b - 2, 0:c1], src[:, 0:c1], ACT.Copy)
                    elif b < 7:
                        ins = a.activation(zkvT[:, b - 5, :], src[:, :], ACT.Copy)
                    elif b < 9:
                        ins = a.activation(mqT[:, b - 7, 0:c1], src[:, 0:c1], ACT.Copy, scale=MD ** -0.5)
                    elif b < 11:
                        ins = a.activation(mkT[:, b - 9, :], src[:, :], ACT.Copy)
                    else:
                        a.activation(gi, src[0:8, :], ACT.Identity, bias=par[0:8, l, PB_GI:PB_GI + 1])
                        ins = a.activation(gf, src[32:40, :], ACT.Identity, bias=par[0:8, l, PB_GF:PB_GF + 1])
                    ins.then_inc(in_evac.sem, 1)
                src = group()
                a.activation(zkr, src[:, 0:P].rearrange("p (t r) -> p t r", t=4), ACT.Copy).then_inc(in_evac.sem, 1)
                for t in range(4):
                    src = group()
                    a.activation(v1[:, t, :, 0:MD], src[:, 0:WT].rearrange("p (h d) -> p h d", h=MH), ACT.Copy).then_inc(in_evac.sem, 1)
                for t in tiles[l]:
                    src = group()
                    a.activation(osig[:, t, :], src[:, 0:WT], ACT.Sigmoid).then_inc(in_evac.sem, 1)

                a.wait_ge(in_evac.sem, in_evac.at(l, 12))
                link(a.activation(gt, gf, ACT.Abs))
                link(a.activation(gt, gt, ACT.Exp, scale=-1.0))
                a.activation(gt, gt, ACT.Ln, bias=1.0).then_inc(lnf_ready.sem, 1)
                a.wait_ge(in_evac.sem, in_evac.at(l, 7))
                for k in range(3):
                    sqn[l] += 1
                    i = sqn[l] + 21 * l
                    a.wait_ge(sq_used.sem, i - 2)
                    a.activation(sq[:, i % 2, 0:c1], zqT[:, k, 0:c1], ACT.Square).then_inc(sq_ready.sem, 1)
                a.wait_ge(ms_ready.sem, ms_ready.at(l, 2))
                a.activation(rms[:, 0:c1], rms[:, 0:c1], ACT.Sqrt).then_inc(rt_ready.sem, 1)
                squares(l, zkvT, 2)
                root(l, 3)
                a.wait_ge(gm_ready.sem, gm_ready.at(l, 1))
                a.activation(gcm[:, 2, :], gcm[:, 2, :], ACT.Exp, scale=-1.0).then_inc(em_ready.sem, 1)
                a.wait_ge(gt_mm.sem, gt_mm.at(l, 1))
                a.activation(gcol[:, :, :, :], ps[0][:, 0:64].rearrange("p (q t r) -> p q t r", q=2, t=4), ACT.Copy).then_inc(gc_ready.sem, 1)
                for c in range(2):
                    a.wait_ge(pool_mm.sem, pool_mm.at(l, c + 1))
                    if c == 0:
                        a.wait_ge(in_mm.sem, in_mm.at(l, 21 if l == 0 else 19))
                    a.activation(hT[:, c, 0:c1], ps[4 + c][:, 0:c1], ACT.Copy,
                                 scale=par[:, l, PB_PS + c:PB_PS + c + 1]).then_inc(pool_out.sem, 1)

                def row_out(n):
                    t, b = n, n % 2
                    g0 = 0 if t in tiles[l] else 1
                    if n >= 2:
                        a.wait_ge(tr_mm.sem, trs(n - 2)[-1])
                    if n == 0:
                        a.wait_ge(gc_ready.sem, gc_ready.at(l, 1))
                        a.wait_ge(pool_mm.sem, pool_mm.at(l, 2))
                    a.wait_ge(qk_mm.sem, qk_mm.at(l, n + 1))
                    if g0 == 0:
                        for f in range(2):
                            a.activation(rowbuf[:, b, 0, 4 * f:4 * f + 4, :],
                                         ps[0 + f][:, 0:384].rearrange("p (h d) -> p h d", h=4), ACT.Copy)
                    for f in range(2):
                        kv = ps[2 + f][:, :].rearrange("p (h d) -> p h d", h=4)
                        a.activation(vrow[:, t, 256 * f:256 * f + 256].rearrange("p (h d) -> p h d", h=4), kv[:, :, NOPE:], ACT.Copy)
                        a.activation(rowbuf[:, b, 1, 4 * f:4 * f + 4, 0:NOPE], kv[:, :, 0:NOPE], ACT.Copy)
                    link(a.activation(rowbuf[:, b, 1, :, NOPE:], zkr[:, t, :].unsqueeze(1).to_broadcast([P, HEADS, ROPE]), ACT.Copy))
                    if n >= 1:
                        a.wait_ge(rss_ready.sem, rss_ready.at(l, n))
                    a.activation(rowsq[:, g0 * 768:1536], rowbuf[:, b, g0:, :, :].rearrange("p g h d -> p (g h d)"),
                                 ACT.Square).then_inc(row_ready.sem, 1)

                def row_root(n):
                    a.wait_ge(rss_ready.sem, rss_ready.at(l, n + 1))
                    g0 = 0 if n in tiles[l] else 8
                    a.activation(rowss[:, 1, g0:16], rowss[:, 0, g0:16], ACT.Sqrt).then_inc(rsq_ready.sem, 1)

                def trs(n):
                    at = sum(4 if m in tiles[l] else 2 for m in range(n))
                    return [tr_mm.at(l, at + j + 1) for j in range(4 if n in tiles[l] else 2)]

                def tr_out(n):
                    what = [(1, f) for f in range(2)]
                    if n in tiles[l]:
                        what = [(0, f) for f in range(2)] + what
                    for (g_, f), v in zip(what, trs(n)):
                        a.wait_ge(tr_mm.sem, v)
                        dst = (qT, kT)[g_]
                        a.activation(dst[0:QK, 4 * f:4 * f + 4, n * P:(n + 1) * P],
                                     ps[4 + (v - 1) % 2][0:QK, :].rearrange("p (h j) -> p h j", h=4), ACT.Copy).then_inc(tr_evac.sem, 1)

                for n in range(4):
                    row_out(n)
                    row_root(n)
                    if n:
                        tr_out(n - 1)
                tr_out(3)

                units = mixer_units(l)

                def expo(i):
                    t, h = units[i]
                    k0 = 0 if t < 2 else SEQ
                    a.wait_ge(smax.sem, smax.at(l, i + 1))
                    if i >= 2:
                        a.wait_ge(pt_mm.sem, pt_mm.at(l, i - 1))
                    if i == 0:
                        a.wait_ge(tr_mm.sem, trs(3)[-1])
                    a.activation(prob[:, i % 2, k0:COLS], ps[i % 2][:, k0:COLS], ACT.Exp, scale=SCALE,
                                 bias=asm[:, i % 2, 1:2], accum_out=asm[:, i % 2, 2:3]).then_inc(e_done.sem, 1)

                def pt_out(i):
                    t, h = units[i]
                    j0 = 0 if t < 2 else 2
                    a.wait_ge(pt_mm.sem, pt_mm.at(l, i + 1))
                    if i >= 2:
                        a.wait_ge(pv_mm.sem, pv_mm.at(l, (i - 2) // 2 + 1) if (i - 2) % 2 else pv_mm.at(l, 1) if i == 2 else pv_mm.at(l, (i - 2) // 2 + 1))
                    a.activation(pt[:, i % 2, j0:, :], ps[2 + i % 2][:, j0 * P:].rearrange("p (j q) -> p j q", q=P), ACT.Copy).then_inc(pt_ready.sem, 1)

                for i in range(len(units) + 1):
                    if i < len(units):
                        expo(i)
                    if i:
                        pt_out(i - 1)

                mu = ml_units(l)

                def decay(i, e):
                    s, h = mu[i]
                    r = e * MH + h
                    u = 2 * i + e
                    a.wait_ge(marg_ready.sem, marg_ready.at(l, u + 1))
                    if u >= 2:
                        a.wait_ge(mP_ready.sem, mP_ready.at(l, u - 1))
                    if u < 2:
                        a.wait_ge(pt_mm.sem, pt_mm.at(l, len(units)))
                        a.wait_ge(pv_mm.sem, pv_mm.at(l, len(units) // 2))
                    for j in range(2):
                        c = 2 * s + j
                        ins = a.activation(mE[:, e, c, :], marg[:, e, j, :], ACT.Exp, bias=gcol[:, 0, c, r:r + 1])
                    if s == 0:
                        for c in (2, 3):
                            ins = a.activation(mE[:, e, c, :], marg[:, e, 2, :], ACT.Exp,
                                               bias=gcol[:, 0, c, r:r + 1])
                    ins.then_inc(mE_ready.sem, 1)

                def num_out(i):
                    s, h = mu[i]
                    a.wait_ge(num_mm.sem, num_mm.at(l, i + 1))
                    if s != mu[0][0] and h == 0:
                        a.wait_ge(hsq_ready.sem, hsq_ready.at(l, 1))
                    a.activation(numS[:, :, :, h, :], ps[6 + i % 2][:, 0:260].rearrange("p (q e d) -> p q e d", q=2, e=2),
                                 ACT.Copy).then_inc(num_evac.sem, 1)

                def head_norm(n):
                    a.wait_ge(hq_ready.sem, hq_ready.at(l, n + 1))
                    a.activation(hq, hs, ACT.Square).then_inc(hsq_ready.sem, 1)
                    a.wait_ge(hss_ready.sem, hss_ready.at(l, n + 1))
                    a.activation(mden[:, 1, 0:8], mden[:, 0, 0:8], ACT.Sqrt).then_inc(hrt_ready.sem, 1)

                def ml_out(n):
                    s = streams[l][n]
                    a.wait_ge(mt_mm.sem, mt_mm.at(l, n + 1))
                    a.activation(hT[:, 6:8, s * SEQ:(s + 1) * SEQ], ps[3][:, :].rearrange("p (c j) -> p c j", c=2), ACT.Copy).then_inc(mt_evac.sem, 1)

                for i in range(len(mu) + 1):
                    if i and i % MH == 0:
                        num_out(i - 1)
                        head_norm(i // MH - 1)
                    if i < len(mu):
                        decay(i, 0)
                        decay(i, 1)
                    if i % MH:
                        num_out(i - 1)
                for n in range(len(streams[l])):
                    ml_out(n)

                a.wait_ge(x_mid.sem, x_mid.at(l, 1))
                a.dma_start(subk[:, :, :], sk_in[l]).then_inc(skw, 16)
                for k in range(KC):
                    a.wait_ge(x_mid.sem, x_mid.at(l, k + 1))
                    sqn[l] += 1
                    i = sqn[l] + 21 * l
                    a.wait_ge(sq_used.sem, i - 2)
                    a.activation(sq[:, i % 2, 0:c1], xT[:, k, 0:c1], ACT.Square).then_inc(sq_ready.sem, 1)
                a.wait_ge(ms_ready.sem, ms_ready.at(l, 4))
                a.activation(rms[:, 0:c1], rms[:, 0:c1], ACT.Sqrt).then_inc(rt_ready.sem, 1)
                for k in range(KC):
                    a.wait_ge(hx_ready.sem, hx_ready.at(l, KC + k + 1))
                    for s in streams[l]:
                        ins = a.activation(hT[:, k, s * SEQ:(s + 1) * SEQ], hT[:, k, s * SEQ:(s + 1) * SEQ], ACT.Identity,
                                           scale=A2[:, k, s:s + 1], bias=modT[:, 24 + k, s:s + 1])
                    ins.then_inc(h_ready.sem, 1)
                for j in range(2 * len(tiles[l])):
                    a.wait_ge(hr_mm.sem, hr_mm.at(l, j + 1))
                    a.activation(hrow[:, j // 2, (j % 2) * 512:(j % 2) * 512 + 512], ps[4 + j % 2][:, :], ACT.Copy).then_inc(hr_ready.sem, 1)
                for q in range(HC):
                    a.wait_ge(pq_mm.sem, pq_mm.at(l, q + 1))
                    if q >= 2:
                        a.wait_ge(psc_mm.sem, psc_mm.at(l, q - 1))
                    a.activation(pq[:, q % 2, 0:c1], ps[q % 2][:, 0:c1], ACT.Copy).then_inc(pq_ready.sem, 1)

                for n in range(len(tiles[l])):
                    tile = n if l == 0 else 4 + n
                    b = tile % 2
                    a.wait_ge(sub_ready.sem, sub_ready.at(l, n + 1))
                    a.activation(bv[:, b, :], bv[:, b, :], ACT.Exp).then_inc(ex_ready.sem, 1)
                    a.wait_ge(u_done.sem, u_done.at(l, n + 1))
                    a.activation(gact[:, :], araw[:, :], ACT.Gelu).then_inc(gelu_ready.sem, 1)
                    a.wait_ge(w_ready.sem, w_ready.at(l, n + 1))
                    with a.Fori(0, SLOTS // DIAGS) as it:
                        for s in range(DIAGS):
                            a.wait_ge(v_used, it * DIAGS + (tile * SLOTS + s + 1 + RING - DIAGS))
                            a.activation(diag[:, s, :], ident, ACT.Copy,
                                         scale=wts[:, b, bass.ds(it * DIAGS + s, 1)]).then_inc(diag_ready, 1)
                    a.wait_ge(acc_done.sem, acc_done.at(l, n + 1))
                    if n:
                        a.wait_ge(yt_mm.sem, yt_mm.at(l, 2 * n))
                    else:
                        a.wait_ge(psc_mm.sem, psc_mm.at(l, HC))
                    a.activation(yrow, acc[:, :], ACT.Copy).then_inc(y_ready.sem, 1)

        @block.vector
        def _(v):
            steps = [0]

            def link(ins):
                steps[0] += 1
                ins.then_inc(dve_step, 1)
                v.wait_ge(dve_step, steps[0])

            def ada_out(l):
                v.wait_ge(ada_mm.sem, ada_mm.at(l, 1))
                link(v.tensor_tensor(modT[:, :, :], ps[5][:, 0:96].rearrange("p (b s) -> p b s", s=2),
                                     par[:, l, PB_ADA:PB_ADA + 48].unsqueeze(2).to_broadcast([P, 48, 2]), ALU.add))
                for A, sc, g_ in ((A1, 8, PB_G1), (A2, 32, PB_G2)):
                    ins = v.scalar_tensor_tensor(out=A[:, :, :], in0=modT[:, sc:sc + 8, :], scalar=1.0,
                                                 in1=par[:, l, g_:g_ + 8].unsqueeze(2).to_broadcast([P, 8, 2]),
                                                 op0=ALU.add, op1=ALU.mult)
                ins.then_inc(mod_ready.sem, 1)

            def inv_rms(l, i, width, c1):
                v.wait_ge(ss_ready.sem, ss_ready.at(l, i))
                v.tensor_scalar(rms[:, 0:c1], ps[0 if i != 3 else 1][:, 0:c1], 1.0 / width, EPS, ALU.mult, ALU.add).then_inc(ms_ready.sem, 1)
                v.wait_ge(rt_ready.sem, rt_ready.at(l, i))
                link(v.reciprocal(rms[:, 0:c1], rms[:, 0:c1]))

            v.memset(zrow[:, :], 0.0).then_inc(init_done, 1)

            for l in range(DEPTH):
                c1 = full[l][1]
                ns = len(streams[l])
                if l == 0:
                    v.wait_ge(loaded, 64)
                v.memset(pu[:, :, :, :], 0.0).then_inc(pad_done, 1)
                v.memset(v1[:, :, :, MD:MD + 1], 1.0)
                link(v.memset(ones8, 1.0))
                if l == 0:
                    ada_out(0)
                inv_rms(l, 1, D, COLS)
                for k in range(KC):
                    v.tensor_tensor(hT[:, k, :], xT[:, k, :], rms[:, :], ALU.mult).then_inc(hx_ready.sem, 1)

                v.wait_ge(lnf_ready.sem, lnf_ready.at(l, 1))
                link(v.scalar_tensor_tensor(out=lf, in0=gf, scalar=0.0, in1=gt, op0=ALU.min, op1=ALU.subtract))
                xs, cs = slice(0, SEQ), slice(SEQ, COLS)
                v.tensor_tensor_scan(BB[:, ::-1], ones8[:, ::-1], lf[:, ::-1], 0.0, ALU.mult, ALU.add)
                link(v.tensor_tensor_scan(BF[:, cs], ones8[:, cs], lf[:, cs], 0.0, ALU.mult, ALU.add))
                link(v.tensor_tensor_scan(BF[:, xs], ones8[:, xs], lf[:, xs], BF[:, COLS - 1:COLS], ALU.mult, ALU.add))
                v.tensor_tensor(cB, gi, BB, ALU.subtract)
                link(v.tensor_tensor(cF, gi, BF, ALU.subtract))
                v.tensor_tensor_scan(MB[:, ::-1], cB[:, ::-1], cB[:, ::-1], NEG, ALU.max, ALU.max)
                link(v.tensor_tensor_scan(MF[:, cs], cF[:, cs], cF[:, cs], NEG, ALU.max, ALU.max))
                link(v.tensor_tensor_scan(MF[:, xs], cF[:, xs], cF[:, xs], MF[:, COLS - 1:COLS], ALU.max, ALU.max))
                v.tensor_tensor(BF, BF, MF, ALU.add)
                link(v.tensor_tensor(BB, BB, MB, ALU.add))
                for j, (f_, b_) in enumerate(((cF, cB), (MF, MB), (BF, BB))):
                    link(v.tensor_scalar(gu, b_, con[0:8, C_DIR + 1:C_DIR + 2], None, ALU.mult))
                    ins = v.scalar_tensor_tensor(out=gcm[:, j, :], in0=f_, scalar=con[0:8, C_DIR:C_DIR + 1], in1=gu,
                                                 op0=ALU.mult, op1=ALU.add)
                    link(ins)
                v.sem_inc(gm_ready.sem, 1)

                inv_rms(l, 2, QRANK, c1)
                for k in range(3):
                    ins = v.scalar_tensor_tensor(out=zqT[:, k, 0:c1], in0=zqT[:, k, 0:c1], scalar=par[:, l, PB_QN + k:PB_QN + k + 1],
                                                 in1=rms[:, 0:c1], op0=ALU.mult, op1=ALU.mult).then_inc(zn_ready.sem, 1)
                v.wait_ge(zn_ready.sem, zn_ready.at(l, 3))
                inv_rms(l, 3, KVRANK, COLS)
                for k in range(2):
                    v.scalar_tensor_tensor(out=zkvT[:, k, :], in0=zkvT[:, k, :], scalar=par[:, l, PB_KVN + k:PB_KVN + k + 1],
                                           in1=rms[:, :], op0=ALU.mult, op1=ALU.mult).then_inc(zn_ready.sem, 1)

                for n in range(4):
                    b = n % 2
                    g0 = 0 if n in tiles[l] else 1
                    gn = 2 - g0
                    v.wait_ge(row_ready.sem, row_ready.at(l, n + 1))
                    if n:
                        v.wait_ge(rsq_ready.sem, rsq_ready.at(l, n))
                    link(v.tensor_reduce(rowss[:, 0, 8 * g0:16], rowsq[:, g0 * 768:1536].rearrange("p (h d) -> p h d", d=QK), AX.X, ALU.add))
                    v.tensor_scalar(rowss[:, 0, 8 * g0:16], rowss[:, 0, 8 * g0:16], 1.0 / QK, EPS, ALU.mult, ALU.add).then_inc(rss_ready.sem, 1)
                    v.wait_ge(rsq_ready.sem, rsq_ready.at(l, n + 1))
                    link(v.reciprocal(rowss[:, 2, 8 * g0:16], rowss[:, 1, 8 * g0:16]))
                    rb = rowbuf[:, b, g0:, :, :].rearrange("p g h d -> p (g h) d")
                    link(v.tensor_tensor(rb, rb, rowss[:, 2, 8 * g0:16].unsqueeze(2).to_broadcast([P, 8 * gn, QK]), ALU.mult))
                    gains = par[:, l, PB_QG + g0 * QK:PB_QG + 2 * QK].rearrange("p (g d) -> p g d", d=QK)
                    rg = rowbuf[:, b, g0:, :, :]
                    link(v.tensor_tensor(rg, rg, gains.unsqueeze(2).to_broadcast([P, gn, HEADS, QK]), ALU.mult))
                    if n < 2:
                        H = 8 * gn
                        hf = ROPE // 2
                        x1, x2 = rb[:, :, NOPE:NOPE + hf], rb[:, :, NOPE + hf:QK]
                        cc = cos[:, n, :].unsqueeze(1).to_broadcast([P, H, hf])
                        ss = sin[:, n, :].unsqueeze(1).to_broadcast([P, H, hf])
                        v.tensor_tensor(rtmp[:, 0, 0:H, :], x1, cc, ALU.mult)
                        v.tensor_tensor(rtmp[:, 1, 0:H, :], x2, ss, ALU.mult)
                        v.tensor_tensor(rtmp[:, 2, 0:H, :], x2, cc, ALU.mult)
                        link(v.tensor_tensor(rtmp[:, 3, 0:H, :], x1, ss, ALU.mult))
                        v.tensor_tensor(x1, rtmp[:, 0, 0:H, :], rtmp[:, 1, 0:H, :], ALU.subtract)
                        link(v.tensor_tensor(x2, rtmp[:, 2, 0:H, :], rtmp[:, 3, 0:H, :], ALU.add))
                    v.sem_inc(rown_ready.sem, 1)

                units = mixer_units(l)

                def unit_max(i):
                    t, h = units[i]
                    k0 = 0 if t < 2 else SEQ
                    v.wait_ge(sc_mm.sem, sc_mm.at(l, i + 1))
                    link(v.tensor_reduce(asm[:, i % 2, 0:1], ps[i % 2][:, k0:COLS], AX.X, ALU.max))
                    v.tensor_scalar(asm[:, i % 2, 1:2], asm[:, i % 2, 0:1], -SCALE, None, ALU.mult).then_inc(smax.sem, 1)

                def unit_norm(i):
                    t, h = units[i]
                    k0 = 0 if t < 2 else SEQ
                    v.wait_ge(e_done.sem, e_done.at(l, i + 1))
                    link(v.reciprocal(asm[:, i % 2, 3:4], asm[:, i % 2, 2:3]))
                    v.tensor_scalar(prob[:, i % 2, k0:COLS], prob[:, i % 2, k0:COLS], asm[:, i % 2, 3:4], None, ALU.mult).then_inc(p_ready.sem, 1)

                def pair_out(j):
                    t, h = units[2 * j]
                    v.wait_ge(pv_mm.sem, pv_mm.at(l, j + 1))
                    v.tensor_copy(hT[:, 2 + h // 2, t * P:(t + 1) * P], ps[4 + j % 2][:, 0:P]).then_inc(attn_out.sem, 1)

                nu = len(units)
                for i in range(nu + 4):
                    if i < nu:
                        unit_max(i)
                    if 1 <= i <= nu:
                        unit_norm(i - 1)
                    if i >= 4 and (i - 4) % 2 == 1:
                        pair_out((i - 4) // 2)

                mu = ml_units(l)

                def masked(i, e):
                    u = 2 * i + e
                    if e == 0:
                        v.wait_ge(st_mm.sem, st_mm.at(l, i + 1))
                    if u >= 2:
                        v.wait_ge(mE_ready.sem, mE_ready.at(l, u - 1))
                    if mu[i][0] == 0:
                        v.tensor_scalar(marg[:, e, 2, :], ps[4 + i % 2][:, e * 256:e * 256 + 256], -1.0, None, ALU.mult)
                    v.tensor_tensor(marg[:, e, 0:2, :], mask[:, e, :, :],
                                    ps[4 + i % 2][:, e * 256:e * 256 + 256].unsqueeze(1).to_broadcast([P, 2, 256]),
                                    ALU.subtract).then_inc(marg_ready.sem, 1)

                def weighted(i, e):
                    s, h = mu[i]
                    u = 2 * i + e
                    v.wait_ge(mE_ready.sem, mE_ready.at(l, u + 1))
                    if i >= 1:
                        v.wait_ge(num_mm.sem, num_mm.at(l, i))
                    b0 = 2 * (i % 2)
                    for j in ((0, 1) if s == 0 else (1,)):
                        ins = v.tensor_tensor(mP[:, e, 2 * j:2 * j + 2, :], mE[:, e, 2 * j:2 * j + 2, :],
                                              ps[b0 + j][:, :].rearrange("p (c q) -> p c q", c=2), ALU.mult)
                    ins.then_inc(mP_ready.sem, 1)

                def combine(n):
                    s = streams[l][n]
                    v.wait_ge(num_evac.sem, num_evac.at(l, MH * (n + 1)))
                    den = numS[:, :, :, :, MD:MD + 1].rearrange("p q e h o -> p (q e h) o")
                    md = mden[:, :, :].unsqueeze(3)
                    link(v.scalar_tensor_tensor(out=md[:, 0, :, :], in0=den, scalar=-1.0, in1=den, op0=ALU.mult, op1=ALU.max))
                    link(v.tensor_tensor(mden[:, 0, :], mden[:, 0, :], gcol[:, 1, 2 * s:2 * s + 2, :].rearrange("p t r -> p (t r)"), ALU.max))
                    link(v.reciprocal(mden[:, 1, :], mden[:, 0, :]))
                    link(v.tensor_tensor(hn.rearrange("p q e h d -> p (q e h) d"), numS[:, :, :, :, 0:MD].rearrange("p q e h d -> p (q e h) d"),
                                         mden[:, 1, :].unsqueeze(2).to_broadcast([P, 16, MD]), ALU.mult))
                    v.tensor_tensor(hs, hn[:, :, 0, :, :], hn[:, :, 1, :, :], ALU.add).then_inc(hq_ready.sem, 1)
                    v.wait_ge(hsq_ready.sem, hsq_ready.at(l, n + 1))
                    link(v.tensor_reduce(mden[:, 0, 0:8], hq.rearrange("p q h d -> p (q h) d"), AX.X, ALU.add))
                    link(v.tensor_scalar(mden[:, 0, 0:8], mden[:, 0, 0:8], 1.0 / MD, EPS, ALU.mult, ALU.add))
                    v.sem_inc(hss_ready.sem, 1)
                    v.wait_ge(hrt_ready.sem, hrt_ready.at(l, n + 1))
                    link(v.reciprocal(mden[:, 2, 0:8], mden[:, 1, 0:8]))
                    h3 = hs.rearrange("p q h d -> p (q h) d")
                    link(v.tensor_tensor(h3, h3, mden[:, 2, 0:8].unsqueeze(2).to_broadcast([P, 8, MD]), ALU.mult))
                    h2 = hs.rearrange("p q h d -> p q (h d)")
                    link(v.tensor_tensor(h2, h2, par[:, l, PB_ML:PB_ML + MH * MD].unsqueeze(1).to_broadcast([P, 2, MH * MD]), ALU.mult))
                    if n:
                        v.wait_ge(mt_mm.sem, mt_mm.at(l, n))
                    v.tensor_tensor(osig[:, 2 * s:2 * s + 2, :], osig[:, 2 * s:2 * s + 2, :], h2, ALU.mult).then_inc(ml_ready.sem, 1)

                for i in range(len(mu)):
                    masked(i, 0)
                    masked(i, 1)
                    weighted(i, 0)
                    weighted(i, 1)
                    if i % MH == MH - 1:
                        combine(i // MH)

                for k in range(KC):
                    v.wait_ge(out_mm.sem, out_mm.at(l, k + 1))
                    for s in streams[l]:
                        ins = v.scalar_tensor_tensor(out=xT[:, k, s * SEQ:(s + 1) * SEQ], in0=ps[4 + k % 2][:, s * SEQ:(s + 1) * SEQ],
                                                     scalar=modT[:, 16 + k, s:s + 1], in1=xT[:, k, s * SEQ:(s + 1) * SEQ],
                                                     op0=ALU.mult, op1=ALU.add)
                    ins.then_inc(x_mid.sem, 1)
                v.wait_ge(x_mid.sem, x_mid.at(l, KC))
                inv_rms(l, 4, D, c1)
                for k in range(KC):
                    v.tensor_tensor(hT[:, k, 0:c1], xT[:, k, 0:c1], rms[:, 0:c1], ALU.mult).then_inc(hx_ready.sem, 1)

                for q in range(HC):
                    v.wait_ge(psc_mm.sem, psc_mm.at(l, q + 1))
                    for t in tiles[l]:
                        sc = ps[2 + q % 2][:, t * P:(t + 1) * P]
                        tv, ti = topv[:, t, q, :], topiu[:, t, q, :]
                        link(v.max(tv[:, 0:8], sc))
                        v.max_index(ti[:, 0:8], tv[:, 0:8], sc)
                        link(v.match_replace(s2[:, 0:P], tv[:, 0:8], sc, NEG))
                        link(v.max(tv[:, 8:16], s2[:, 0:P]))
                        link(v.max_index(ti[:, 8:16], tv[:, 8:16], s2[:, 0:P]))
                    v.sem_inc(top_done.sem, 1)
                for t in tiles[l]:
                    link(v.tensor_copy(topi[:, t, :, :], topiu[:, t, :, :]))

                def choose(n):
                    t = tiles[l][n]
                    b = (n if l == 0 else 4 + n) % 2
                    c4 = cand.rearrange("p (h i j) -> p h i j", h=PH, i=PTOP)
                    tv = topv[:, t, :, :].rearrange("p (h c) k -> p h c k", c=2)
                    ti = topi[:, t, :, :].rearrange("p (h c) k -> p h c k", c=2)
                    link(v.tensor_tensor(c4, tv[:, :, 0, :].unsqueeze(3).to_broadcast([P, PH, PTOP, PTOP]),
                                         tv[:, :, 1, :].unsqueeze(2).to_broadcast([P, PH, PTOP, PTOP]), ALU.add))
                    for h in range(PH):
                        cd = cand[:, h * 256:(h + 1) * 256]
                        o = h * PTOP
                        link(v.max(bv[:, b, o:o + 8], cd))
                        v.max_index(bi[:, o:o + 8], bv[:, b, o:o + 8], cd)
                        link(v.match_replace(s2[:, :], bv[:, b, o:o + 8], cd, NEG))
                        link(v.max(bv[:, b, o + 8:o + 16], s2[:, :]))
                        link(v.max_index(bi[:, o + 8:o + 16], bv[:, b, o + 8:o + 16], s2[:, :]))
                    biI = bi[:, :].bitcast(I32)
                    r1I, r2I = r1[:, :].bitcast(I32), r2[:, :].bitcast(I32)
                    v.tensor_scalar(r1I, biI, 4, None, ALU.arith_shift_right)
                    link(v.tensor_scalar(r2I, biI, 15, None, ALU.bitwise_and))
                    for r_, rI, c in ((r1, r1I, 0), (r2, r2I, 1)):
                        link(v.tensor_copy(bf[:, :], rI))
                        link(v.tensor_tensor(c4, bf[:, :].rearrange("p (h k) -> p h k", h=PH).unsqueeze(3).to_broadcast([P, PH, PTOP, PTOP]),
                                             iota16.unsqueeze(1).unsqueeze(1).to_broadcast([P, PH, PTOP, PTOP]), ALU.is_equal))
                        link(v.tensor_tensor(c4, c4, ti[:, :, c, :].unsqueeze(2).to_broadcast([P, PH, PTOP, PTOP]), ALU.mult))
                        link(v.tensor_reduce(r_[:, :], cand.rearrange("p (s j) -> p s j", j=PTOP), AX.X, ALU.add))
                    link(v.scalar_tensor_tensor(out=idx[:, b, :], in0=r1[:, :], scalar=float(PKEYS), in1=r2[:, :], op0=ALU.mult, op1=ALU.add))
                    v.sem_inc(idx_ready.sem, 1)
                    b3 = bv[:, b, :].rearrange("p (h k) -> p h k", h=PH)
                    link(v.tensor_copy(esum[:, 0, :].unsqueeze(2), b3[:, :, 0:1]))
                    v.tensor_tensor(b3, b3, esum[:, 0, :].unsqueeze(2).to_broadcast([P, PH, PTOP]), ALU.subtract).then_inc(sub_ready.sem, 1)

                def dots(n):
                    t = tiles[l][n]
                    tile = n if l == 0 else 4 + n
                    v.wait_ge(hr_ready.sem, hr_ready.at(l, 2 * n + 2))
                    with v.Fori(0, ITERS) as it:
                        for s in range(RING):
                            v.wait_ge(landed[s], it * 16 + (tile * 2 * ITERS + 1) * 16)
                            v.scalar_tensor_tensor(out=ring[:, s, :], in0=ring[:, s, :], scalar=1.0, in1=hrow[:, t, :],
                                                   op0=ALU.mult, op1=ALU.mult,
                                                   accum_out=araw[:, bass.ds(it * RING + s, 1)]).then_inc(u_used, 1)
                    v.wait_ge(u_used, (tile + 1) * SLOTS + RING)
                    v.sem_inc(u_done.sem, 1)

                def weights(n):
                    b = (n if l == 0 else 4 + n) % 2
                    b3 = bv[:, b, :].rearrange("p (h k) -> p h k", h=PH)
                    w3 = wts[:, b, :].rearrange("p (h k) -> p h k", h=PH)
                    v.wait_ge(ex_ready.sem, ex_ready.at(l, n + 1))
                    link(v.tensor_reduce(esum[:, 0, :], b3, AX.X, ALU.add))
                    link(v.reciprocal(esum[:, 1, :], esum[:, 0, :]))
                    link(v.tensor_tensor(w3, b3, esum[:, 1, :].unsqueeze(2).to_broadcast([P, PH, PTOP]), ALU.mult))
                    v.wait_ge(gelu_ready.sem, gelu_ready.at(l, n + 1))
                    link(v.tensor_tensor(wts[:, b, :], wts[:, b, :], gact[:, :], ALU.mult))
                    v.sem_inc(w_ready.sem, 1)

                def add_experts(n):
                    t = tiles[l][n]
                    s = t // 2
                    for f in range(2):
                        v.wait_ge(yt_mm.sem, yt_mm.at(l, 2 * n + f + 1))
                        for j in range(4):
                            k = 4 * f + j
                            ins = v.scalar_tensor_tensor(out=xT[:, k, t * P:(t + 1) * P], in0=ps[f][:, j * P:(j + 1) * P],
                                                         scalar=modT0(k, s), in1=xT[:, k, t * P:(t + 1) * P],
                                                         op0=ALU.mult, op1=ALU.add)
                            link(ins)
                    v.sem_inc(x_done.sem, 1)

                link(v.tensor_copy(gate_f[:, :, :], modT[:, 40:48, :]))

                def modT0(k, s):
                    return gate_f[:, k, s:s + 1]

                for n in range(len(tiles[l])):
                    choose(n)
                    dots(n)
                    weights(n)
                    if n:
                        add_experts(n - 1)
                    if l == 0 and n == 1:
                        ada_out(1)
                add_experts(len(tiles[l]) - 1)

        @block.tensor
        def _(p):
            def tile_in(n):
                p.wait_ge(w_landed[n % WSLOTS], 16 * (n // WSLOTS + 1))
                return wring[:, n % WSLOTS, :, :]

            def ada(l):
                base = l * LAYER_TILES
                with p.Fori(0, ADA_TILES // WSLOTS) as i:
                    for s in range(WSLOTS):
                        p.wait_ge(w_landed[s], i * 16 + 16 * (base // WSLOTS + 1))
                        for b in range(2):
                            for k in range(KC):
                                mm = p.matmul(ps[5][:, bass.ds(i * (4 * WSLOTS) + (4 * s + 2 * b), 2)], wring[:, s, k, b * P:(b + 1) * P], cS[:, k, :],
                                              start=(k == 0), stop=(k == KC - 1))
                        mm.then_inc(w_free, 1)
                p.wait_ge(w_free, WSLOTS + base + ADA_TILES)
                p.sem_inc(ada_mm.sem, 1)

            sqn = [0]

            def sum_squares(l, n, bank, c1, sig):
                for k in range(n):
                    sqn[0] += 1
                    p.wait_ge(sq_ready.sem, sqn[0])
                    mm = p.matmul(ps[bank][:, 0:c1], ones, sq[:, sqn[0] % 2, 0:c1], start=(k == 0), stop=(k == n - 1)).then_inc(sq_used.sem, 1)
                p.wait_ge(sq_used.sem, sqn[0])
                p.sem_inc(ss_ready.sem, 1)

            p.sem_inc(w_free, WSLOTS)
            p.wait_ge(cs_ready, 1)
            ada(0)
            for l in range(DEPTH):
                c1 = full[l][1]
                ns = len(streams[l])
                base = l * LAYER_TILES + ADA_TILES
                sum_squares(l, KC, 0, COLS, 1)

                g = [0]

                def group():
                    g[0] += 1
                    if g[0] > 2:
                        p.wait_ge(in_evac.sem, in_evac.at(l, g[0] - 2))
                    return ps[2 + g[0] % 2]

                for b in range(12):
                    if b % 2 == 0:
                        wt = tile_in(base + b // 2)
                    dst = group()
                    n = c1 if (b < 5 or 7 <= b < 9) else COLS
                    m = P if b < 11 else 40
                    o = (b % 2) * P
                    for k in range(KC):
                        if b == 0:
                            p.wait_ge(h_ready.sem, h_ready.at(l, k + 1))
                        mm = p.matmul(dst[0:m, 0:n], wt[:, k, o:o + m], hT[:, k, 0:n], start=(k == 0), stop=(k == KC - 1))
                    mm.then_inc(in_mm.sem, 1)
                    if b % 2 == 1 and b < 11:
                        p.wait_ge(in_mm.sem, in_mm.at(l, g[0]))
                        p.sem_inc(w_free, 1)
                dst = group()
                for t in range(4):
                    for k in range(KC):
                        mm = p.matmul(dst[:, t * ROPE:(t + 1) * ROPE], hT[:, k, t * P:(t + 1) * P], wt[:, k, P + 40:P + 72], start=(k == 0), stop=(k == KC - 1))
                mm.then_inc(in_mm.sem, 1)
                p.wait_ge(in_mm.sem, in_mm.at(l, g[0]))
                p.sem_inc(w_free, 1)
                for j in range(2):
                    wt = tile_in(base + 6 + j)
                    for t in (range(4) if j == 0 else tiles[l]):
                        dst = group()
                        for k in range(KC):
                            mm = p.matmul(dst[:, 0:WT], hT[:, k, t * P:(t + 1) * P], wt[:, k, :], start=(k == 0), stop=(k == KC - 1))
                        mm.then_inc(in_mm.sem, 1)
                    p.wait_ge(in_mm.sem, in_mm.at(l, g[0]))
                    p.sem_inc(w_free, 1)

                sum_squares(l, 3, 0, c1, 2)
                sum_squares(l, 2, 1, COLS, 3)

                p.wait_ge(gm_ready.sem, gm_ready.at(l, 1))
                p.wait_ge(em_ready.sem, em_ready.at(l, 1))
                p.wait_ge(ms_ready.sem, ms_ready.at(l, 2))
                for q, j in ((0, 0), (1, 2)):
                    for t in range(4):
                        mm = p.transpose(ps[0][:, q * 32 + t * 8:q * 32 + t * 8 + 8], gcm[:, j, t * P:(t + 1) * P], ident[0:8, 0:8])
                mm.then_inc(gt_mm.sem, 1)

                p.wait_ge(mixw, 48 * (l + 1))
                p.wait_ge(pool_ready.sem, pool_ready.at(l, 1))
                if l == 0:
                    p.wait_ge(mod_ready.sem, 1)
                for c in range(2):
                    for f in range(2):
                        mm = p.matmul(ps[4 + c][64 * f:64 * f + 64, 0:c1], poolw[64 * f:64 * f + 64, c, :],
                                      pa_[64 * f:64 * f + 64, c, 0:ns, PAD:PAD + SEQ], start=True, stop=True)
                    mm.then_inc(pool_mm.sem, 1)

                def trs(n):
                    at = sum(4 if m in tiles[l] else 2 for m in range(n))
                    return [tr_mm.at(l, at + j + 1) for j in range(4 if n in tiles[l] else 2)]

                def qk_rows(n):
                    if n == 0:
                        p.wait_ge(zn_ready.sem, zn_ready.at(l, 5))
                        p.wait_ge(gc_ready.sem, gc_ready.at(l, 1))
                        p.wait_ge(in_evac.sem, in_evac.at(l, 21 if l == 0 else 19))
                    else:
                        p.wait_ge(row_ready.sem, row_ready.at(l, n))
                    if n in tiles[l]:
                        for f in range(2):
                            for k in range(3):
                                p.matmul(ps[f][:, 0:384], zqT[:, k, n * P:(n + 1) * P], uqw[:, k, f * 384:(f + 1) * 384], start=(k == 0), stop=(k == 2))
                    for f in range(2):
                        for k in range(2):
                            mm = p.matmul(ps[2 + f][:, :], zkvT[:, k, n * P:(n + 1) * P], ukvw[:, k, f * 512:(f + 1) * 512], start=(k == 0), stop=(k == 1))
                    mm.then_inc(qk_mm.sem, 1)

                def row_transposes(n):
                    p.wait_ge(rown_ready.sem, rown_ready.at(l, n + 1))
                    if n == 0:
                        p.wait_ge(pool_out.sem, pool_out.at(l, 2))
                    what = [(1, f) for f in range(2)]
                    if n in tiles[l]:
                        what = [(0, f) for f in range(2)] + what
                    for (g_, f), val in zip(what, trs(n)):
                        if val - 2 > tr_mm.start[l]:
                            p.wait_ge(tr_evac.sem, val - 2)
                        for j in range(4):
                            mm = p.transpose(ps[4 + (val - 1) % 2][0:QK, j * P:(j + 1) * P], rowbuf[:, n % 2, g_, 4 * f + j, :], ident)
                        mm.then_inc(tr_mm.sem, 1)

                for n in range(4):
                    qk_rows(n)
                    if n:
                        row_transposes(n - 1)
                row_transposes(3)

                units = mixer_units(l)
                nu = len(units)

                def scores(i):
                    t, h = units[i]
                    k0 = 0 if t < 2 else SEQ
                    if i == 0:
                        p.wait_ge(tr_evac.sem, trs(3)[-1])
                    if i >= 2:
                        p.wait_ge(e_done.sem, e_done.at(l, i - 1))
                    p.matmul(ps[i % 2][:, k0:COLS], qT[0:QK, h, t * P:(t + 1) * P], kT[0:QK, h, k0:COLS], start=True, stop=True).then_inc(sc_mm.sem, 1)

                def prob_transposes(i):
                    t, h = units[i]
                    p.wait_ge(p_ready.sem, p_ready.at(l, i + 1))
                    if i >= 2:
                        p.wait_ge(pt_ready.sem, pt_ready.at(l, i - 1))
                    for j in range(0 if t < 2 else 2, 4):
                        mm = p.transpose(ps[2 + i % 2][:, j * P:(j + 1) * P], prob[:, i % 2, j * P:(j + 1) * P], ident)
                    mm.then_inc(pt_mm.sem, 1)

                def outputs(i):
                    t, h = units[i]
                    j_ = i // 2
                    p.wait_ge(pt_ready.sem, pt_ready.at(l, i + 1))
                    if i % 2 == 0 and j_ >= 2:
                        p.wait_ge(attn_out.sem, attn_out.at(l, j_ - 1))
                    f = h % 2
                    js = range(0 if t < 2 else 2, 4)
                    for j in js:
                        mm = p.matmul(ps[4 + j_ % 2][64 * f:64 * f + 64, 0:P], vrow[:, j, h * VD:(h + 1) * VD], pt[:, i % 2, j, :],
                                      start=(j == js[0]), stop=(j == 3))
                    if f:
                        mm.then_inc(pv_mm.sem, 1)

                for i in range(nu + 2):
                    if i < nu:
                        scores(i)
                    if 1 <= i <= nu:
                        prob_transposes(i - 1)
                    if i >= 2:
                        outputs(i - 2)

                mu = ml_units(l)

                def state_scores(i):
                    s, h = mu[i]
                    f, c = h % 2, h // 2
                    if i == 0:
                        p.wait_ge(attn_out.sem, attn_out.at(l, nu // 2))
                    if i >= 2:
                        p.wait_ge(mP_ready.sem, mP_ready.at(l, 2 * i - 2))
                    for kc in (range(4) if s == 0 else (2, 3)):
                        p.matmul(ps[2 * (i % 2) + kc // 2][:, (kc % 2) * 256:(kc % 2) * 256 + 256],
                                 mkT[64 * f:64 * f + 64, c, kc * P:(kc + 1) * P], mqT[64 * f:64 * f + 64, c, s * SEQ:(s + 1) * SEQ],
                                 start=True, stop=True)
                    for e in range(DIRS):
                        r = e * MH + h
                        mm = p.matmul(ps[4 + i % 2][:, e * 256:e * 256 + 256], ident[0:8, r:r + 1].to_broadcast([8, P]),
                                      gcm[:, 1, s * SEQ:(s + 1) * SEQ], start=True, stop=True)
                    mm.then_inc(st_mm.sem, 1)

                def numerators(i):
                    s, h = mu[i]
                    p.wait_ge(mP_ready.sem, mP_ready.at(l, 2 * i + 2))
                    if i >= 2:
                        p.wait_ge(num_evac.sem, num_evac.at(l, i - 1))
                    kcs = list(range(4)) if s == 0 else [2, 3]
                    for e in range(DIRS):
                        for q in range(2):
                            o = (q * 2 + e) * (MD + 1)
                            for kc in kcs:
                                mm = p.matmul(ps[6 + i % 2][:, o:o + MD + 1], mP[:, e, kc, q * P:(q + 1) * P], v1[:, kc, h, :],
                                              start=(kc == kcs[0]), stop=(kc == 3))
                    mm.then_inc(num_mm.sem, 1)

                def ml_transposes(n):
                    s = streams[l][n]
                    p.wait_ge(ml_ready.sem, ml_ready.at(l, n + 1))
                    if n:
                        p.wait_ge(mt_evac.sem, mt_evac.at(l, n))
                    for c in range(2):
                        for q in range(2):
                            mm = p.transpose(ps[3][:, c * SEQ + q * P:c * SEQ + (q + 1) * P], osig[:, 2 * s + q, c * P:(c + 1) * P], ident)
                    mm.then_inc(mt_mm.sem, 1)

                for i in range(len(mu) + 1):
                    if i < len(mu):
                        state_scores(i)
                    if i:
                        numerators(i - 1)
                for n in range(len(streams[l])):
                    ml_transposes(n)

                for b in range(8):
                    if b % 2 == 0:
                        wt = tile_in(base + IN_TILES + b // 2)
                    if b == 0:
                        p.wait_ge(mt_evac.sem, mt_evac.at(l, len(streams[l])))
                        p.wait_ge(marg_ready.sem, marg_ready.at(l, 2 * len(mu)))
                    if b >= 2:
                        p.wait_ge(x_mid.sem, x_mid.at(l, b - 1))
                    for k in range(KC):
                        mm = p.matmul(ps[4 + b % 2][:, 0:c1], wt[:, k, (b % 2) * P:(b % 2 + 1) * P], hT[:, k, 0:c1], start=(k == 0), stop=(k == KC - 1))
                    mm.then_inc(out_mm.sem, 1)
                    if b % 2:
                        p.wait_ge(out_mm.sem, out_mm.at(l, b + 1))
                        p.sem_inc(w_free, 1)
                sum_squares(l, KC, 0, c1, 4)

                for j in range(2 * len(tiles[l])):
                    t, f = j // 2, j % 2
                    if j < 2:
                        p.wait_ge(x_mid.sem, x_mid.at(l, KC))
                        p.wait_ge(h_ready.sem, h_ready.at(l, 2 * KC))
                    else:
                        p.wait_ge(hr_ready.sem, hr_ready.at(l, j - 1))
                    for k in range(4):
                        mm = p.transpose(ps[4 + j % 2][:, k * P:(k + 1) * P], hT[:, 4 * f + k, t * P:(t + 1) * P], ident)
                    mm.then_inc(hr_mm.sem, 1)

                def query(q):
                    if q % 2 == 0:
                        tile_in(base + IN_TILES + OUT_TILES + q // 2)
                    wt = wring[:, (base + IN_TILES + OUT_TILES + q // 2) % WSLOTS, :, :]
                    if q == 0:
                        p.wait_ge(ms_ready.sem, ms_ready.at(l, 4))
                    if q >= 2:
                        p.wait_ge(pq_ready.sem, pq_ready.at(l, q - 1))
                    for k in range(KC):
                        mm = p.matmul(ps[q % 2][:, 0:c1], wt[:, k, (q % 2) * P:(q % 2 + 1) * P], hT[:, k, 0:c1], start=(k == 0), stop=(k == KC - 1))
                    mm.then_inc(pq_mm.sem, 1)
                    if q % 2:
                        p.wait_ge(pq_mm.sem, pq_mm.at(l, q + 1))
                        p.sem_inc(w_free, 1)

                def key_scores(q):
                    p.wait_ge(pq_ready.sem, pq_ready.at(l, q + 1))
                    if q == 0:
                        p.wait_ge(skw, 16 * (l + 1))
                    if q >= 2:
                        p.wait_ge(top_done.sem, top_done.at(l, q - 1))
                    for t in tiles[l]:
                        mm = p.matmul(ps[2 + q % 2][:, t * P:(t + 1) * P], pq[:, q % 2, t * P:(t + 1) * P], subk[:, q, :], start=True, stop=True)
                    mm.then_inc(psc_mm.sem, 1)

                for q in range(HC + 1):
                    if q < HC:
                        query(q)
                    if q:
                        key_scores(q - 1)

                for n in range(len(tiles[l])):
                    tile = n if l == 0 else 4 + n
                    if n:
                        p.wait_ge(y_ready.sem, y_ready.at(l, n))
                    if tile == 0:
                        p.wait_ge(init_done, 1)
                    for f in range(2):
                        p.matmul(acc[:, f * 512:f * 512 + 512], zrow[0:1, :], con[0:1, 0:512], start=True, stop=False, skip_group_check=True)
                    with p.Fori(0, ITERS) as it:
                        for s in range(RING):
                            p.wait_ge(landed[s], it * 16 + (tile * 2 * ITERS + ITERS + 1) * 16)
                            p.wait_ge(diag_ready, it * RING + (tile * SLOTS + s + 1))
                            for f in range(2):
                                mm = p.matmul(acc[:, f * 512:f * 512 + 512], diag[:, s % DIAGS, :], ring[:, s, f * 512:f * 512 + 512],
                                              start=False, stop=False, skip_group_check=True)
                            mm.then_inc(v_used, 1)
                    for f in range(2):
                        mm = p.matmul(acc[:, f * 512:f * 512 + 512], zrow[0:1, :], con[0:1, 0:512], start=False, stop=True, skip_group_check=True)
                    mm.then_inc(acc_done.sem, 1)
                    if l == 0 and n == 0:
                        ada(1)
                    p.wait_ge(y_ready.sem, y_ready.at(l, n + 1))
                    for f in range(2):
                        if n:
                            p.wait_ge(x_done.sem, x_done.at(l, n))
                        for j in range(4):
                            mm = p.transpose(ps[f][:, j * P:(j + 1) * P], yrow[:, (4 * f + j) * P:(4 * f + j + 1) * P], ident)
                        mm.then_inc(yt_mm.sem, 1)


def constants():
    con = np.zeros((P, CB), np.float32)
    con[:, C_ID:C_ID + P] = np.eye(P)
    con[:, C_ONE:C_ONE + P] = 1.0
    key = np.arange(256)[:, None]
    query = np.arange(256)[None, :]
    allowed = (query >= key, query <= key)
    for e in range(2):
        m = np.where(allowed[e], 0.0, NEG)
        for k in range(2):
            o = C_MASK + (e * 2 + k) * 256
            con[:, o:o + 256] = m[k * P:(k + 1) * P]
    t = np.arange(SEQ)
    for g, w in enumerate(WINDOWS):
        n = np.clip(t + w // 2, 0, SEQ) - np.clip(t - w // 2, 0, SEQ)
        o = C_INV + (g // 2) * 256
        con[(g % 2) * 64:(g % 2) * 64 + 64, o:o + 256] = 1.0 / n
    per = ROPE // 2
    freqs = np.float32(ROPE_BASE) ** (-np.arange(0, per, 2, dtype=np.float32) / np.float32(per))
    row = (t // GRID_W).astype(np.float32)
    col = (t % GRID_W).astype(np.float32)
    ang = np.concatenate([row[:, None] * freqs, col[:, None] * freqs], axis=-1)
    con[:, C_COS:C_COS + 32] = np.cos(ang).reshape(2, P, 16).transpose(1, 0, 2).reshape(P, 32)
    con[:, C_SIN:C_SIN + 32] = np.sin(ang).reshape(2, P, 16).transpose(1, 0, 2).reshape(P, 32)
    con[0:4, C_DIR] = 1.0
    con[4:8, C_DIR + 1] = 1.0
    con[:, C_IOTA:C_IOTA + 16] = np.arange(16)
    return con


def kernel(**inputs):
    import concourse.bacc as _bacc
    from concourse.bass_utils import run_bass_kernel_spmd as _run

    i = {k: np.asarray(v) for k, v in inputs.items()}
    f32 = np.float32

    def chan(a, n):
        return a.reshape(n, P).T

    x_in = np.concatenate([i["x"][0], i["ctx"][0]], axis=0).T.reshape(KC, P, COLS).transpose(1, 0, 2)
    c_in = np.stack([i["c"][0], i["c_ctx"]], axis=-1).reshape(KC, P, 2).transpose(1, 0, 2)
    par = np.zeros((P, DEPTH, PB), f32)
    tiles = np.zeros((DEPTH, LAYER_TILES, P, KC, WT), f32)
    for l in range(DEPTH):
        par[:, l, PB_ADA:PB_ADA + 48] = chan(i["b_ada"][l], 48)
        par[:, l, PB_G1:PB_G1 + 8] = chan(i["norm1_gain"][l], 8)
        par[:, l, PB_G2:PB_G2 + 8] = chan(i["norm2_gain"][l], 8)
        par[:, l, PB_PS:PB_PS + 2] = chan(i["pool_scale"][l], 2)
        par[:, l, PB_QN:PB_QN + 3] = chan(i["mla_q_norm"][l], 3)
        par[:, l, PB_KVN:PB_KVN + 2] = chan(i["mla_kv_norm"][l], 2)
        gb = i["ml_gate_bias"][l].reshape(4, MH)
        par[0:4, l, PB_GI], par[4:8, l, PB_GI] = gb[0], gb[2]
        par[0:4, l, PB_GF], par[4:8, l, PB_GF] = gb[1], gb[3]
        par[:, l, PB_QG:PB_QG + QK] = i["q_norm"][l]
        par[:, l, PB_KG:PB_KG + QK] = i["k_norm"][l]
        par[:, l, PB_ML:PB_ML + MH * MD] = i["ml_out_norm"][l].reshape(-1)
        w = i["w_in"][l]
        wi = np.zeros((D, IN_TILES * WT), f32)
        wi[:, 0:896] = w[:, 0:896]
        wi[:, 896:1408] = w[:, 928:1440]
        g = w[:, 1952:1968].reshape(D, 4, MH)
        wi[:, 1408:1412], wi[:, 1412:1416] = g[:, 0], g[:, 2]
        wi[:, 1440:1444], wi[:, 1444:1448] = g[:, 1], g[:, 3]
        wi[:, 1448:1480] = w[:, 896:928]
        wi[:, 1536:2048] = w[:, 1440:1952]
        at = 0
        for m in (i["w_ada"][l], wi, i["w_out"][l], i["peer_wq"][l]):
            n = m.shape[1] // WT
            tiles[l, at:at + n] = m.reshape(KC, P, n, WT).transpose(2, 1, 0, 3)
            at += n
    uq = i["w_uq"].reshape(DEPTH, 3, P, 768).transpose(0, 2, 1, 3)
    ukv = i["w_ukv"].reshape(DEPTH, 2, P, 1024).transpose(0, 2, 1, 3)
    pw = i["pool_w"].reshape(DEPTH, 2, 2 * PGROUP, PGROUP).transpose(0, 2, 1, 3)
    sk = i["peer_subkeys"].reshape(DEPTH, HC, PKEYS, PDK).transpose(0, 3, 1, 2)

    nc = _bacc.Bacc("TRN2", target_bir_lowering=False, num_devices=1)
    arrays = {}

    def put(name, a):
        a = np.ascontiguousarray(a)
        arrays[name + "_dram"] = a
        return nc.dram_tensor(name + "_dram", a.shape, mybir.dt.from_np(a.dtype), kind="ExternalInput").ap()

    args = [put("x", x_in), put("c", c_in), put("par", par), put("con", constants()),
            put("w", tiles.reshape(DEPTH * LAYER_TILES, P, KC * WT)), put("uq", uq), put("ukv", ukv), put("pw", pw), put("sk", sk)]
    args.append([put(f"u{l}", i["peer_u"][l]) for l in range(DEPTH)])
    args.append([put(f"v{l}", i["peer_v"][l]) for l in range(DEPTH)])
    args.append(nc.dram_tensor("out_dram", (P, KC, SEQ), F32, kind="ExternalOutput").ap())
    build(nc, *args)
    r = _run(nc, [arrays], core_ids=[0])
    return np.ascontiguousarray(r.results[0]["out_dram"].transpose(2, 1, 0)).reshape(1, SEQ, D)
```

```python
from contextlib import ExitStack

import numpy as np

import concourse.bass as bass
from concourse import mybir

ALU = mybir.AluOpType
ACT = mybir.ActivationFunctionType
AX = mybir.AxisListType
F32 = mybir.dt.float32
I32 = mybir.dt.int32
U32 = mybir.dt.uint32

P = 128
D = 1024
KC = D // P
SEQ = 256
CTX = 256
COLS = SEQ + CTX
DEPTH = 2
EPS = 1e-6
NEG = -1e30
GRID_W = 64

WINDOWS = (2, 4, 8, 16)
PGROUP = 64
PAD = max(WINDOWS) // 2
PLEN = SEQ + 2 * PAD

HEADS, NOPE, ROPE, QK, VD = 8, 64, 32, 96, 64
QRANK, KVRANK = 384, 256
SCALE = QK ** -0.5
ROPE_BASE = 10000.0

MH, MD = 4, 64
DIRS = 2

PH, PTOP, PKEYS, PDK = 8, 16, 128, 128
HC = 2 * PH
SLOTS = PH * PTOP

WT = 256
WSLOTS = 4
ADA_TILES = 6 * D // WT
ADA_FIRST = 2 * D // WT
PAIRS = (ADA_TILES - ADA_FIRST) // 2
PAIRS_AT = (2, 4, 5, 6, 8)
IN_TILES = 8
OUT_TILES = D // WT
PQ_TILES = HC * PDK // WT
LAYER_TILES = ADA_TILES + IN_TILES + OUT_TILES + PQ_TILES

RING = 8
GROUP = 2
DIAGS = 4

PB_ADA, PB_G1, PB_G2, PB_PS, PB_QN, PB_KVN, PB_GI, PB_GF = 0, 48, 56, 64, 66, 69, 71, 72
PB_QG, PB_KG, PB_ML = 73, 73 + QK, 73 + 2 * QK
PB = PB_ML + MH * MD
C_ID, C_ONE = 0, 128
C_MASK = 256
C_INV = C_MASK + DIRS * 2 * 256
C_COS = C_INV + 2 * 256
C_SIN = C_COS + 32
C_DIR = C_SIN + 32
C_IOTA = C_DIR + 2
CB = C_IOTA + 16


class Signal:

    def __init__(self, ctx, nc, name, first, second):
        self.sem = ctx.enter_context(nc.semaphore(name))
        self.start = (0, first)
        self.each = (first, second)

    def at(self, layer, n):
        assert 0 < n <= self.each[layer]
        return self.start[layer] + n


def build(nc, x_in, c_in, par_in, con_in, w_in, uq_in, ukv_in, pw_in, sk_in, uv_tabs, out):
    with ExitStack() as ctx:
        def sb(name, shape, dt=F32):
            return ctx.enter_context(nc.sbuf_tensor(name, shape, dt))

        def sem(name):
            return ctx.enter_context(nc.semaphore(name))

        def signal(name, first, second=None):
            return Signal(ctx, nc, name, first, first if second is None else second)

        ps = [ctx.enter_context(nc.psum_tensor(f"bank{i}", [P, 512], F32)) for i in range(6)]
        acc = ctx.enter_context(nc.psum_tensor("bank67", [P, 1024], F32))
        ps += [acc[:, 0:512], acc[:, 512:1024]]

        xT = sb("xT", [P, KC, COLS])
        hT = sb("hT", [P, KC, COLS])
        wring = sb("wring", [P, WSLOTS, KC, WT])
        regA = sb("regA", [P, RING * 2 * D])
        regB = sb("regB", [P, 8336])
        mlaw = sb("mlaw", [P, 3 * 768 + 2 * 1024])
        subk = sb("subk", [P, HC, PKEYS])
        poolw = sb("poolw", [P, 2, PGROUP])
        con = sb("con", [P, CB])
        par = sb("par", [P, DEPTH, PB])
        cT = sb("cT", [P, KC, 2])
        cS = sb("cS", [P, KC, 2])
        modT = sb("modT", [P, 48, 2])
        A1 = sb("A1", [P, KC, 2])
        A2 = sb("A2", [P, KC, 2])
        sqreg = sb("sqreg", [P, 2 * COLS])
        rms = sb("rms", [P, COLS])
        zrow = sb("zrow", [1, P])
        idx = sb("idx", [P, 2, SLOTS], I32)
        stage = sb("stage", [P, RING], I32)
        esum = sb("esum", [P, 2, PH])

        def shaped(reg, off, a, b=None, c=None):
            if b is None:
                return reg[:, off:off + a]
            if c is None:
                return reg[:, off:off + a * b].rearrange("p (a b) -> p a b", a=a)
            return reg[:, off:off + a * b * c].rearrange("p (a b c) -> p a b c", a=a, b=b)

        ring = shaped(regA, 0, RING, 2 * D)
        pu = shaped(regA, 0, 2, 2, PLEN)
        pa_ = shaped(regA, 1088, 2, 2, PLEN)
        pb_ = shaped(regA, 2176, 2, 2, PLEN)
        rows = shaped(regA, 4096, 12, COLS)[0:8]
        gi, gf, gt, lf, BF, BB, cF, cB, MF, MB, ones8, gu = (rows[:, i, :] for i in range(12))
        qT = shaped(regA, 0, HEADS, COLS)
        kT = shaped(regA, 4096, HEADS, COLS)
        vrow = shaped(regA, 8192, 4, HEADS * VD)
        rowbuf = regA[:, 10240:13312].rearrange("p (b g h d) -> p b g h d", b=2, g=2, h=HEADS)
        rowsq = regA[:, 13312:14848]
        pt = shaped(regA, 10240, 2, 4, P)
        prob = shaped(regA, 14848, 2, COLS)
        marg = shaped(regA, 10752, DIRS, 3, 256)
        mE = shaped(regA, 12288, DIRS, 4, 256)
        mP = shaped(regA, 14336, DIRS, 4, 256)
        hn = regA[:, 0:1024].rearrange("p (q e h d) -> p q e h d", q=2, e=2, h=MH)
        hs = shaped(regA, 1024, 2, MH, MD)
        hq = shaped(regA, 1536, 2, MH, MD)
        zqT = shaped(regB, 0, 3, COLS)
        zkvT = shaped(regB, 1536, 2, COLS)
        mqT = shaped(regB, 2560, 2, COLS)
        mkT = shaped(regB, 3584, 2, COLS)
        v1 = shaped(regB, 4608, 4, MH, MD + 1)
        osig = shaped(regB, 5648, 4, MH * MD)
        zkr = shaped(regB, 6672, 4, ROPE)
        gcm = shaped(regB, 6800, 3, COLS)[0:8]
        numS = regB[:, 0:1040].rearrange("p (q e h d) -> p q e h d", q=2, e=2, h=MH)
        hrow = shaped(regB, 0, 4, D)
        topv = shaped(regB, 4096, 4, HC, PTOP)
        modrow = shaped(regB, 7168, 2, WT)[0:2]
        cand = regB[:, 6144:7168]
        uqw = shaped(mlaw, 0, 3, 768)
        ukvw = shaped(mlaw, 2304, 2, 1024)
        yrow = mlaw[:, 0:1024]
        pq = shaped(mlaw, 1024, 2, COLS)
        topiu = mlaw[:, 2048:3072].bitcast(U32).rearrange("p (t c k) -> p t c k", t=4, c=HC)
        s2 = mlaw[:, 3072:3328]
        bi = mlaw[:, 3328:3456].bitcast(U32)
        araw, gact = (mlaw[:, 3456 + i * SLOTS:3456 + (i + 1) * SLOTS] for i in range(2))
        pairrow = regA[0:2, 15872:15872 + 2 * WT]
        sq = shaped(sqreg, 0, 2, COLS)
        diag = shaped(sqreg, 0, DIAGS, P)
        bv = shaped(sqreg, 512, 2, SLOTS)
        wts = shaped(sqreg, 768, 2, SLOTS)
        rtmp = shaped(regA, 14848, 4, 16, 16)
        ident = con[:, C_ID:C_ID + P]
        ones = con[:, C_ONE:C_ONE + P]
        mask = con[:, C_MASK:C_MASK + 1024].rearrange("p (e k j) -> p e k j", e=2, k=2)
        inv = con[:, C_INV:C_INV + 512].rearrange("p (c j) -> p c j", c=2)
        cos = con[:, C_COS:C_COS + 32].rearrange("p (t f) -> p t f", t=2)
        sin = con[:, C_SIN:C_SIN + 32].rearrange("p (t f) -> p t f", t=2)
        iota16 = con[:, C_IOTA:C_IOTA + 16]
        gcol = sb("gcol", [P, 2, 4, 8])
        rowss = sb("rowss", [P, 3, 16])
        mden = sb("mden", [P, 3, 16])
        asm = sb("asm", [P, 2, 4])
        gate_f = sb("gate_f", [P, KC, 2])

        full = [(0, COLS), (0, SEQ)]
        tiles = [[0, 1, 2, 3], [0, 1]]
        streams = [[0, 1], [0]]

        loaded = sem("loaded")
        w_landed = [sem(f"w_landed{i}") for i in range(WSLOTS)]
        w_free = sem("w_free")
        mixw = sem("mixw")
        skw = sem("skw")
        cs_ready = sem("cs_ready")
        init_done = sem("init_done")
        pad_done = sem("pad_done")
        ada_mm = signal("ada_mm", ADA_FIRST, ADA_TILES)
        ada_row = signal("ada_row", ADA_FIRST, ADA_TILES)
        ada_tr = signal("ada_tr", ADA_FIRST, ADA_TILES)
        pair_mm = signal("pair_mm", PAIRS)
        pair_row = signal("pair_row", PAIRS)
        pair_tr = signal("pair_tr", PAIRS)
        rest_ready = sem("rest_ready")
        mod_ready = signal("mod_ready", 1)
        sq_ready = signal("sq_ready", 21)
        sq_used = signal("sq_used", 21)
        ss_ready = signal("ss_ready", 4)
        ms_ready = signal("ms_ready", 4)
        rt_ready = signal("rt_ready", 4)
        hx_ready = signal("hx_ready", 16)
        h_ready = signal("h_ready", 16)
        in_mm = signal("in_mm", 21, 19)
        in_evac = signal("in_evac", 21, 19)
        lnf_ready = signal("lnf_ready", 1)
        gm_ready = signal("gm_ready", 1)
        em_ready = signal("em_ready", 1)
        gt_mm = signal("gt_mm", 1)
        gc_ready = signal("gc_ready", 1)
        pool_ready = signal("pool_ready", 1)
        pool_mm = signal("pool_mm", 2)
        pool_out = signal("pool_out", 2)
        zn_ready = signal("zn_ready", 5)
        qk_mm = signal("qk_mm", 4)
        row_ready = signal("row_ready", 4)
        rss_ready = signal("rss_ready", 4)
        rsq_ready = signal("rsq_ready", 4)
        rown_ready = signal("rown_ready", 4)
        tr_mm = signal("tr_mm", 16, 12)
        tr_evac = signal("tr_evac", 16, 12)
        NU = [32, 16]
        sc_mm = signal("sc_mm", *NU)
        smax = signal("smax", *NU)
        e_done = signal("e_done", *NU)
        p_ready = signal("p_ready", *NU)
        pt_mm = signal("pt_mm", *NU)
        pt_ready = signal("pt_ready", *NU)
        pv_mm = signal("pv_mm", 16, 8)
        attn_out = signal("attn_out", 16, 8)
        st_mm = signal("st_mm", 8, 4)
        marg_ready = signal("marg_ready", 16, 8)
        mE_ready = signal("mE_ready", 16, 8)
        mP_ready = signal("mP_ready", 16, 8)
        num_mm = signal("num_mm", 8, 4)
        num_evac = signal("num_evac", 8, 4)
        hq_ready = signal("hq_ready", 2, 1)
        hsq_ready = signal("hsq_ready", 2, 1)
        hss_ready = signal("hss_ready", 2, 1)
        hrt_ready = signal("hrt_ready", 2, 1)
        ml_ready = signal("ml_ready", 2, 1)
        mt_mm = signal("mt_mm", 2, 1)
        mt_evac = signal("mt_evac", 2, 1)
        out_mm = signal("out_mm", 8)
        x_mid = signal("x_mid", 8)
        hr_mm = signal("hr_mm", 8, 4)
        hr_ready = signal("hr_ready", 8, 4)
        pq_mm = signal("pq_mm", 16)
        pq_ready = signal("pq_ready", 16)
        psc_mm = signal("psc_mm", 16)
        top_done = signal("top_done", 8)
        NT = (4, 2)
        idx_ready = signal("idx_ready", 8 * NT[0], 8 * NT[1])
        sub_ready = signal("sub_ready", 8 * NT[0], 8 * NT[1])
        ex_ready = signal("ex_ready", 8 * NT[0], 8 * NT[1])
        acc_done = signal("acc_done", *NT)
        y_ready = signal("y_ready", *NT)
        yt_mm = signal("yt_mm", 8, 4)
        x_done = signal("x_done", *NT)
        landed = [sem(f"landed{i}") for i in range(RING)]
        staged = sem("staged")
        pool_turn = sem("pool_turn")
        dotted = sem("dotted")
        gelu_ready = sem("gelu_ready")
        v_used = sem("v_used")
        diag_ready = sem("diag_ready")
        s_out = sem("s_out")
        dve_step = sem("dve_step")
        act_step = sem("act_step")
        gp_step = sem("gp_step")

        def mixer_units(l):
            return [(t, h) for t in tiles[l] for h in range(HEADS)]

        def ml_units(l):
            return [(s, h) for s in streams[l] for h in range(MH)]

        block = ctx.enter_context(nc.Block())

        @block.sync
        def _(sp):
            sp.dma_start(cT[:, :, :], c_in).then_inc(loaded, 16)
            sp.dma_start(par[:, :, :], par_in).then_inc(loaded, 16)
            sp.dma_start(con[:, :], con_in).then_inc(loaded, 16)
            sp.dma_start(xT[:, :, :], x_in).then_inc(loaded, 16)
            with sp.Fori(0, DEPTH * LAYER_TILES // WSLOTS) as i:
                for s in range(WSLOTS):
                    sp.wait_ge(w_free, i * WSLOTS + s + 1)
                    sp.dma_start(wring[:, s, :, :].rearrange("p k c -> p (k c)"), w_in[bass.ds(i * WSLOTS + s, 1), :, :]
                                 .rearrange("o p n -> p (o n)")).then_inc(w_landed[s], 16)
            sp.wait_ge(x_done.sem, x_done.at(1, 2))
            sp.dma_start(out, xT[:, :, 0:SEQ]).then_inc(s_out, 16)
            sp.wait_ge(s_out, 16)

        @block.gpsimd
        def _(g):
            steps = [0]

            def link(ins):
                steps[0] += 1
                ins.then_inc(gp_step, 1)
                g.wait_ge(gp_step, steps[0])

            def pool_windows(l):
                ns = len(streams[l])
                g.wait_ge(pad_done, l + 1)
                g.wait_ge(in_evac.sem, in_evac.at(l, 2))

                def lo(t, c, n0, n1, shift, part=slice(0, P)):
                    return t[part, c, 0:ns, PAD + n0 + shift:PAD + n1 + shift]

                for c in range(2):
                    link(g.tensor_tensor(lo(pa_, c, -7, 263, 0), lo(pu, c, -7, 263, -1), lo(pu, c, -7, 263, 0), ALU.add))
                    link(g.tensor_tensor(lo(pb_, c, -6, 262, 0), lo(pa_, c, -6, 262, -1), lo(pa_, c, -6, 262, 1), ALU.add))
                    if c == 1:
                        link(g.tensor_tensor(lo(pa_, c, -4, 260, 0), lo(pb_, c, -4, 260, -2), lo(pb_, c, -4, 260, 2), ALU.add))
                        link(g.tensor_tensor(lo(pb_, c, 0, 256, 0, slice(64, P)), lo(pa_, c, 0, 256, -4, slice(64, P)),
                                             lo(pa_, c, 0, 256, 4, slice(64, P)), ALU.add))
                    iv = inv[:, c, :].unsqueeze(1).to_broadcast([P, ns, SEQ])
                    link(g.tensor_tensor(lo(pa_, c, 0, 256, 0, slice(0, 64)), lo(pa_, c, 0, 256, 0, slice(0, 64)), iv[0:64], ALU.mult))
                    link(g.tensor_tensor(lo(pa_, c, 0, 256, 0, slice(64, P)), lo(pb_, c, 0, 256, 0, slice(64, P)), iv[64:P], ALU.mult))
                    g.tensor_tensor(lo(pa_, c, 0, 256, 0), lo(pa_, c, 0, 256, 0), lo(pu, c, 0, 256, 0), ALU.subtract).then_inc(gp_step, 1)
                    steps[0] += 1
                g.wait_ge(gp_step, steps[0])
                g.sem_inc(pool_ready.sem, 1)

            def gathers(l, n, h):
                tile = n if l == 0 else 4 + n
                at = (tile * PH + h) * PTOP
                with g.Fori(0, PTOP // RING) as it:
                    for f in range(RING // GROUP):
                        g.wait_ge(v_used, it * RING + (at + GROUP * (f + 1)))
                        g.sem_inc(pool_turn, 1)
                        g.tensor_copy(stage[:, f * GROUP:(f + 1) * GROUP],
                                      idx[:, tile % 2, bass.ds(it * RING + (h * PTOP + f * GROUP), GROUP)]).then_inc(staged, 1)
                        g.wait_ge(staged, it * (RING // GROUP) + (at // GROUP + f + 1))
                        g.sem_inc(pool_turn, 1)
                        for s in range(GROUP * f, GROUP * (f + 1)):
                            g.indirect_dma_start(ring[:, s, :], None, uv_tabs[l],
                                                 bass.IndirectOffsetOnAxis(stage[:, s:s + 1], 0)).then_inc(landed[s], 16)

            g.sem_inc(v_used, RING)
            for l in range(DEPTH):
                pool_windows(l)
                for n in range(len(tiles[l])):
                    for h in range(PH):
                        g.wait_ge(idx_ready.sem, idx_ready.at(l, n * PH + h + 1))
                        gathers(l, n, h)

        @block.scalar
        def _(a):
            steps = [0]

            def link(ins):
                steps[0] += 1
                ins.then_inc(act_step, 1)
                a.wait_ge(act_step, steps[0])

            sqn = [0, 0]

            def squares(l, src, n):
                for k in range(n):
                    sqn[l] += 1
                    i = sqn[l] + 21 * l
                    if i > 2:
                        a.wait_ge(sq_used.sem, i - 2)
                    a.activation(sq[:, i % 2, :], src[:, k, :], ACT.Square).then_inc(sq_ready.sem, 1)

            def root(l, i):
                a.wait_ge(ms_ready.sem, ms_ready.at(l, i))
                a.activation(rms[:, :], rms[:, :], ACT.Sqrt).then_inc(rt_ready.sem, 1)

            def modulate(l, which):
                A, shift = (A1, 0) if which == 0 else (A2, 24)
                a.wait_ge(mod_ready.sem, mod_ready.at(l, 1))
                for k in range(KC):
                    a.wait_ge(hx_ready.sem, hx_ready.at(l, which * KC + k + 1))
                    for s in range(2):
                        ins = a.activation(hT[:, k, s * SEQ:(s + 1) * SEQ], hT[:, k, s * SEQ:(s + 1) * SEQ], ACT.Identity,
                                           scale=A[:, k, s:s + 1], bias=modT[:, shift + k, s:s + 1])
                    ins.then_inc(h_ready.sem, 1)

            a.wait_ge(loaded, 64)
            link(a.activation(cS[:, :, :], cT[:, :, :], ACT.Silu))
            a.sem_inc(cs_ready, 1)

            def ada_rows(l, j0, j1):
                for j in range(j0, j1):
                    a.wait_ge(ada_mm.sem, ada_mm.at(l, j + 1))
                    if j >= 2:
                        a.wait_ge(ada_tr.sem, ada_tr.at(l, j - 1))
                    a.activation(modrow[:, j % 2, :], ps[4 + j % 2][0:2, 0:WT], ACT.Copy).then_inc(ada_row.sem, 1)

            def pair_rows(l, q0, q1):
                if l == 0:
                    for q in range(q0, q1):
                        a.wait_ge(pair_mm.sem, q + 1)
                        if q:
                            a.wait_ge(pair_tr.sem, q)
                        a.activation(pairrow, ps[6][0:2, :], ACT.Copy).then_inc(pair_row.sem, 1)

            ada_rows(0, 0, ADA_FIRST)
            for l in range(DEPTH):
                c1 = full[l][1]
                if l == 0:
                    a.dma_start(uqw, uq_in[l]).then_inc(mixw, 16)
                    a.dma_start(ukvw, ukv_in[l]).then_inc(mixw, 16)
                    a.dma_start(poolw[:, :, :], pw_in[l]).then_inc(mixw, 16)
                else:
                    a.wait_ge(x_done.sem, x_done.at(0, 4))
                    a.wait_ge(yt_mm.sem, yt_mm.at(0, 8))
                    a.dma_start(uqw, uq_in[l]).then_inc(mixw, 16)
                    a.dma_start(ukvw, ukv_in[l]).then_inc(mixw, 16)
                    a.dma_start(poolw[:, :, :], pw_in[l]).then_inc(mixw, 16)
                squares(l, xT, KC)
                root(l, 1)
                modulate(l, 0)

                g = [0]

                def group():
                    g[0] += 1
                    a.wait_ge(in_mm.sem, in_mm.at(l, g[0]))
                    return ps[2 + g[0] % 2]

                for b in range(12):
                    src = group()
                    if b < 2:
                        if b == 0:
                            a.wait_ge(pad_done, l + 1)
                        ns = len(streams[l])
                        ins = a.activation(pu[:, b, 0:ns, PAD:PAD + SEQ],
                                           src[:, 0:c1].rearrange("p (s j) -> p s j", s=ns), ACT.Copy)
                    elif b < 5:
                        ins = a.activation(zqT[:, b - 2, 0:c1], src[:, 0:c1], ACT.Copy)
                    elif b < 7:
                        ins = a.activation(zkvT[:, b - 5, :], src[:, :], ACT.Copy)
                    elif b < 9:
                        ins = a.activation(mqT[:, b - 7, 0:c1], src[:, 0:c1], ACT.Copy, scale=MD ** -0.5)
                    elif b < 11:
                        ins = a.activation(mkT[:, b - 9, :], src[:, :], ACT.Copy)
                    else:
                        a.activation(gi, src[0:8, :], ACT.Identity, bias=par[0:8, l, PB_GI:PB_GI + 1])
                        ins = a.activation(gf, src[32:40, :], ACT.Identity, bias=par[0:8, l, PB_GF:PB_GF + 1])
                    ins.then_inc(in_evac.sem, 1)
                src = group()
                a.activation(zkr, src[:, 0:P].rearrange("p (t r) -> p t r", t=4), ACT.Copy).then_inc(in_evac.sem, 1)
                for t in range(4):
                    src = group()
                    a.activation(v1[:, t, :, 0:MD], src[:, 0:WT].rearrange("p (h d) -> p h d", h=MH), ACT.Copy).then_inc(in_evac.sem, 1)
                for t in tiles[l]:
                    src = group()
                    a.activation(osig[:, t, :], src[:, 0:WT], ACT.Sigmoid).then_inc(in_evac.sem, 1)

                a.wait_ge(in_evac.sem, in_evac.at(l, 12))
                link(a.activation(gt, gf, ACT.Abs))
                link(a.activation(gt, gt, ACT.Exp, scale=-1.0))
                a.activation(gt, gt, ACT.Ln, bias=1.0).then_inc(lnf_ready.sem, 1)
                a.wait_ge(in_evac.sem, in_evac.at(l, 7))
                for k in range(3):
                    sqn[l] += 1
                    i = sqn[l] + 21 * l
                    a.wait_ge(sq_used.sem, i - 2)
                    a.activation(sq[:, i % 2, 0:c1], zqT[:, k, 0:c1], ACT.Square).then_inc(sq_ready.sem, 1)
                a.wait_ge(ms_ready.sem, ms_ready.at(l, 2))
                a.activation(rms[:, 0:c1], rms[:, 0:c1], ACT.Sqrt).then_inc(rt_ready.sem, 1)
                squares(l, zkvT, 2)
                root(l, 3)
                pair_rows(l, 0, 1)
                a.wait_ge(gm_ready.sem, gm_ready.at(l, 1))
                a.activation(gcm[:, 2, :], gcm[:, 2, :], ACT.Exp, scale=-1.0).then_inc(em_ready.sem, 1)
                a.wait_ge(gt_mm.sem, gt_mm.at(l, 1))
                a.activation(gcol[:, :, :, :], ps[0][:, 0:64].rearrange("p (q t r) -> p q t r", q=2, t=4), ACT.Copy).then_inc(gc_ready.sem, 1)
                for c in range(2):
                    a.wait_ge(pool_mm.sem, pool_mm.at(l, c + 1))
                    if c == 0:
                        a.wait_ge(in_mm.sem, in_mm.at(l, 21 if l == 0 else 19))
                    a.activation(hT[:, c, 0:c1], ps[4 + c][:, 0:c1], ACT.Copy,
                                 scale=par[:, l, PB_PS + c:PB_PS + c + 1]).then_inc(pool_out.sem, 1)

                def row_root(n):
                    a.wait_ge(rss_ready.sem, rss_ready.at(l, n + 1))
                    g0 = 0 if n in tiles[l] else 8
                    a.activation(rowss[:, 1, g0:16], rowss[:, 0, g0:16], ACT.Sqrt).then_inc(rsq_ready.sem, 1)

                def row_out(n):
                    t, b = n, n % 2
                    g0 = 0 if t in tiles[l] else 1
                    if n >= 2:
                        a.wait_ge(tr_mm.sem, trs(n - 2)[-1])
                    if n == 0:
                        a.wait_ge(gc_ready.sem, gc_ready.at(l, 1))
                        a.wait_ge(pool_mm.sem, pool_mm.at(l, 2))
                    a.wait_ge(qk_mm.sem, qk_mm.at(l, n + 1))
                    if g0 == 0:
                        for f in range(2):
                            a.activation(rowbuf[:, b, 0, 4 * f:4 * f + 4, :],
                                         ps[0 + f][:, 0:384].rearrange("p (h d) -> p h d", h=4), ACT.Copy)
                    for f in range(2):
                        kv = ps[2 + f][:, :].rearrange("p (h d) -> p h d", h=4)
                        a.activation(vrow[:, t, 256 * f:256 * f + 256].rearrange("p (h d) -> p h d", h=4), kv[:, :, NOPE:], ACT.Copy)
                        a.activation(rowbuf[:, b, 1, 4 * f:4 * f + 4, 0:NOPE], kv[:, :, 0:NOPE], ACT.Copy)
                    link(a.activation(rowbuf[:, b, 1, :, NOPE:], zkr[:, t, :].unsqueeze(1).to_broadcast([P, HEADS, ROPE]), ACT.Copy))
                    a.activation(rowsq[:, g0 * 768:1536], rowbuf[:, b, g0:, :, :].rearrange("p g h d -> p (g h d)"),
                                 ACT.Square).then_inc(row_ready.sem, 1)

                def trs(n):
                    at = sum(4 if m in tiles[l] else 2 for m in range(n))
                    return [tr_mm.at(l, at + j + 1) for j in range(4 if n in tiles[l] else 2)]

                def tr_out(n):
                    what = [(1, f) for f in range(2)]
                    if n in tiles[l]:
                        what = [(0, f) for f in range(2)] + what
                    for (g_, f), v in zip(what, trs(n)):
                        a.wait_ge(tr_mm.sem, v)
                        dst = (qT, kT)[g_]
                        a.activation(dst[0:QK, 4 * f:4 * f + 4, n * P:(n + 1) * P],
                                     ps[4 + (v - 1) % 2][0:QK, :].rearrange("p (h j) -> p h j", h=4), ACT.Copy).then_inc(tr_evac.sem, 1)

                pair_rows(l, 1, 2)
                row_out(0)
                for n in range(4):
                    if n:
                        tr_out(n - 1)
                    row_root(n)
                    pair_rows(l, PAIRS_AT[n], PAIRS_AT[n + 1])
                    if n < 3:
                        row_out(n + 1)
                tr_out(3)

                units = mixer_units(l)

                def expo(i):
                    t, h = units[i]
                    k0 = 0 if t < 2 else SEQ
                    a.wait_ge(smax.sem, smax.at(l, i + 1))
                    if i >= 2:
                        a.wait_ge(pt_mm.sem, pt_mm.at(l, i - 1))
                    if i == 0:
                        a.wait_ge(tr_mm.sem, trs(3)[-1])
                    a.activation(prob[:, i % 2, k0:COLS], ps[i % 2][:, k0:COLS], ACT.Exp, scale=SCALE,
                                 bias=asm[:, i % 2, 1:2], accum_out=asm[:, i % 2, 2:3]).then_inc(e_done.sem, 1)

                def pt_out(i):
                    t, h = units[i]
                    j0 = 0 if t < 2 else 2
                    a.wait_ge(pt_mm.sem, pt_mm.at(l, i + 1))
                    if i >= 2:
                        a.wait_ge(pv_mm.sem, pv_mm.at(l, (i - 2) // 2 + 1) if (i - 2) % 2 else pv_mm.at(l, 1) if i == 2 else pv_mm.at(l, (i - 2) // 2 + 1))
                    a.activation(pt[:, i % 2, j0:, :], ps[2 + i % 2][:, j0 * P:].rearrange("p (j q) -> p j q", q=P), ACT.Copy).then_inc(pt_ready.sem, 1)

                for i in range(len(units) + 2):
                    if i < len(units):
                        expo(i)
                    if i >= 2:
                        pt_out(i - 2)

                mu = ml_units(l)

                def decay(i, e):
                    s, h = mu[i]
                    r = e * MH + h
                    u = 2 * i + e
                    a.wait_ge(marg_ready.sem, marg_ready.at(l, u + 1))
                    if u >= 2:
                        a.wait_ge(mP_ready.sem, mP_ready.at(l, u - 1))
                    if u < 2:
                        a.wait_ge(pt_mm.sem, pt_mm.at(l, len(units)))
                        a.wait_ge(pv_mm.sem, pv_mm.at(l, len(units) // 2))
                    for j in range(2):
                        c = 2 * s + j
                        ins = a.activation(mE[:, e, c, :], marg[:, e, j, :], ACT.Exp, bias=gcol[:, 0, c, r:r + 1])
                    if s == 0:
                        for c in (2, 3):
                            ins = a.activation(mE[:, e, c, :], marg[:, e, 2, :], ACT.Exp,
                                               bias=gcol[:, 0, c, r:r + 1])
                    ins.then_inc(mE_ready.sem, 1)

                def num_out(i):
                    s, h = mu[i]
                    a.wait_ge(num_mm.sem, num_mm.at(l, i + 1))
                    if s != mu[0][0] and h == 0:
                        a.wait_ge(hsq_ready.sem, hsq_ready.at(l, 1))
                    a.activation(numS[:, :, :, h, :], ps[6 + i % 2][:, 0:260].rearrange("p (q e d) -> p q e d", q=2, e=2),
                                 ACT.Copy).then_inc(num_evac.sem, 1)

                def head_norm(n):
                    a.wait_ge(hq_ready.sem, hq_ready.at(l, n + 1))
                    a.activation(hq, hs, ACT.Square).then_inc(hsq_ready.sem, 1)
                    a.wait_ge(hss_ready.sem, hss_ready.at(l, n + 1))
                    a.activation(mden[:, 1, 0:8], mden[:, 0, 0:8], ACT.Sqrt).then_inc(hrt_ready.sem, 1)

                def ml_out(n):
                    s = streams[l][n]
                    a.wait_ge(mt_mm.sem, mt_mm.at(l, n + 1))
                    a.activation(hT[:, 6:8, s * SEQ:(s + 1) * SEQ], ps[3][:, :].rearrange("p (c j) -> p c j", c=2), ACT.Copy).then_inc(mt_evac.sem, 1)

                for i in range(len(mu) + 1):
                    if i < len(mu):
                        decay(i, 0)
                        decay(i, 1)
                    if i > MH and (i - 1) % MH == 0:
                        head_norm((i - 1) // MH - 1)
                    if i:
                        num_out(i - 1)
                head_norm(len(streams[l]) - 1)
                for n in range(len(streams[l])):
                    ml_out(n)

                a.wait_ge(x_mid.sem, x_mid.at(l, 1))
                a.dma_start(subk[:, :, :], sk_in[l]).then_inc(skw, 16)
                for k in range(KC):
                    a.wait_ge(x_mid.sem, x_mid.at(l, k + 1))
                    sqn[l] += 1
                    i = sqn[l] + 21 * l
                    a.wait_ge(sq_used.sem, i - 2)
                    a.activation(sq[:, i % 2, 0:c1], xT[:, k, 0:c1], ACT.Square).then_inc(sq_ready.sem, 1)
                a.wait_ge(ms_ready.sem, ms_ready.at(l, 4))
                a.activation(rms[:, 0:c1], rms[:, 0:c1], ACT.Sqrt).then_inc(rt_ready.sem, 1)
                for k in range(KC):
                    a.wait_ge(hx_ready.sem, hx_ready.at(l, KC + k + 1))
                    for s in streams[l]:
                        ins = a.activation(hT[:, k, s * SEQ:(s + 1) * SEQ], hT[:, k, s * SEQ:(s + 1) * SEQ], ACT.Identity,
                                           scale=A2[:, k, s:s + 1], bias=modT[:, 24 + k, s:s + 1])
                    ins.then_inc(h_ready.sem, 1)
                def queries(h):
                    for q in (2 * h, 2 * h + 1):
                        a.wait_ge(pq_mm.sem, pq_mm.at(l, q + 1))
                        if q >= 2:
                            a.wait_ge(psc_mm.sem, psc_mm.at(l, q - 1))
                        a.activation(pq[:, q % 2, 0:c1], ps[q % 2][:, 0:c1], ACT.Copy).then_inc(pq_ready.sem, 1)

                def exponentials(n, h):
                    b = (n if l == 0 else 4 + n) % 2
                    o = h * PTOP
                    a.wait_ge(sub_ready.sem, sub_ready.at(l, n * PH + h + 1))
                    a.activation(bv[:, b, o:o + PTOP], bv[:, b, o:o + PTOP], ACT.Exp).then_inc(ex_ready.sem, 1)

                nt = len(tiles[l])

                def gelus(n, h, r0, r1):
                    at = ((n if l == 0 else 4 + n) * PH + h) * PTOP
                    with a.Fori(r0 * RING // GROUP, r1 * RING // GROUP) as i:
                        a.wait_ge(dotted, i * GROUP + (at + GROUP))
                        a.activation(gact[:, bass.ds(i * GROUP + h * PTOP, GROUP)], araw[:, bass.ds(i * GROUP + h * PTOP, GROUP)],
                                     ACT.Gelu).then_inc(gelu_ready, 1)

                queries(0)
                for j in range(2 * len(tiles[l])):
                    a.wait_ge(hr_mm.sem, hr_mm.at(l, j + 1))
                    a.activation(hrow[:, j // 2, (j % 2) * 512:(j % 2) * 512 + 512], ps[4 + j % 2][:, :], ACT.Copy).then_inc(hr_ready.sem, 1)
                queries(1)
                exponentials(0, 0)
                for n in range(nt):
                    for h in range(PH):
                        if n == 0:
                            gelus(n, h, 0, 1)
                            if h < PH - 2:
                                queries(h + 2)
                        if h < PH - 1 or n < nt - 1:
                            exponentials(n + (h + 1) // PH, (h + 1) % PH)
                        gelus(n, h, int(n == 0), 2)
                        if l == 0 and n == 1:
                            ada_rows(1, 3 * h, 3 * h + 3)
                    a.wait_ge(acc_done.sem, acc_done.at(l, n + 1))
                    if n:
                        a.wait_ge(yt_mm.sem, yt_mm.at(l, 2 * n))
                    a.activation(yrow, acc[:, :], ACT.Copy).then_inc(y_ready.sem, 1)

        @block.vector
        def _(v):
            steps = [0]

            def link(ins):
                steps[0] += 1
                ins.then_inc(dve_step, 1)
                v.wait_ge(dve_step, steps[0])

            def modulation(l, m0, m1, bank, scales):
                link(v.tensor_tensor(modT[:, m0:m1, :], bank[:, 2 * m0:2 * m1].rearrange("p (b s) -> p b s", s=2),
                                     par[:, l, PB_ADA + m0:PB_ADA + m1].unsqueeze(2).to_broadcast([P, m1 - m0, 2]), ALU.add))
                for A, sc, g_ in scales:
                    link(v.scalar_tensor_tensor(out=A[:, :, :], in0=modT[:, sc:sc + 8, :], scalar=1.0,
                                                in1=par[:, l, g_:g_ + 8].unsqueeze(2).to_broadcast([P, 8, 2]),
                                                op0=ALU.add, op1=ALU.mult))

            mix_scale, ff_scale = (A1, 8, PB_G1), (A2, 32, PB_G2)

            def inv_rms(l, i, width, c1):
                v.wait_ge(ss_ready.sem, ss_ready.at(l, i))
                v.tensor_scalar(rms[:, 0:c1], ps[0 if i != 3 else 1][:, 0:c1], 1.0 / width, EPS, ALU.mult, ALU.add).then_inc(ms_ready.sem, 1)
                v.wait_ge(rt_ready.sem, rt_ready.at(l, i))
                link(v.reciprocal(rms[:, 0:c1], rms[:, 0:c1]))

            v.memset(zrow[:, :], 0.0).then_inc(init_done, 1)

            for l in range(DEPTH):
                c1 = full[l][1]
                ns = len(streams[l])
                if l == 0:
                    v.wait_ge(loaded, 64)
                v.memset(pu[:, :, :, :], 0.0).then_inc(pad_done, 1)
                v.memset(v1[:, :, :, MD:MD + 1], 1.0)
                link(v.memset(ones8, 1.0))
                if l == 0:
                    v.wait_ge(ada_tr.sem, ada_tr.at(0, ADA_FIRST))
                    modulation(0, 0, 16, ps[3], [mix_scale])
                    v.sem_inc(mod_ready.sem, 1)
                inv_rms(l, 1, D, COLS)
                for k in range(KC):
                    v.tensor_tensor(hT[:, k, :], xT[:, k, :], rms[:, :], ALU.mult).then_inc(hx_ready.sem, 1)

                v.wait_ge(lnf_ready.sem, lnf_ready.at(l, 1))
                link(v.scalar_tensor_tensor(out=lf, in0=gf, scalar=0.0, in1=gt, op0=ALU.min, op1=ALU.subtract))
                xs, cs = slice(0, SEQ), slice(SEQ, COLS)
                v.tensor_tensor_scan(BB[:, ::-1], ones8[:, ::-1], lf[:, ::-1], 0.0, ALU.mult, ALU.add)
                link(v.tensor_tensor_scan(BF[:, cs], ones8[:, cs], lf[:, cs], 0.0, ALU.mult, ALU.add))
                link(v.tensor_tensor_scan(BF[:, xs], ones8[:, xs], lf[:, xs], BF[:, COLS - 1:COLS], ALU.mult, ALU.add))
                v.tensor_tensor(cB, gi, BB, ALU.subtract)
                link(v.tensor_tensor(cF, gi, BF, ALU.subtract))
                v.tensor_tensor_scan(MB[:, ::-1], cB[:, ::-1], cB[:, ::-1], NEG, ALU.max, ALU.max)
                link(v.tensor_tensor_scan(MF[:, cs], cF[:, cs], cF[:, cs], NEG, ALU.max, ALU.max))
                link(v.tensor_tensor_scan(MF[:, xs], cF[:, xs], cF[:, xs], MF[:, COLS - 1:COLS], ALU.max, ALU.max))
                v.tensor_tensor(BF, BF, MF, ALU.add)
                link(v.tensor_tensor(BB, BB, MB, ALU.add))
                for j, (f_, b_) in enumerate(((cF, cB), (MF, MB), (BF, BB))):
                    link(v.tensor_scalar(gu, b_, con[0:8, C_DIR + 1:C_DIR + 2], None, ALU.mult))
                    ins = v.scalar_tensor_tensor(out=gcm[:, j, :], in0=f_, scalar=con[0:8, C_DIR:C_DIR + 1], in1=gu,
                                                 op0=ALU.mult, op1=ALU.add)
                    link(ins)
                v.sem_inc(gm_ready.sem, 1)

                inv_rms(l, 2, QRANK, c1)
                for k in range(3):
                    ins = v.scalar_tensor_tensor(out=zqT[:, k, 0:c1], in0=zqT[:, k, 0:c1], scalar=par[:, l, PB_QN + k:PB_QN + k + 1],
                                                 in1=rms[:, 0:c1], op0=ALU.mult, op1=ALU.mult).then_inc(zn_ready.sem, 1)
                v.wait_ge(zn_ready.sem, zn_ready.at(l, 3))
                inv_rms(l, 3, KVRANK, COLS)
                for k in range(2):
                    v.scalar_tensor_tensor(out=zkvT[:, k, :], in0=zkvT[:, k, :], scalar=par[:, l, PB_KVN + k:PB_KVN + k + 1],
                                           in1=rms[:, :], op0=ALU.mult, op1=ALU.mult).then_inc(zn_ready.sem, 1)

                for n in range(4):
                    b = n % 2
                    g0 = 0 if n in tiles[l] else 1
                    gn = 2 - g0
                    v.wait_ge(row_ready.sem, row_ready.at(l, n + 1))
                    if n:
                        v.wait_ge(rsq_ready.sem, rsq_ready.at(l, n))
                    link(v.tensor_reduce(rowss[:, 0, 8 * g0:16], rowsq[:, g0 * 768:1536].rearrange("p (h d) -> p h d", d=QK), AX.X, ALU.add))
                    v.tensor_scalar(rowss[:, 0, 8 * g0:16], rowss[:, 0, 8 * g0:16], 1.0 / QK, EPS, ALU.mult, ALU.add).then_inc(rss_ready.sem, 1)
                    v.wait_ge(rsq_ready.sem, rsq_ready.at(l, n + 1))
                    link(v.reciprocal(rowss[:, 2, 8 * g0:16], rowss[:, 1, 8 * g0:16]))
                    rb = rowbuf[:, b, g0:, :, :].rearrange("p g h d -> p (g h) d")
                    link(v.tensor_tensor(rb, rb, rowss[:, 2, 8 * g0:16].unsqueeze(2).to_broadcast([P, 8 * gn, QK]), ALU.mult))
                    gains = par[:, l, PB_QG + g0 * QK:PB_QG + 2 * QK].rearrange("p (g d) -> p g d", d=QK)
                    rg = rowbuf[:, b, g0:, :, :]
                    link(v.tensor_tensor(rg, rg, gains.unsqueeze(2).to_broadcast([P, gn, HEADS, QK]), ALU.mult))
                    if n < 2:
                        H = 8 * gn
                        hf = ROPE // 2
                        x1, x2 = rb[:, :, NOPE:NOPE + hf], rb[:, :, NOPE + hf:QK]
                        cc = cos[:, n, :].unsqueeze(1).to_broadcast([P, H, hf])
                        ss = sin[:, n, :].unsqueeze(1).to_broadcast([P, H, hf])
                        v.tensor_tensor(rtmp[:, 0, 0:H, :], x1, cc, ALU.mult)
                        v.tensor_tensor(rtmp[:, 1, 0:H, :], x2, ss, ALU.mult)
                        v.tensor_tensor(rtmp[:, 2, 0:H, :], x2, cc, ALU.mult)
                        link(v.tensor_tensor(rtmp[:, 3, 0:H, :], x1, ss, ALU.mult))
                        v.tensor_tensor(x1, rtmp[:, 0, 0:H, :], rtmp[:, 1, 0:H, :], ALU.subtract)
                        link(v.tensor_tensor(x2, rtmp[:, 2, 0:H, :], rtmp[:, 3, 0:H, :], ALU.add))
                    v.sem_inc(rown_ready.sem, 1)

                units = mixer_units(l)

                def unit_max(i):
                    t, h = units[i]
                    k0 = 0 if t < 2 else SEQ
                    v.wait_ge(sc_mm.sem, sc_mm.at(l, i + 1))
                    link(v.tensor_reduce(asm[:, i % 2, 0:1], ps[i % 2][:, k0:COLS], AX.X, ALU.max))
                    v.tensor_scalar(asm[:, i % 2, 1:2], asm[:, i % 2, 0:1], -SCALE, None, ALU.mult).then_inc(smax.sem, 1)

                def unit_norm(i):
                    t, h = units[i]
                    k0 = 0 if t < 2 else SEQ
                    v.wait_ge(e_done.sem, e_done.at(l, i + 1))
                    link(v.reciprocal(asm[:, i % 2, 3:4], asm[:, i % 2, 2:3]))
                    v.tensor_scalar(prob[:, i % 2, k0:COLS], prob[:, i % 2, k0:COLS], asm[:, i % 2, 3:4], None, ALU.mult).then_inc(p_ready.sem, 1)

                def pair_out(j):
                    t, h = units[2 * j]
                    v.wait_ge(pv_mm.sem, pv_mm.at(l, j + 1))
                    v.tensor_copy(hT[:, 2 + h // 2, t * P:(t + 1) * P], ps[4 + j % 2][:, 0:P]).then_inc(attn_out.sem, 1)

                nu = len(units)
                for i in range(nu + 4):
                    if i < nu:
                        unit_max(i)
                    if 1 <= i <= nu:
                        unit_norm(i - 1)
                    if i >= 4 and (i - 4) % 2 == 1:
                        pair_out((i - 4) // 2)

                if l == 0:
                    v.wait_ge(pair_tr.sem, PAIRS)
                    modulation(0, 16, 48, ps[7], [ff_scale])
                    v.sem_inc(rest_ready, 1)

                mu = ml_units(l)

                def masked(i, e):
                    u = 2 * i + e
                    if e == 0:
                        v.wait_ge(st_mm.sem, st_mm.at(l, i + 1))
                    if u >= 2:
                        v.wait_ge(mE_ready.sem, mE_ready.at(l, u - 1))
                    if mu[i][0] == 0:
                        v.tensor_scalar(marg[:, e, 2, :], ps[4 + i % 2][:, e * 256:e * 256 + 256], -1.0, None, ALU.mult)
                    v.tensor_tensor(marg[:, e, 0:2, :], mask[:, e, :, :],
                                    ps[4 + i % 2][:, e * 256:e * 256 + 256].unsqueeze(1).to_broadcast([P, 2, 256]),
                                    ALU.subtract).then_inc(marg_ready.sem, 1)

                def weighted(i, e):
                    s, h = mu[i]
                    u = 2 * i + e
                    v.wait_ge(mE_ready.sem, mE_ready.at(l, u + 1))
                    if i >= 1:
                        v.wait_ge(num_mm.sem, num_mm.at(l, i))
                    b0 = 2 * (i % 2)
                    for j in ((0, 1) if s == 0 else (1,)):
                        ins = v.tensor_tensor(mP[:, e, 2 * j:2 * j + 2, :], mE[:, e, 2 * j:2 * j + 2, :],
                                              ps[b0 + j][:, :].rearrange("p (c q) -> p c q", c=2), ALU.mult)
                    ins.then_inc(mP_ready.sem, 1)

                def combine(n):
                    s = streams[l][n]
                    v.wait_ge(num_evac.sem, num_evac.at(l, MH * (n + 1)))
                    den = numS[:, :, :, :, MD:MD + 1].rearrange("p q e h o -> p (q e h) o")
                    md = mden[:, :, :].unsqueeze(3)
                    link(v.scalar_tensor_tensor(out=md[:, 0, :, :], in0=den, scalar=-1.0, in1=den, op0=ALU.mult, op1=ALU.max))
                    link(v.tensor_tensor(mden[:, 0, :], mden[:, 0, :], gcol[:, 1, 2 * s:2 * s + 2, :].rearrange("p t r -> p (t r)"), ALU.max))
                    link(v.reciprocal(mden[:, 1, :], mden[:, 0, :]))
                    link(v.tensor_tensor(hn.rearrange("p q e h d -> p (q e h) d"), numS[:, :, :, :, 0:MD].rearrange("p q e h d -> p (q e h) d"),
                                         mden[:, 1, :].unsqueeze(2).to_broadcast([P, 16, MD]), ALU.mult))
                    v.tensor_tensor(hs, hn[:, :, 0, :, :], hn[:, :, 1, :, :], ALU.add).then_inc(hq_ready.sem, 1)
                    v.wait_ge(hsq_ready.sem, hsq_ready.at(l, n + 1))
                    link(v.tensor_reduce(mden[:, 0, 0:8], hq.rearrange("p q h d -> p (q h) d"), AX.X, ALU.add))
                    link(v.tensor_scalar(mden[:, 0, 0:8], mden[:, 0, 0:8], 1.0 / MD, EPS, ALU.mult, ALU.add))
                    v.sem_inc(hss_ready.sem, 1)
                    v.wait_ge(hrt_ready.sem, hrt_ready.at(l, n + 1))
                    link(v.reciprocal(mden[:, 2, 0:8], mden[:, 1, 0:8]))
                    h3 = hs.rearrange("p q h d -> p (q h) d")
                    link(v.tensor_tensor(h3, h3, mden[:, 2, 0:8].unsqueeze(2).to_broadcast([P, 8, MD]), ALU.mult))
                    h2 = hs.rearrange("p q h d -> p q (h d)")
                    link(v.tensor_tensor(h2, h2, par[:, l, PB_ML:PB_ML + MH * MD].unsqueeze(1).to_broadcast([P, 2, MH * MD]), ALU.mult))
                    if n:
                        v.wait_ge(mt_mm.sem, mt_mm.at(l, n))
                    v.tensor_tensor(osig[:, 2 * s:2 * s + 2, :], osig[:, 2 * s:2 * s + 2, :], h2, ALU.mult).then_inc(ml_ready.sem, 1)

                masked(0, 0)
                masked(0, 1)
                for i in range(len(mu)):
                    weighted(i, 0)
                    weighted(i, 1)
                    if i + 1 < len(mu):
                        masked(i + 1, 0)
                        masked(i + 1, 1)
                    if i >= MH and i % MH == 0:
                        combine(i // MH - 1)
                combine(len(streams[l]) - 1)

                for k in range(KC):
                    v.wait_ge(out_mm.sem, out_mm.at(l, k + 1))
                    for s in streams[l]:
                        ins = v.scalar_tensor_tensor(out=xT[:, k, s * SEQ:(s + 1) * SEQ], in0=ps[4 + k % 2][:, s * SEQ:(s + 1) * SEQ],
                                                     scalar=modT[:, 16 + k, s:s + 1], in1=xT[:, k, s * SEQ:(s + 1) * SEQ],
                                                     op0=ALU.mult, op1=ALU.add)
                    ins.then_inc(x_mid.sem, 1)
                v.wait_ge(x_mid.sem, x_mid.at(l, KC))
                inv_rms(l, 4, D, c1)
                for k in range(KC):
                    v.tensor_tensor(hT[:, k, 0:c1], xT[:, k, 0:c1], rms[:, 0:c1], ALU.mult).then_inc(hx_ready.sem, 1)

                link(v.tensor_copy(gate_f[:, :, :], modT[:, 40:48, :]))

                def top_keys(h):
                    for q in (2 * h, 2 * h + 1):
                        v.wait_ge(psc_mm.sem, psc_mm.at(l, q + 1))
                        for t in tiles[l]:
                            sc = ps[2 + q % 2][:, t * P:(t + 1) * P]
                            tv, ti = topv[:, t, q, :], topiu[:, t, q, :]
                            link(v.max(tv[:, 0:8], sc))
                            v.max_index(ti[:, 0:8], tv[:, 0:8], sc)
                            link(v.match_replace(s2[:, 0:P], tv[:, 0:8], sc, NEG))
                            link(v.max(tv[:, 8:16], s2[:, 0:P]))
                            ins = v.max_index(ti[:, 8:16], tv[:, 8:16], s2[:, 0:P])
                            link(ins)
                    v.sem_inc(top_done.sem, 1)

                def choose(n, h):
                    t = tiles[l][n]
                    b = (n if l == 0 else 4 + n) % 2
                    o = h * PTOP
                    cd = cand[:, 0:256]
                    c3 = cd.rearrange("p (i j) -> p i j", i=PTOP)
                    eq = cand[:, 256:768].rearrange("p (c s j) -> p c s j", c=2, s=PTOP)
                    tf = cand[:, 768:800].rearrange("p (c k) -> p c k", c=2)
                    v.tensor_copy(tf, topiu[:, t, 2 * h:2 * h + 2, :])
                    link(v.tensor_tensor(c3, topv[:, t, 2 * h, :].unsqueeze(2).to_broadcast([P, PTOP, PTOP]),
                                         topv[:, t, 2 * h + 1, :].unsqueeze(1).to_broadcast([P, PTOP, PTOP]), ALU.add))
                    best = bv[:, b, o:o + PTOP]
                    link(v.max(best[:, 0:8], cd))
                    v.max_index(bi[:, 0:8], best[:, 0:8], cd)
                    link(v.match_replace(s2[:, :], best[:, 0:8], cd, NEG))
                    link(v.max(best[:, 8:16], s2[:, :]))
                    link(v.max_index(bi[:, 8:16], best[:, 8:16], s2[:, :]))
                    rank = cand[:, 800:832]
                    rankI = rank.bitcast(I32)
                    biI = bi[:, 0:PTOP].bitcast(I32)
                    v.tensor_scalar(rankI[:, 0:16], biI, 4, None, ALU.arith_shift_right)
                    link(v.tensor_scalar(rankI[:, 16:32], biI, 15, None, ALU.bitwise_and))
                    link(v.tensor_copy(cand[:, 832:864], rankI))
                    link(v.tensor_tensor(eq, cand[:, 832:864].rearrange("p (c s) -> p c s", c=2).unsqueeze(3).to_broadcast([P, 2, PTOP, PTOP]),
                                         iota16.unsqueeze(1).unsqueeze(1).to_broadcast([P, 2, PTOP, PTOP]), ALU.is_equal))
                    link(v.tensor_tensor(eq, eq, tf.unsqueeze(2).to_broadcast([P, 2, PTOP, PTOP]), ALU.mult))
                    link(v.tensor_reduce(cand[:, 864:896], cand[:, 256:768].rearrange("p (s j) -> p s j", j=PTOP), AX.X, ALU.add))
                    link(v.scalar_tensor_tensor(out=idx[:, b, o:o + PTOP], in0=cand[:, 864:880], scalar=float(PKEYS), in1=cand[:, 880:896],
                                                op0=ALU.mult, op1=ALU.add))
                    v.sem_inc(idx_ready.sem, 1)
                    link(v.tensor_copy(esum[:, 0, 0:1], best[:, 0:1]))
                    v.tensor_scalar(best, best, esum[:, 0, 0:1], None, ALU.subtract).then_inc(sub_ready.sem, 1)

                def gates(n, h):
                    b = (n if l == 0 else 4 + n) % 2
                    o = h * PTOP
                    v.wait_ge(ex_ready.sem, ex_ready.at(l, n * PH + h + 1))
                    link(v.tensor_reduce(esum[:, 0, 1:2], bv[:, b, o:o + PTOP], AX.X, ALU.add))
                    link(v.reciprocal(esum[:, 1, 1:2], esum[:, 0, 1:2]))
                    link(v.tensor_scalar(wts[:, b, o:o + PTOP], bv[:, b, o:o + PTOP], esum[:, 1, 1:2], None, ALU.mult))

                def slots(n, h, r0, r1):
                    t = tiles[l][n]
                    tile = n if l == 0 else 4 + n
                    b = tile % 2
                    if h == 0 and r0 == 0:
                        v.wait_ge(hr_ready.sem, hr_ready.at(l, 2 * n + 2))
                    at = (tile * PH + h) * PTOP
                    with v.Fori(r0, r1) as it:
                        for f in range(RING // GROUP):
                            for s in range(GROUP * f, GROUP * (f + 1)):
                                v.wait_ge(landed[s], it * 16 + (at // RING + 1) * 16)
                                v.scalar_tensor_tensor(out=ring[:, s, 0:D], in0=ring[:, s, 0:D], scalar=1.0, in1=hrow[:, t, :],
                                                       op0=ALU.mult, op1=ALU.mult,
                                                       accum_out=araw[:, bass.ds(it * RING + (h * PTOP + s), 1)]).then_inc(dotted, 1)
                            v.wait_ge(gelu_ready, it * (RING // GROUP) + (at // GROUP + f + 1))
                            for s in range(GROUP * f, GROUP * (f + 1)):
                                v.wait_ge(v_used, it * RING + (at + s + 1 + RING - DIAGS))
                                v.tensor_scalar(diag[:, s % DIAGS, :], ident, gact[:, bass.ds(it * RING + (h * PTOP + s), 1)],
                                                wts[:, b, bass.ds(it * RING + (h * PTOP + s), 1)], ALU.mult, ALU.mult).then_inc(diag_ready, 1)

                def add_experts(n):
                    t = tiles[l][n]
                    s = t // 2
                    for f in range(2):
                        v.wait_ge(yt_mm.sem, yt_mm.at(l, 2 * n + f + 1))
                        for j in range(4):
                            k = 4 * f + j
                            ins = v.scalar_tensor_tensor(out=xT[:, k, t * P:(t + 1) * P], in0=ps[4 + f][:, j * P:(j + 1) * P],
                                                         scalar=gate_f[:, k, s:s + 1], in1=xT[:, k, t * P:(t + 1) * P],
                                                         op0=ALU.mult, op1=ALU.add)
                            link(ins)
                    v.sem_inc(x_done.sem, 1)

                nt = len(tiles[l])
                top_keys(0)
                choose(0, 0)
                for n in range(nt):
                    for h in range(PH):
                        gates(n, h)
                        if n == 0:
                            slots(n, h, 0, 1)
                        if n == 0 and h < PH - 1:
                            top_keys(h + 1)
                        if h < PH - 1 or n < nt - 1:
                            choose(n + (h + 1) // PH, (h + 1) % PH)
                        slots(n, h, int(n == 0), 2)
                        if h == 0 and n:
                            add_experts(n - 1)
                    if l == 0 and n == 1:
                        v.wait_ge(ada_tr.sem, ada_tr.at(1, ADA_TILES))
                        modulation(1, 0, 48, ps[3], [mix_scale, ff_scale])
                        v.sem_inc(mod_ready.sem, 1)
                add_experts(nt - 1)

        @block.tensor
        def _(p):
            def tile_in(n):
                p.wait_ge(w_landed[n % WSLOTS], 16 * (n // WSLOTS + 1))
                return wring[:, n % WSLOTS, :, :]

            def ada_tiles(l, j0, j1):
                def turn(j):
                    p.wait_ge(ada_row.sem, ada_row.at(l, j + 1))
                    for b in range(2):
                        mm = p.transpose(ps[3][:, (2 * j + b) * 2:(2 * j + b) * 2 + 2], modrow[:, j % 2, b * P:(b + 1) * P], ident[0:2, 0:2])
                    mm.then_inc(ada_tr.sem, 1)

                for j in range(j0, j1):
                    wt = tile_in(l * LAYER_TILES + j)
                    if j - j0 >= 2:
                        p.wait_ge(ada_row.sem, ada_row.at(l, j - 1))
                    for k in range(KC):
                        mm = p.matmul(ps[4 + j % 2][0:2, 0:WT], cS[:, k, :], wt[:, k, :], start=(k == 0), stop=(k == KC - 1))
                    mm.then_inc(ada_mm.sem, 1)
                    if j > j0:
                        turn(j - 1)
                    p.wait_ge(ada_mm.sem, ada_mm.at(l, j + 1))
                    p.sem_inc(w_free, 1)
                turn(j1 - 1)

            sqn = [0]

            def sum_squares(l, n, bank, c1, sig):
                for k in range(n):
                    sqn[0] += 1
                    p.wait_ge(sq_ready.sem, sqn[0])
                    mm = p.matmul(ps[bank][:, 0:c1], ones, sq[:, sqn[0] % 2, 0:c1], start=(k == 0), stop=(k == n - 1)).then_inc(sq_used.sem, 1)
                p.wait_ge(sq_used.sem, sqn[0])
                p.sem_inc(ss_ready.sem, 1)

            p.sem_inc(w_free, WSLOTS)
            p.wait_ge(cs_ready, 1)
            def pair_turn(q):
                p.wait_ge(pair_row.sem, q + 1)
                for b in range(4):
                    o = 2 * (2 * ADA_FIRST + 4 * q + b)
                    mm = p.transpose(ps[7][:, o:o + 2], pairrow[:, b * P:(b + 1) * P], ident[0:2, 0:2])
                mm.then_inc(pair_tr.sem, 1)

            def ada_pairs(l, q0, q1):
                if l == 0:
                    for q in range(q0, q1):
                        if q:
                            pair_turn(q - 1)
                        for f in range(2):
                            wt = tile_in(ADA_FIRST + IN_TILES + 2 * q + f)
                            for k in range(KC):
                                mm = p.matmul(ps[6][0:2, f * WT:(f + 1) * WT], cS[:, k, :], wt[:, k, :], start=(k == 0), stop=(k == KC - 1))
                        mm.then_inc(pair_mm.sem, 1)
                        p.wait_ge(pair_mm.sem, q + 1)
                        p.sem_inc(w_free, 2)

            ada_tiles(0, 0, ADA_FIRST)
            for l in range(DEPTH):
                c1 = full[l][1]
                ns = len(streams[l])
                base = ADA_FIRST if l == 0 else LAYER_TILES + ADA_TILES
                out_base = l * LAYER_TILES + ADA_TILES + IN_TILES
                query_base = out_base + OUT_TILES
                sum_squares(l, KC, 0, COLS, 1)

                g = [0]

                def group():
                    g[0] += 1
                    if g[0] > 2:
                        p.wait_ge(in_evac.sem, in_evac.at(l, g[0] - 2))
                    return ps[2 + g[0] % 2]

                for b in range(12):
                    if b % 2 == 0:
                        wt = tile_in(base + b // 2)
                    dst = group()
                    n = c1 if (b < 5 or 7 <= b < 9) else COLS
                    m = P if b < 11 else 40
                    o = (b % 2) * P
                    for k in range(KC):
                        if b == 0:
                            p.wait_ge(h_ready.sem, h_ready.at(l, k + 1))
                        mm = p.matmul(dst[0:m, 0:n], wt[:, k, o:o + m], hT[:, k, 0:n], start=(k == 0), stop=(k == KC - 1))
                    mm.then_inc(in_mm.sem, 1)
                    if b % 2 == 1 and b < 11:
                        p.wait_ge(in_mm.sem, in_mm.at(l, g[0]))
                        p.sem_inc(w_free, 1)
                dst = group()
                for t in range(4):
                    for k in range(KC):
                        mm = p.matmul(dst[:, t * ROPE:(t + 1) * ROPE], hT[:, k, t * P:(t + 1) * P], wt[:, k, P + 40:P + 72], start=(k == 0), stop=(k == KC - 1))
                mm.then_inc(in_mm.sem, 1)
                p.wait_ge(in_mm.sem, in_mm.at(l, g[0]))
                p.sem_inc(w_free, 1)
                for j in range(2):
                    wt = tile_in(base + 6 + j)
                    for t in (range(4) if j == 0 else tiles[l]):
                        dst = group()
                        for k in range(KC):
                            mm = p.matmul(dst[:, 0:WT], hT[:, k, t * P:(t + 1) * P], wt[:, k, :], start=(k == 0), stop=(k == KC - 1))
                        mm.then_inc(in_mm.sem, 1)
                    p.wait_ge(in_mm.sem, in_mm.at(l, g[0]))
                    p.sem_inc(w_free, 1)

                sum_squares(l, 3, 0, c1, 2)
                sum_squares(l, 2, 1, COLS, 3)
                ada_pairs(l, 0, 1)

                p.wait_ge(gm_ready.sem, gm_ready.at(l, 1))
                p.wait_ge(em_ready.sem, em_ready.at(l, 1))
                p.wait_ge(ms_ready.sem, ms_ready.at(l, 2))
                for q, j in ((0, 0), (1, 2)):
                    for t in range(4):
                        mm = p.transpose(ps[0][:, q * 32 + t * 8:q * 32 + t * 8 + 8], gcm[:, j, t * P:(t + 1) * P], ident[0:8, 0:8])
                mm.then_inc(gt_mm.sem, 1)

                p.wait_ge(mixw, 48 * (l + 1))
                p.wait_ge(pool_ready.sem, pool_ready.at(l, 1))
                if l == 0:
                    p.wait_ge(mod_ready.sem, 1)
                for c in range(2):
                    for f in range(2):
                        mm = p.matmul(ps[4 + c][64 * f:64 * f + 64, 0:c1], poolw[64 * f:64 * f + 64, c, :],
                                      pa_[64 * f:64 * f + 64, c, 0:ns, PAD:PAD + SEQ], start=True, stop=True)
                    mm.then_inc(pool_mm.sem, 1)

                def trs(n):
                    at = sum(4 if m in tiles[l] else 2 for m in range(n))
                    return [tr_mm.at(l, at + j + 1) for j in range(4 if n in tiles[l] else 2)]

                def qk_rows(n):
                    if n == 0:
                        p.wait_ge(zn_ready.sem, zn_ready.at(l, 5))
                        p.wait_ge(gc_ready.sem, gc_ready.at(l, 1))
                        p.wait_ge(in_evac.sem, in_evac.at(l, 21 if l == 0 else 19))
                    else:
                        p.wait_ge(row_ready.sem, row_ready.at(l, n))
                    if n in tiles[l]:
                        for f in range(2):
                            for k in range(3):
                                p.matmul(ps[f][:, 0:384], zqT[:, k, n * P:(n + 1) * P], uqw[:, k, f * 384:(f + 1) * 384], start=(k == 0), stop=(k == 2))
                    for f in range(2):
                        for k in range(2):
                            mm = p.matmul(ps[2 + f][:, :], zkvT[:, k, n * P:(n + 1) * P], ukvw[:, k, f * 512:(f + 1) * 512], start=(k == 0), stop=(k == 1))
                    mm.then_inc(qk_mm.sem, 1)

                def row_transposes(n):
                    p.wait_ge(rown_ready.sem, rown_ready.at(l, n + 1))
                    if n == 0:
                        p.wait_ge(pool_out.sem, pool_out.at(l, 2))
                    what = [(1, f) for f in range(2)]
                    if n in tiles[l]:
                        what = [(0, f) for f in range(2)] + what
                    for (g_, f), val in zip(what, trs(n)):
                        if val - 2 > tr_mm.start[l]:
                            p.wait_ge(tr_evac.sem, val - 2)
                        for j in range(4):
                            mm = p.transpose(ps[4 + (val - 1) % 2][0:QK, j * P:(j + 1) * P], rowbuf[:, n % 2, g_, 4 * f + j, :], ident)
                        mm.then_inc(tr_mm.sem, 1)

                ada_pairs(l, 1, 2)
                for n in range(4):
                    qk_rows(n)
                    if n:
                        row_transposes(n - 1)
                    ada_pairs(l, PAIRS_AT[n], PAIRS_AT[n + 1])
                row_transposes(3)
                if l == 0:
                    pair_turn(PAIRS - 1)

                units = mixer_units(l)
                nu = len(units)

                def scores(i):
                    t, h = units[i]
                    k0 = 0 if t < 2 else SEQ
                    if i == 0:
                        p.wait_ge(tr_evac.sem, trs(3)[-1])
                    if i >= 2:
                        p.wait_ge(e_done.sem, e_done.at(l, i - 1))
                    p.matmul(ps[i % 2][:, k0:COLS], qT[0:QK, h, t * P:(t + 1) * P], kT[0:QK, h, k0:COLS], start=True, stop=True).then_inc(sc_mm.sem, 1)

                def prob_transposes(i):
                    t, h = units[i]
                    p.wait_ge(p_ready.sem, p_ready.at(l, i + 1))
                    if i >= 2:
                        p.wait_ge(pt_ready.sem, pt_ready.at(l, i - 1))
                    for j in range(0 if t < 2 else 2, 4):
                        mm = p.transpose(ps[2 + i % 2][:, j * P:(j + 1) * P], prob[:, i % 2, j * P:(j + 1) * P], ident)
                    mm.then_inc(pt_mm.sem, 1)

                def outputs(i):
                    t, h = units[i]
                    j_ = i // 2
                    p.wait_ge(pt_ready.sem, pt_ready.at(l, i + 1))
                    if i % 2 == 0 and j_ >= 2:
                        p.wait_ge(attn_out.sem, attn_out.at(l, j_ - 1))
                    f = h % 2
                    js = range(0 if t < 2 else 2, 4)
                    for j in js:
                        mm = p.matmul(ps[4 + j_ % 2][64 * f:64 * f + 64, 0:P], vrow[:, j, h * VD:(h + 1) * VD], pt[:, i % 2, j, :],
                                      start=(j == js[0]), stop=(j == 3))
                    if f:
                        mm.then_inc(pv_mm.sem, 1)

                for i in range(nu + 3):
                    if i < nu:
                        scores(i)
                    if 2 <= i < nu + 2:
                        prob_transposes(i - 2)
                    if i >= 3:
                        outputs(i - 3)

                mu = ml_units(l)

                def state_scores(i):
                    s, h = mu[i]
                    f, c = h % 2, h // 2
                    if i == 0:
                        p.wait_ge(attn_out.sem, attn_out.at(l, nu // 2))
                    if i >= 2:
                        p.wait_ge(mP_ready.sem, mP_ready.at(l, 2 * i - 2))
                    for kc in (range(4) if s == 0 else (2, 3)):
                        p.matmul(ps[2 * (i % 2) + kc // 2][:, (kc % 2) * 256:(kc % 2) * 256 + 256],
                                 mkT[64 * f:64 * f + 64, c, kc * P:(kc + 1) * P], mqT[64 * f:64 * f + 64, c, s * SEQ:(s + 1) * SEQ],
                                 start=True, stop=True)
                    for e in range(DIRS):
                        r = e * MH + h
                        mm = p.matmul(ps[4 + i % 2][:, e * 256:e * 256 + 256], ident[0:8, r:r + 1].to_broadcast([8, P]),
                                      gcm[:, 1, s * SEQ:(s + 1) * SEQ], start=True, stop=True)
                    mm.then_inc(st_mm.sem, 1)

                def numerators(i):
                    s, h = mu[i]
                    if l == 0 and i == 1:
                        p.wait_ge(rest_ready, 1)
                    p.wait_ge(mP_ready.sem, mP_ready.at(l, 2 * i + 2))
                    if i >= 2:
                        p.wait_ge(num_evac.sem, num_evac.at(l, i - 1))
                    for e in range(DIRS):
                        for q in range(2):
                            o = (q * 2 + e) * (MD + 1)
                            kcs = [c for c in range(2 * s, 4) if c != 2 * s + 1 - e or q != e]
                            for kc in kcs:
                                mm = p.matmul(ps[6 + i % 2][:, o:o + MD + 1], mP[:, e, kc, q * P:(q + 1) * P], v1[:, kc, h, :],
                                              start=(kc == kcs[0]), stop=(kc == kcs[-1]))
                    mm.then_inc(num_mm.sem, 1)

                def ml_transposes(n):
                    s = streams[l][n]
                    p.wait_ge(ml_ready.sem, ml_ready.at(l, n + 1))
                    if n:
                        p.wait_ge(mt_evac.sem, mt_evac.at(l, n))
                    for c in range(2):
                        for q in range(2):
                            mm = p.transpose(ps[3][:, c * SEQ + q * P:c * SEQ + (q + 1) * P], osig[:, 2 * s + q, c * P:(c + 1) * P], ident)
                    mm.then_inc(mt_mm.sem, 1)

                for i in range(len(mu) + 1):
                    if i < len(mu):
                        state_scores(i)
                    if i:
                        numerators(i - 1)
                for n in range(len(streams[l])):
                    ml_transposes(n)

                for b in range(8):
                    if b % 2 == 0:
                        wt = tile_in(out_base + b // 2)
                    if b == 0:
                        p.wait_ge(mt_evac.sem, mt_evac.at(l, len(streams[l])))
                        p.wait_ge(marg_ready.sem, marg_ready.at(l, 2 * len(mu)))
                    if b >= 2:
                        p.wait_ge(x_mid.sem, x_mid.at(l, b - 1))
                    for k in range(KC):
                        mm = p.matmul(ps[4 + b % 2][:, 0:c1], wt[:, k, (b % 2) * P:(b % 2 + 1) * P], hT[:, k, 0:c1], start=(k == 0), stop=(k == KC - 1))
                    mm.then_inc(out_mm.sem, 1)
                    if b % 2:
                        p.wait_ge(out_mm.sem, out_mm.at(l, b + 1))
                        p.sem_inc(w_free, 1)
                sum_squares(l, KC, 0, c1, 4)

                def query(q):
                    if q % 2 == 0:
                        tile_in(query_base + q // 2)
                    wt = wring[:, (query_base + q // 2) % WSLOTS, :, :]
                    if q == 0:
                        p.wait_ge(ms_ready.sem, ms_ready.at(l, 4))
                        p.wait_ge(h_ready.sem, h_ready.at(l, 2 * KC))
                    if q >= 2:
                        p.wait_ge(pq_ready.sem, pq_ready.at(l, q - 1))
                    for k in range(KC):
                        mm = p.matmul(ps[q % 2][:, 0:c1], wt[:, k, (q % 2) * P:(q % 2 + 1) * P], hT[:, k, 0:c1], start=(k == 0), stop=(k == KC - 1))
                    mm.then_inc(pq_mm.sem, 1)
                    if q % 2:
                        p.wait_ge(pq_mm.sem, pq_mm.at(l, q + 1))
                        p.sem_inc(w_free, 1)

                def key_scores(q):
                    p.wait_ge(pq_ready.sem, pq_ready.at(l, q + 1))
                    if q == 0:
                        p.wait_ge(skw, 16 * (l + 1))
                    if q >= 2:
                        p.wait_ge(top_done.sem, top_done.at(l, q // 2))
                    for t in tiles[l]:
                        mm = p.matmul(ps[2 + q % 2][:, t * P:(t + 1) * P], pq[:, q % 2, t * P:(t + 1) * P], subk[:, q, :], start=True, stop=True)
                    mm.then_inc(psc_mm.sem, 1)

                def queries(h):
                    query(2 * h)
                    query(2 * h + 1)

                def head_scores(h):
                    key_scores(2 * h)
                    key_scores(2 * h + 1)

                nt = len(tiles[l])

                def turn_sums(n):
                    p.wait_ge(y_ready.sem, y_ready.at(l, n + 1))
                    if n:
                        p.wait_ge(x_done.sem, x_done.at(l, n))
                    for f in range(2):
                        for j in range(4):
                            mm = p.transpose(ps[4 + f][:, j * P:(j + 1) * P], yrow[:, (4 * f + j) * P:(4 * f + j + 1) * P], ident)
                        mm.then_inc(yt_mm.sem, 1)

                def sums(tile, h, r0, r1):
                    at = (tile * PH + h) * PTOP
                    with p.Fori(r0, r1) as it:
                        for s in range(RING):
                            p.wait_ge(diag_ready, it * RING + (at + s + 1))
                            for f in range(2):
                                mm = p.matmul(acc[:, f * 512:f * 512 + 512], diag[:, s % DIAGS, :], ring[:, s, D + f * 512:D + f * 512 + 512],
                                              start=False, stop=False, skip_group_check=True)
                            mm.then_inc(v_used, 1)

                queries(0)
                head_scores(0)
                for j in range(2 * len(tiles[l])):
                    t, f = j // 2, j % 2
                    if j < 2:
                        p.wait_ge(x_mid.sem, x_mid.at(l, KC))
                        p.wait_ge(h_ready.sem, h_ready.at(l, 2 * KC))
                    else:
                        p.wait_ge(hr_ready.sem, hr_ready.at(l, j - 1))
                    for k in range(4):
                        mm = p.transpose(ps[4 + j % 2][:, k * P:(k + 1) * P], hT[:, 4 * f + k, t * P:(t + 1) * P], ident)
                    mm.then_inc(hr_mm.sem, 1)

                queries(1)
                for n in range(nt):
                    tile = n if l == 0 else 4 + n
                    if n:
                        turn_sums(n - 1)
                    if tile == 0:
                        p.wait_ge(init_done, 1)
                    for f in range(2):
                        p.matmul(acc[:, f * 512:f * 512 + 512], zrow[0:1, :], con[0:1, 0:512], start=True, stop=False, skip_group_check=True)
                    for h in range(PH):
                        if n == 0 and h < PH - 1:
                            head_scores(h + 1)
                        if n == 0:
                            sums(tile, h, 0, 1)
                            if h < PH - 2:
                                queries(h + 2)
                        sums(tile, h, int(n == 0), 2)
                        if l == 0 and n == 1:
                            if h == 0:
                                p.wait_ge(x_done.sem, x_done.at(l, 1))
                            ada_tiles(1, 3 * h, 3 * h + 3)
                    for f in range(2):
                        mm = p.matmul(acc[:, f * 512:f * 512 + 512], zrow[0:1, :], con[0:1, 0:512], start=False, stop=True, skip_group_check=True)
                    mm.then_inc(acc_done.sem, 1)
                turn_sums(nt - 1)


def constants():
    con = np.zeros((P, CB), np.float32)
    con[:, C_ID:C_ID + P] = np.eye(P)
    con[:, C_ONE:C_ONE + P] = 1.0
    key = np.arange(256)[:, None]
    query = np.arange(256)[None, :]
    allowed = (query >= key, query <= key)
    for e in range(2):
        m = np.where(allowed[e], 0.0, NEG)
        for k in range(2):
            o = C_MASK + (e * 2 + k) * 256
            con[:, o:o + 256] = m[k * P:(k + 1) * P]
    t = np.arange(SEQ)
    for g, w in enumerate(WINDOWS):
        n = np.clip(t + w // 2, 0, SEQ) - np.clip(t - w // 2, 0, SEQ)
        o = C_INV + (g // 2) * 256
        con[(g % 2) * 64:(g % 2) * 64 + 64, o:o + 256] = 1.0 / n
    per = ROPE // 2
    freqs = np.float32(ROPE_BASE) ** (-np.arange(0, per, 2, dtype=np.float32) / np.float32(per))
    row = (t // GRID_W).astype(np.float32)
    col = (t % GRID_W).astype(np.float32)
    ang = np.concatenate([row[:, None] * freqs, col[:, None] * freqs], axis=-1)
    con[:, C_COS:C_COS + 32] = np.cos(ang).reshape(2, P, 16).transpose(1, 0, 2).reshape(P, 32)
    con[:, C_SIN:C_SIN + 32] = np.sin(ang).reshape(2, P, 16).transpose(1, 0, 2).reshape(P, 32)
    con[0:4, C_DIR] = 1.0
    con[4:8, C_DIR + 1] = 1.0
    con[:, C_IOTA:C_IOTA + 16] = np.arange(16)
    return con


def kernel(**inputs):
    import concourse.bacc as _bacc
    from concourse.bass_utils import run_bass_kernel_spmd as _run

    i = {k: np.asarray(v) for k, v in inputs.items()}
    f32 = np.float32

    def chan(a, n):
        return a.reshape(n, P).T

    x_in = np.concatenate([i["x"][0], i["ctx"][0]], axis=0).T.reshape(KC, P, COLS).transpose(1, 0, 2)
    c_in = np.stack([i["c"][0], i["c_ctx"]], axis=-1).reshape(KC, P, 2).transpose(1, 0, 2)
    par = np.zeros((P, DEPTH, PB), f32)
    tiles = np.zeros((DEPTH, LAYER_TILES, P, KC, WT), f32)
    for l in range(DEPTH):
        par[:, l, PB_ADA:PB_ADA + 48] = chan(i["b_ada"][l], 48)
        par[:, l, PB_G1:PB_G1 + 8] = chan(i["norm1_gain"][l], 8)
        par[:, l, PB_G2:PB_G2 + 8] = chan(i["norm2_gain"][l], 8)
        par[:, l, PB_PS:PB_PS + 2] = chan(i["pool_scale"][l], 2)
        par[:, l, PB_QN:PB_QN + 3] = chan(i["mla_q_norm"][l], 3)
        par[:, l, PB_KVN:PB_KVN + 2] = chan(i["mla_kv_norm"][l], 2)
        gb = i["ml_gate_bias"][l].reshape(4, MH)
        par[0:4, l, PB_GI], par[4:8, l, PB_GI] = gb[0], gb[2]
        par[0:4, l, PB_GF], par[4:8, l, PB_GF] = gb[1], gb[3]
        par[:, l, PB_QG:PB_QG + QK] = i["q_norm"][l]
        par[:, l, PB_KG:PB_KG + QK] = i["k_norm"][l]
        par[:, l, PB_ML:PB_ML + MH * MD] = i["ml_out_norm"][l].reshape(-1)
        w = i["w_in"][l]
        wi = np.zeros((D, IN_TILES * WT), f32)
        wi[:, 0:896] = w[:, 0:896]
        wi[:, 896:1408] = w[:, 928:1440]
        g = w[:, 1952:1968].reshape(D, 4, MH)
        wi[:, 1408:1412], wi[:, 1412:1416] = g[:, 0], g[:, 2]
        wi[:, 1440:1444], wi[:, 1444:1448] = g[:, 1], g[:, 3]
        wi[:, 1448:1480] = w[:, 896:928]
        wi[:, 1536:2048] = w[:, 1440:1952]
        at = 0
        ada, c = i["w_ada"][l], ADA_FIRST * WT
        for m in ((ada[:, :c], wi, ada[:, c:]) if l == 0 else (ada, wi)) + (i["w_out"][l], i["peer_wq"][l]):
            n = m.shape[1] // WT
            tiles[l, at:at + n] = m.reshape(KC, P, n, WT).transpose(2, 1, 0, 3)
            at += n
    uq = i["w_uq"].reshape(DEPTH, 3, P, 768).transpose(0, 2, 1, 3)
    ukv = i["w_ukv"].reshape(DEPTH, 2, P, 1024).transpose(0, 2, 1, 3)
    pw = i["pool_w"].reshape(DEPTH, 2, 2 * PGROUP, PGROUP).transpose(0, 2, 1, 3)
    sk = i["peer_subkeys"].reshape(DEPTH, HC, PKEYS, PDK).transpose(0, 3, 1, 2)

    nc = _bacc.Bacc("TRN2", target_bir_lowering=False, num_devices=1)
    arrays = {}

    def put(name, a):
        a = np.ascontiguousarray(a)
        arrays[name + "_dram"] = a
        return nc.dram_tensor(name + "_dram", a.shape, mybir.dt.from_np(a.dtype), kind="ExternalInput").ap()

    args = [put("x", x_in), put("c", c_in), put("par", par), put("con", constants()),
            put("w", tiles.reshape(DEPTH * LAYER_TILES, P, KC * WT)), put("uq", uq), put("ukv", ukv), put("pw", pw), put("sk", sk)]
    args.append([put(f"uv{l}", np.concatenate([i["peer_u"][l], i["peer_v"][l]], axis=1)) for l in range(DEPTH)])
    args.append(nc.dram_tensor("out_dram", (P, KC, SEQ), F32, kind="ExternalOutput").ap())
    build(nc, *args)
    r = _run(nc, [arrays], core_ids=[0])
    return np.ascontiguousarray(r.results[0]["out_dram"].transpose(2, 1, 0)).reshape(1, SEQ, D)
```

```python
from contextlib import ExitStack

import numpy as np

import concourse.bass as bass
from concourse import mybir

ALU = mybir.AluOpType
ACT = mybir.ActivationFunctionType
AX = mybir.AxisListType
F32 = mybir.dt.float32
I32 = mybir.dt.int32
U32 = mybir.dt.uint32

P = 128
D = 1024
KC = D // P
SEQ = 256
CTX = 256
COLS = SEQ + CTX
DEPTH = 2
EPS = 1e-6
NEG = -1e30
GRID_W = 64

WINDOWS = (2, 4, 8, 16)
PGROUP = 64
PAD = max(WINDOWS) // 2
PLEN = SEQ + 2 * PAD

HEADS, NOPE, ROPE, QK, VD = 8, 64, 32, 96, 64
QRANK, KVRANK = 384, 256
SCALE = QK ** -0.5
ROPE_BASE = 10000.0

MH, MD = 4, 64
DIRS = 2

PH, PTOP, PKEYS, PDK = 8, 16, 128, 128
HC = 2 * PH
SLOTS = PH * PTOP

WT = 256
WSLOTS = 4
ADA_TILES = 6 * D // WT
ADA_FIRST = 2 * D // WT
PAIRS = (ADA_TILES - ADA_FIRST) // 2
STEPS = 4
PAIRS_AT = (1, 3, 5, 6, 8)
IN_TILES = 8
OUT_TILES = D // WT
PQ_TILES = HC * PDK // WT
LAYER_TILES = ADA_TILES + IN_TILES + OUT_TILES + PQ_TILES

RING = 8
GROUP = 2
DIAGS = 4

PB_ADA, PB_G1, PB_G2, PB_PS, PB_QN, PB_KVN, PB_GI, PB_GF = 0, 48, 56, 64, 66, 69, 71, 72
PB_QG, PB_KG, PB_ML = 73, 73 + QK, 73 + 2 * QK
PB = PB_ML + MH * MD
C_ID, C_ONE = 0, 128
C_MASK = 256
C_INV = C_MASK + DIRS * 2 * 256
C_COS = C_INV + 2 * 256
C_SIN = C_COS + 32
C_DIR = C_SIN + 32
C_IOTA = C_DIR + 2
CB = C_IOTA + 16


class Signal:

    def __init__(self, ctx, nc, name, first, second):
        self.sem = ctx.enter_context(nc.semaphore(name))
        self.start = (0, first)
        self.each = (first, second)

    def at(self, layer, n):
        assert 0 < n <= self.each[layer]
        return self.start[layer] + n


def build(nc, x_in, c_in, par_in, con_in, w_in, uq_in, ukv_in, pw_in, sk_in, uv_tabs, out):
    with ExitStack() as ctx:
        def sb(name, shape, dt=F32):
            return ctx.enter_context(nc.sbuf_tensor(name, shape, dt))

        def sem(name):
            return ctx.enter_context(nc.semaphore(name))

        def signal(name, first, second=None):
            return Signal(ctx, nc, name, first, first if second is None else second)

        ps = [ctx.enter_context(nc.psum_tensor(f"bank{i}", [P, 512], F32)) for i in range(6)]
        acc = ctx.enter_context(nc.psum_tensor("bank67", [P, 1024], F32))
        ps += [acc[:, 0:512], acc[:, 512:1024]]

        xT = sb("xT", [P, KC, COLS])
        hT = sb("hT", [P, KC, COLS])
        wring = sb("wring", [P, WSLOTS, KC, WT])
        regA = sb("regA", [P, RING * 2 * D])
        regB = sb("regB", [P, 8336])
        mlaw = sb("mlaw", [P, 3 * 768 + 2 * 1024])
        subk = sb("subk", [P, HC, PKEYS])
        poolw = sb("poolw", [P, 2, PGROUP])
        con = sb("con", [P, CB])
        par = sb("par", [P, DEPTH, PB])
        cT = sb("cT", [P, KC, 2])
        cS = sb("cS", [P, KC, 2])
        modT = sb("modT", [P, 48, 2])
        A1 = sb("A1", [P, KC, 2])
        A2 = sb("A2", [P, KC, 2])
        sqreg = sb("sqreg", [P, 2 * COLS])
        rms = sb("rms", [P, COLS])
        zrow = sb("zrow", [1, P])
        idx = sb("idx", [P, 2, SLOTS], I32)
        stage = sb("stage", [P, RING], I32)
        esum = sb("esum", [P, 2, PH])

        def shaped(reg, off, a, b=None, c=None):
            if b is None:
                return reg[:, off:off + a]
            if c is None:
                return reg[:, off:off + a * b].rearrange("p (a b) -> p a b", a=a)
            return reg[:, off:off + a * b * c].rearrange("p (a b c) -> p a b c", a=a, b=b)

        ring = shaped(regA, 0, RING, 2 * D)
        pu = shaped(regA, 0, 2, 2, PLEN)
        pa_ = shaped(regA, 1088, 2, 2, PLEN)
        pb_ = shaped(regA, 2176, 2, 2, PLEN)
        rows = shaped(regA, 4096, 12, COLS)[0:8]
        gi, gf, gt, lf, BF, BB, cF, cB, MF, MB, ones8, gu = (rows[:, i, :] for i in range(12))
        qT = shaped(regA, 0, HEADS, COLS)
        kT = shaped(regA, 4096, HEADS, COLS)
        vrow = shaped(regA, 8192, 4, HEADS * VD)
        rowbuf = regA[:, 10240:13312].rearrange("p (b g h d) -> p b g h d", b=2, g=2, h=HEADS)
        rowsq = regA[:, 13312:14848]
        pt = shaped(regA, 10240, 2, 4, P)
        prob = shaped(regA, 14848, 2, COLS)
        marg = shaped(regA, 11264, DIRS, 3, 256)
        mE = shaped(regA, 12800, DIRS, 4, 256)
        mP = shaped(mlaw, 0, DIRS, 4, 256)
        hn = mlaw[:, 2048:3072].rearrange("p (q e h d) -> p q e h d", q=2, e=2, h=MH)
        hs = shaped(mlaw, 3072, 2, MH, MD)
        hq = shaped(mlaw, 3584, 2, MH, MD)
        zqT = shaped(regB, 0, 3, COLS)
        zkvT = shaped(regB, 1536, 2, COLS)
        mqT = shaped(regB, 2560, 2, COLS)
        mkT = shaped(regB, 3584, 2, COLS)
        v1 = shaped(regB, 4608, 4, MH, MD + 1)
        osig = shaped(regB, 5648, 4, MH * MD)
        zkr = shaped(regB, 6672, 4, ROPE)
        zkc = regA[:, 10240:10240 + COLS]
        gcm = shaped(regB, 6800, 3, COLS)[0:8]
        numS = regB[:, 0:1040].rearrange("p (q e h d) -> p q e h d", q=2, e=2, h=MH)
        hrow = shaped(regB, 0, 4, D)
        topv = shaped(regB, 4096, 4, HC, PTOP)
        modrow = shaped(regB, 7168, 2, WT)[0:2]
        cand = regB[:, 6144:7168]
        uqw = shaped(mlaw, 0, 3, 768)
        ukvw = shaped(mlaw, 2304, 2, 1024)
        yrow = mlaw[:, 0:1024]
        pq = shaped(mlaw, 1024, 2, COLS)
        topiu = mlaw[:, 2048:3072].bitcast(U32).rearrange("p (t c k) -> p t c k", t=4, c=HC)
        s2 = mlaw[:, 3072:3328]
        bi = mlaw[:, 3328:3456].bitcast(U32)
        araw, gact = (mlaw[:, 3456 + i * SLOTS:3456 + (i + 1) * SLOTS] for i in range(2))
        pairrow = regA[0:2, 15872:15872 + 2 * WT]
        sq = shaped(sqreg, 0, 2, COLS)
        diag = shaped(sqreg, 0, DIAGS, P)
        bv = shaped(sqreg, 512, 2, SLOTS)
        wts = shaped(sqreg, 768, 2, SLOTS)
        rtmp = shaped(regA, 14848, 4, 16, 16)
        ident = con[:, C_ID:C_ID + P]
        ones = con[:, C_ONE:C_ONE + P]
        mask = con[:, C_MASK:C_MASK + 1024].rearrange("p (e k j) -> p e k j", e=2, k=2)
        inv = con[:, C_INV:C_INV + 512].rearrange("p (c j) -> p c j", c=2)
        cos = con[:, C_COS:C_COS + 32].rearrange("p (t f) -> p t f", t=2)
        sin = con[:, C_SIN:C_SIN + 32].rearrange("p (t f) -> p t f", t=2)
        iota16 = con[:, C_IOTA:C_IOTA + 16]
        gcol = sb("gcol", [P, 2, 4, 8])
        rowss = sb("rowss", [P, 3, 16])
        mden = sb("mden", [P, 3, 16])
        asm = sb("asm", [P, 2, 4])
        gate_f = sb("gate_f", [P, KC, 2])

        full = [(0, COLS), (0, SEQ)]
        tiles = [[0, 1, 2, 3], [0, 1]]
        streams = [[0, 1], [0]]

        c_loaded = sem("c_loaded")
        con_loaded = sem("con_loaded")
        loaded = sem("loaded")
        w_landed = [sem(f"w_landed{i}") for i in range(WSLOTS)]
        w_free = sem("w_free")
        mixw = sem("mixw")
        skw = sem("skw")
        cs_ready = sem("cs_ready")
        init_done = sem("init_done")
        pad_done = sem("pad_done")
        ada_mm = signal("ada_mm", ADA_FIRST, ADA_TILES)
        ada_row = signal("ada_row", ADA_FIRST, ADA_TILES)
        ada_tr = signal("ada_tr", ADA_FIRST, ADA_TILES)
        pair_mm = signal("pair_mm", PAIRS)
        pair_row = signal("pair_row", PAIRS)
        pair_tr = signal("pair_tr", PAIRS)
        rest_ready = sem("rest_ready")
        mod_ready = signal("mod_ready", 1)
        sq_ready = signal("sq_ready", 21)
        sq_used = signal("sq_used", 21)
        ss_ready = signal("ss_ready", 4)
        ms_ready = signal("ms_ready", 4)
        rt_ready = signal("rt_ready", 4)
        hx_ready = signal("hx_ready", 16)
        h_ready = signal("h_ready", 16)
        in_mm = signal("in_mm", 21, 19)
        in_evac = signal("in_evac", 21, 19)
        lnf_ready = signal("lnf_ready", 1)
        gm_ready = signal("gm_ready", 1)
        em_ready = signal("em_ready", 1)
        gt_mm = signal("gt_mm", 1)
        gc_ready = signal("gc_ready", 1)
        pool_ready = signal("pool_ready", 1)
        pool_mm = signal("pool_mm", 2)
        pool_out = signal("pool_out", 2)
        zn_ready = signal("zn_ready", 5)
        qk_mm = signal("qk_mm", 4)
        row_ready = signal("row_ready", 4)
        rss_ready = signal("rss_ready", 4)
        rsq_ready = signal("rsq_ready", 4)
        rown_ready = signal("rown_ready", 4)
        tr_mm = signal("tr_mm", 16, 12)
        tr_evac = signal("tr_evac", 16, 12)
        NU = [32, 16]
        sc_mm = signal("sc_mm", *NU)
        smax = signal("smax", *NU)
        e_done = signal("e_done", *NU)
        p_ready = signal("p_ready", *NU)
        pt_mm = signal("pt_mm", *NU)
        pt_ready = signal("pt_ready", *NU)
        pv_mm = signal("pv_mm", 16, 8)
        attn_out = signal("attn_out", 16, 8)
        st_mm = signal("st_mm", 8, 4)
        marg_ready = signal("marg_ready", 16, 8)
        mE_ready = signal("mE_ready", 16, 8)
        mP_ready = signal("mP_ready", 16, 8)
        num_mm = signal("num_mm", 8, 4)
        num_evac = signal("num_evac", 8, 4)
        hq_ready = signal("hq_ready", 2, 1)
        hsq_ready = signal("hsq_ready", 2, 1)
        hss_ready = signal("hss_ready", 2, 1)
        hrt_ready = signal("hrt_ready", 2, 1)
        ml_ready = signal("ml_ready", 2, 1)
        mt_mm = signal("mt_mm", 2, 1)
        mt_evac = signal("mt_evac", 2, 1)
        out_mm = signal("out_mm", 8)
        x_mid = signal("x_mid", 8)
        hr_mm = signal("hr_mm", 8, 4)
        hr_ready = signal("hr_ready", 8, 4)
        pq_mm = signal("pq_mm", 16)
        pq_ready = signal("pq_ready", 16)
        psc_mm = signal("psc_mm", 16)
        top_done = signal("top_done", HC)
        NT = (4, 2)
        idx_ready = signal("idx_ready", 8 * NT[0], 8 * NT[1])
        sub_ready = signal("sub_ready", 8 * NT[0], 8 * NT[1])
        ex_ready = signal("ex_ready", 8 * NT[0], 8 * NT[1])
        acc_done = signal("acc_done", *NT)
        y_ready = signal("y_ready", *NT)
        yt_mm = signal("yt_mm", 8, 4)
        x_done = signal("x_done", *NT)
        landed = [sem(f"landed{i}") for i in range(RING)]
        staged = sem("staged")
        pool_turn = sem("pool_turn")
        dotted = sem("dotted")
        gelu_ready = sem("gelu_ready")
        v_used = sem("v_used")
        diag_ready = sem("diag_ready")
        s_out = sem("s_out")
        dve_step = sem("dve_step")
        act_step = sem("act_step")
        gp_step = sem("gp_step")

        def mixer_units(l):
            return [(t, h) for t in tiles[l] for h in range(HEADS)]

        def ml_units(l):
            return [(s, h) for s in streams[l] for h in range(MH)]

        block = ctx.enter_context(nc.Block())

        @block.sync
        def _(sp):
            sp.dma_start(cT[:, :, :], c_in).then_inc(c_loaded, 16)
            sp.dma_start(con[:, :], con_in).then_inc(con_loaded, 16)
            with sp.Fori(0, DEPTH * LAYER_TILES // WSLOTS) as i:
                for s in range(WSLOTS):
                    sp.wait_ge(w_free, i * WSLOTS + s + 1)
                    sp.dma_start(wring[:, s, :, :].rearrange("p k c -> p (k c)"), w_in[bass.ds(i * WSLOTS + s, 1), :, :]
                                 .rearrange("o p n -> p (o n)")).then_inc(w_landed[s], 16)
            sp.wait_ge(x_done.sem, x_done.at(1, 2))
            sp.dma_start(out, xT[:, :, 0:SEQ]).then_inc(s_out, 16)
            sp.wait_ge(s_out, 16)

        @block.gpsimd
        def _(g):
            steps = [0]

            def link(ins):
                steps[0] += 1
                ins.then_inc(gp_step, 1)
                g.wait_ge(gp_step, steps[0])

            def pool_windows(l):
                ns = len(streams[l])
                g.wait_ge(pad_done, l + 1)
                g.wait_ge(in_evac.sem, in_evac.at(l, 2))

                def lo(t, c, n0, n1, shift, part=slice(0, P)):
                    return t[part, c, 0:ns, PAD + n0 + shift:PAD + n1 + shift]

                for c in range(2):
                    link(g.tensor_tensor(lo(pa_, c, -7, 263, 0), lo(pu, c, -7, 263, -1), lo(pu, c, -7, 263, 0), ALU.add))
                    link(g.tensor_tensor(lo(pb_, c, -6, 262, 0), lo(pa_, c, -6, 262, -1), lo(pa_, c, -6, 262, 1), ALU.add))
                    if c == 1:
                        link(g.tensor_tensor(lo(pa_, c, -4, 260, 0), lo(pb_, c, -4, 260, -2), lo(pb_, c, -4, 260, 2), ALU.add))
                        link(g.tensor_tensor(lo(pb_, c, 0, 256, 0, slice(64, P)), lo(pa_, c, 0, 256, -4, slice(64, P)),
                                             lo(pa_, c, 0, 256, 4, slice(64, P)), ALU.add))
                    iv = inv[:, c, :].unsqueeze(1).to_broadcast([P, ns, SEQ])
                    link(g.tensor_tensor(lo(pa_, c, 0, 256, 0, slice(0, 64)), lo(pa_, c, 0, 256, 0, slice(0, 64)), iv[0:64], ALU.mult))
                    link(g.tensor_tensor(lo(pa_, c, 0, 256, 0, slice(64, P)), lo(pb_, c, 0, 256, 0, slice(64, P)), iv[64:P], ALU.mult))
                    g.tensor_tensor(lo(pa_, c, 0, 256, 0), lo(pa_, c, 0, 256, 0), lo(pu, c, 0, 256, 0), ALU.subtract).then_inc(gp_step, 1)
                    steps[0] += 1
                g.wait_ge(gp_step, steps[0])
                g.sem_inc(pool_ready.sem, 1)

            def gathers(l, n, h):
                tile = n if l == 0 else 4 + n
                at = (tile * PH + h) * PTOP
                with g.Fori(0, PTOP // RING) as it:
                    for f in range(RING // GROUP):
                        g.wait_ge(v_used, it * RING + (at + GROUP * (f + 1)))
                        g.sem_inc(pool_turn, 1)
                        g.tensor_copy(stage[:, f * GROUP:(f + 1) * GROUP],
                                      idx[:, tile % 2, bass.ds(it * RING + (h * PTOP + f * GROUP), GROUP)]).then_inc(staged, 1)
                        g.wait_ge(staged, it * (RING // GROUP) + (at // GROUP + f + 1))
                        g.sem_inc(pool_turn, 1)
                        for s in range(GROUP * f, GROUP * (f + 1)):
                            g.indirect_dma_start(ring[:, s, :], None, uv_tabs[l],
                                                 bass.IndirectOffsetOnAxis(stage[:, s:s + 1], 0)).then_inc(landed[s], 16)

            g.sem_inc(v_used, RING)
            for l in range(DEPTH):
                pool_windows(l)
                for n in range(len(tiles[l])):
                    for h in range(PH):
                        g.wait_ge(idx_ready.sem, idx_ready.at(l, n * PH + h + 1))
                        gathers(l, n, h)

        @block.scalar
        def _(a):
            steps = [0]

            def link(ins):
                steps[0] += 1
                ins.then_inc(act_step, 1)
                a.wait_ge(act_step, steps[0])

            sqn = [0, 0]

            def squares(l, src, n):
                for k in range(n):
                    sqn[l] += 1
                    i = sqn[l] + 21 * l
                    if i > 2:
                        a.wait_ge(sq_used.sem, i - 2)
                    a.activation(sq[:, i % 2, :], src[:, k, :], ACT.Square).then_inc(sq_ready.sem, 1)

            def root(l, i):
                a.wait_ge(ms_ready.sem, ms_ready.at(l, i))
                a.activation(rms[:, :], rms[:, :], ACT.Sqrt).then_inc(rt_ready.sem, 1)

            def modulate(l, which):
                A, shift = (A1, 0) if which == 0 else (A2, 24)
                a.wait_ge(mod_ready.sem, mod_ready.at(l, 1))
                for k in range(KC):
                    a.wait_ge(hx_ready.sem, hx_ready.at(l, which * KC + k + 1))
                    for s in range(2):
                        ins = a.activation(hT[:, k, s * SEQ:(s + 1) * SEQ], hT[:, k, s * SEQ:(s + 1) * SEQ], ACT.Identity,
                                           scale=A[:, k, s:s + 1], bias=modT[:, shift + k, s:s + 1])
                    ins.then_inc(h_ready.sem, 1)

            a.wait_ge(c_loaded, 16)
            link(a.activation(cS[:, :, :], cT[:, :, :], ACT.Silu))
            a.sem_inc(cs_ready, 1)
            a.dma_start(xT[:, :, :], x_in).then_inc(loaded, 16)
            a.dma_start(par[:, :, :], par_in).then_inc(loaded, 16)

            def ada_rows(l, j0, j1):
                for j in range(j0, j1):
                    a.wait_ge(ada_mm.sem, ada_mm.at(l, j + 1))
                    if j >= 2:
                        a.wait_ge(ada_tr.sem, ada_tr.at(l, j - 1))
                    a.activation(modrow[:, j % 2, :], ps[4 + j % 2][0:2, 0:WT], ACT.Copy).then_inc(ada_row.sem, 1)

            def pair_rows(l, q0, q1):
                if l == 0:
                    for q in range(q0, q1):
                        a.wait_ge(pair_mm.sem, q + 1)
                        if q:
                            a.wait_ge(pair_tr.sem, q)
                        a.activation(pairrow, ps[6][0:2, :], ACT.Copy).then_inc(pair_row.sem, 1)

            ada_rows(0, 0, ADA_FIRST // 2)
            a.wait_ge(loaded, 32)
            squares(0, xT, KC)
            root(0, 1)
            ada_rows(0, ADA_FIRST // 2, ADA_FIRST)
            for l in range(DEPTH):
                c1 = full[l][1]
                if l == 0:
                    a.dma_start(uqw, uq_in[l]).then_inc(mixw, 16)
                    a.dma_start(ukvw, ukv_in[l]).then_inc(mixw, 16)
                    a.dma_start(poolw[:, :, :], pw_in[l]).then_inc(mixw, 16)
                else:
                    a.wait_ge(x_done.sem, x_done.at(0, 4))
                    a.wait_ge(yt_mm.sem, yt_mm.at(0, 8))
                    a.dma_start(uqw, uq_in[l]).then_inc(mixw, 16)
                    a.dma_start(ukvw, ukv_in[l]).then_inc(mixw, 16)
                    a.dma_start(poolw[:, :, :], pw_in[l]).then_inc(mixw, 16)
                    squares(l, xT, KC)
                    root(l, 1)
                modulate(l, 0)

                g = [0]

                def group():
                    g[0] += 1
                    a.wait_ge(in_mm.sem, in_mm.at(l, g[0]))
                    return ps[2 + g[0] % 2]

                for b in range(12):
                    src = group()
                    if b < 2:
                        if b == 0:
                            a.wait_ge(pad_done, l + 1)
                        ns = len(streams[l])
                        ins = a.activation(pu[:, b, 0:ns, PAD:PAD + SEQ],
                                           src[:, 0:c1].rearrange("p (s j) -> p s j", s=ns), ACT.Copy)
                    elif b < 5:
                        ins = a.activation(zqT[:, b - 2, 0:c1], src[:, 0:c1], ACT.Copy)
                    elif b < 7:
                        ins = a.activation(zkvT[:, b - 5, :], src[:, :], ACT.Copy)
                    elif b < 9:
                        ins = a.activation(mqT[:, b - 7, 0:c1], src[:, 0:c1], ACT.Copy, scale=MD ** -0.5)
                    elif b < 11:
                        ins = a.activation(mkT[:, b - 9, :], src[:, :], ACT.Copy)
                    else:
                        a.activation(gi, src[0:8, :], ACT.Identity, bias=par[0:8, l, PB_GI:PB_GI + 1])
                        a.activation(gf, src[32:40, :], ACT.Identity, bias=par[0:8, l, PB_GF:PB_GF + 1])
                        ins = a.activation(zkc[64:64 + ROPE, :], src[64:64 + ROPE, :], ACT.Copy)
                    ins.then_inc(in_evac.sem, 1)

                a.wait_ge(in_evac.sem, in_evac.at(l, 12))
                link(a.activation(gt, gf, ACT.Abs))
                link(a.activation(gt, gt, ACT.Exp, scale=-1.0))
                a.activation(gt, gt, ACT.Ln, bias=1.0).then_inc(lnf_ready.sem, 1)
                for t in range(4):
                    src = group()
                    a.activation(v1[:, t, :, 0:MD], src[:, 0:WT].rearrange("p (h d) -> p h d", h=MH), ACT.Copy).then_inc(in_evac.sem, 1)
                for k in range(3):
                    sqn[l] += 1
                    i = sqn[l] + 21 * l
                    a.wait_ge(sq_used.sem, i - 2)
                    a.activation(sq[:, i % 2, 0:c1], zqT[:, k, 0:c1], ACT.Square).then_inc(sq_ready.sem, 1)
                squares(l, zkvT, 2)
                src = group()
                a.activation(zkr, src[:, 0:P].rearrange("p (t r) -> p t r", t=4), ACT.Copy).then_inc(in_evac.sem, 1)
                a.wait_ge(ms_ready.sem, ms_ready.at(l, 2))
                a.activation(rms[:, 0:c1], rms[:, 0:c1], ACT.Sqrt).then_inc(rt_ready.sem, 1)
                for t in tiles[l]:
                    src = group()
                    a.activation(osig[:, t, :], src[:, 0:WT], ACT.Sigmoid).then_inc(in_evac.sem, 1)
                    if t == 0:
                        root(l, 3)
                a.wait_ge(gm_ready.sem, gm_ready.at(l, 1))
                a.activation(gcm[:, 2, :], gcm[:, 2, :], ACT.Exp, scale=-1.0).then_inc(em_ready.sem, 1)
                pair_rows(l, 0, 1)
                a.wait_ge(gt_mm.sem, gt_mm.at(l, 1))
                a.activation(gcol[:, :, :, :], ps[0][:, 0:64].rearrange("p (q t r) -> p q t r", q=2, t=4), ACT.Copy).then_inc(gc_ready.sem, 1)
                for c in range(2):
                    a.wait_ge(pool_mm.sem, pool_mm.at(l, c + 1))
                    if c == 0:
                        a.wait_ge(in_mm.sem, in_mm.at(l, 21 if l == 0 else 19))
                    a.activation(hT[:, c, 0:c1], ps[4 + c][:, 0:c1], ACT.Copy,
                                 scale=par[:, l, PB_PS + c:PB_PS + c + 1]).then_inc(pool_out.sem, 1)

                def row_root(n):
                    a.wait_ge(rss_ready.sem, rss_ready.at(l, n + 1))
                    g0 = 0 if n in tiles[l] else 8
                    a.activation(rowss[:, 1, g0:16], rowss[:, 0, g0:16], ACT.Sqrt).then_inc(rsq_ready.sem, 1)

                def row_out(n):
                    t, b = n, n % 2
                    g0 = 0 if t in tiles[l] else 1
                    if n >= 2:
                        a.wait_ge(tr_mm.sem, trs(n - 2)[-1])
                    if n == 0:
                        a.wait_ge(gc_ready.sem, gc_ready.at(l, 1))
                        a.wait_ge(pool_mm.sem, pool_mm.at(l, 2))
                    a.wait_ge(qk_mm.sem, qk_mm.at(l, n + 1))
                    if g0 == 0:
                        for f in range(2):
                            a.activation(rowbuf[:, b, 0, 4 * f:4 * f + 4, :],
                                         ps[0 + f][:, 0:384].rearrange("p (h d) -> p h d", h=4), ACT.Copy)
                    for f in range(2):
                        kv = ps[2 + f][:, :].rearrange("p (h d) -> p h d", h=4)
                        a.activation(vrow[:, t, 256 * f:256 * f + 256].rearrange("p (h d) -> p h d", h=4), kv[:, :, NOPE:], ACT.Copy)
                        a.activation(rowbuf[:, b, 1, 4 * f:4 * f + 4, 0:NOPE], kv[:, :, 0:NOPE], ACT.Copy)
                    link(a.activation(rowbuf[:, b, 1, :, NOPE:], zkr[:, t, :].unsqueeze(1).to_broadcast([P, HEADS, ROPE]), ACT.Copy))
                    a.activation(rowsq[:, g0 * 768:1536], rowbuf[:, b, g0:, :, :].rearrange("p g h d -> p (g h d)"),
                                 ACT.Square).then_inc(row_ready.sem, 1)

                def trs(n):
                    at = sum(4 if m in tiles[l] else 2 for m in range(n))
                    return [tr_mm.at(l, at + j + 1) for j in range(4 if n in tiles[l] else 2)]

                def tr_out(n):
                    what = [(1, f) for f in range(2)]
                    if n in tiles[l]:
                        what = [(0, f) for f in range(2)] + what
                    for (g_, f), v in zip(what, trs(n)):
                        a.wait_ge(tr_mm.sem, v)
                        dst = (qT, kT)[g_]
                        a.activation(dst[0:QK, 4 * f:4 * f + 4, n * P:(n + 1) * P],
                                     ps[4 + (v - 1) % 2][0:QK, :].rearrange("p (h j) -> p h j", h=4), ACT.Copy).then_inc(tr_evac.sem, 1)

                row_out(0)
                for n in range(4):
                    if n:
                        tr_out(n - 1)
                    row_root(n)
                    pair_rows(l, PAIRS_AT[n], PAIRS_AT[n + 1])
                    if n < 3:
                        row_out(n + 1)
                tr_out(3)

                units = mixer_units(l)

                def expo(i):
                    t, h = units[i]
                    k0 = 0 if t < 2 else SEQ
                    a.wait_ge(smax.sem, smax.at(l, i + 1))
                    if i >= 2:
                        a.wait_ge(pt_mm.sem, pt_mm.at(l, i - 1))
                    if i == 0:
                        a.wait_ge(tr_mm.sem, trs(3)[-1])
                    a.activation(prob[:, i % 2, k0:COLS], ps[i % 2][:, k0:COLS], ACT.Exp, scale=SCALE,
                                 bias=asm[:, i % 2, 1:2], accum_out=asm[:, i % 2, 2:3]).then_inc(e_done.sem, 1)

                def pt_out(i):
                    t, h = units[i]
                    j0 = 0 if t < 2 else 2
                    a.wait_ge(pt_mm.sem, pt_mm.at(l, i + 1))
                    if i >= 2:
                        a.wait_ge(pv_mm.sem, pv_mm.at(l, (i - 2) // 2 + 1) if (i - 2) % 2 else pv_mm.at(l, 1) if i == 2 else pv_mm.at(l, (i - 2) // 2 + 1))
                    a.activation(pt[:, i % 2, j0:, :], ps[2][:, j0 * P:].rearrange("p (j q) -> p j q", q=P), ACT.Copy).then_inc(pt_ready.sem, 1)

                mu = ml_units(l)

                def decay(i, e):
                    s, h = mu[i]
                    r = e * MH + h
                    u = 2 * i + e
                    a.wait_ge(marg_ready.sem, marg_ready.at(l, u + 1))
                    if u >= 2:
                        a.wait_ge(mP_ready.sem, mP_ready.at(l, u - 1))
                    for j in range(2):
                        c = 2 * s + j
                        ins = a.activation(mE[:, e, c, :], marg[:, e, j, :], ACT.Exp, bias=gcol[:, 0, c, r:r + 1])
                    if s == 0:
                        for c in (2, 3):
                            ins = a.activation(mE[:, e, c, :], marg[:, e, 2, :], ACT.Exp,
                                               bias=gcol[:, 0, c, r:r + 1])
                    ins.then_inc(mE_ready.sem, 1)

                def num_out(i):
                    s, h = mu[i]
                    a.wait_ge(num_mm.sem, num_mm.at(l, i + 1))
                    if s != mu[0][0] and h == 0:
                        a.wait_ge(hsq_ready.sem, hsq_ready.at(l, 1))
                    a.activation(numS[:, :, :, h, :], ps[7][:, 0:260].rearrange("p (q e d) -> p q e d", q=2, e=2),
                                 ACT.Copy).then_inc(num_evac.sem, 1)

                def head_norm(n):
                    a.wait_ge(hq_ready.sem, hq_ready.at(l, n + 1))
                    a.activation(hq, hs, ACT.Square).then_inc(hsq_ready.sem, 1)
                    a.wait_ge(hss_ready.sem, hss_ready.at(l, n + 1))
                    a.activation(mden[:, 1, 0:8], mden[:, 0, 0:8], ACT.Sqrt).then_inc(hrt_ready.sem, 1)

                def ml_out(n):
                    s = streams[l][n]
                    a.wait_ge(mt_mm.sem, mt_mm.at(l, n + 1))
                    a.activation(hT[:, 6:8, s * SEQ:(s + 1) * SEQ], ps[3][:, :].rearrange("p (c j) -> p c j", c=2), ACT.Copy).then_inc(mt_evac.sem, 1)

                nu = len(units)
                for i in range(nu + 4):
                    u, r = i // STEPS, i % STEPS
                    if i < nu:
                        expo(i)
                    if 2 <= i < nu + 2:
                        pt_out(i - 2)
                    if r == 1 and u:
                        num_out(u - 1)
                    if r in (1, 2) and u < len(mu):
                        decay(u, r - 1)
                    if r == 3 and u == MH and len(streams[l]) > 1:
                        head_norm(0)
                head_norm(len(streams[l]) - 1)
                for n in range(len(streams[l])):
                    ml_out(n)

                a.wait_ge(x_mid.sem, x_mid.at(l, 1))
                a.dma_start(subk[:, :, :], sk_in[l]).then_inc(skw, 16)
                for k in range(KC):
                    a.wait_ge(x_mid.sem, x_mid.at(l, k + 1))
                    sqn[l] += 1
                    i = sqn[l] + 21 * l
                    a.wait_ge(sq_used.sem, i - 2)
                    a.activation(sq[:, i % 2, 0:c1], xT[:, k, 0:c1], ACT.Square).then_inc(sq_ready.sem, 1)
                a.wait_ge(ms_ready.sem, ms_ready.at(l, 4))
                a.activation(rms[:, 0:c1], rms[:, 0:c1], ACT.Sqrt).then_inc(rt_ready.sem, 1)
                for k in range(KC):
                    a.wait_ge(hx_ready.sem, hx_ready.at(l, KC + k + 1))
                    for s in streams[l]:
                        ins = a.activation(hT[:, k, s * SEQ:(s + 1) * SEQ], hT[:, k, s * SEQ:(s + 1) * SEQ], ACT.Identity,
                                           scale=A2[:, k, s:s + 1], bias=modT[:, 24 + k, s:s + 1])
                    ins.then_inc(h_ready.sem, 1)
                def query(q):
                    a.wait_ge(pq_mm.sem, pq_mm.at(l, q + 1))
                    if q >= 2:
                        a.wait_ge(psc_mm.sem, psc_mm.at(l, q - 1))
                    a.activation(pq[:, q % 2, 0:c1], ps[q % 2][:, 0:c1], ACT.Copy).then_inc(pq_ready.sem, 1)

                def exponentials(n, h):
                    b = (n if l == 0 else 4 + n) % 2
                    o = h * PTOP
                    a.wait_ge(sub_ready.sem, sub_ready.at(l, n * PH + h + 1))
                    a.activation(bv[:, b, o:o + PTOP], bv[:, b, o:o + PTOP], ACT.Exp).then_inc(ex_ready.sem, 1)

                nt = len(tiles[l])

                def gelus(n, h, g0, g1):
                    at = ((n if l == 0 else 4 + n) * PH + h) * PTOP
                    with a.Fori(g0, g1) as i:
                        a.wait_ge(dotted, i * GROUP + (at + GROUP))
                        a.activation(gact[:, bass.ds(i * GROUP + h * PTOP, GROUP)], araw[:, bass.ds(i * GROUP + h * PTOP, GROUP)],
                                     ACT.Gelu).then_inc(gelu_ready, 1)

                query(0)
                query(1)
                for j in range(2 * len(tiles[l])):
                    a.wait_ge(hr_mm.sem, hr_mm.at(l, j + 1))
                    a.activation(hrow[:, j // 2, (j % 2) * 512:(j % 2) * 512 + 512], ps[4 + j % 2][:, :], ACT.Copy).then_inc(hr_ready.sem, 1)
                query(2)
                query(3)
                exponentials(0, 0)
                query(4)
                query(5)
                for n in range(nt):
                    for h in range(PH):
                        if n == 0:
                            gelus(n, h, 0, 2)
                        if h < PH - 1 or n < nt - 1:
                            exponentials(n + (h + 1) // PH, (h + 1) % PH)
                        if n:
                            gelus(n, h, 0, 8)
                        else:
                            gelus(n, h, 2, 4)
                            if h < PH - 3:
                                query(2 * h + 6)
                            gelus(n, h, 4, 8)
                            if h < PH - 3:
                                query(2 * h + 7)
                        if l == 0 and n == 1:
                            ada_rows(1, 3 * h, 3 * h + 3)
                    a.wait_ge(acc_done.sem, acc_done.at(l, n + 1))
                    if n:
                        a.wait_ge(yt_mm.sem, yt_mm.at(l, 2 * n))
                    a.activation(yrow, acc[:, :], ACT.Copy).then_inc(y_ready.sem, 1)

        @block.vector
        def _(v):
            steps = [0]

            def link(ins):
                steps[0] += 1
                ins.then_inc(dve_step, 1)
                v.wait_ge(dve_step, steps[0])

            def modulation(l, m0, m1, bank, scales):
                link(v.tensor_tensor(modT[:, m0:m1, :], bank[:, 2 * m0:2 * m1].rearrange("p (b s) -> p b s", s=2),
                                     par[:, l, PB_ADA + m0:PB_ADA + m1].unsqueeze(2).to_broadcast([P, m1 - m0, 2]), ALU.add))
                for A, sc, g_ in scales:
                    link(v.scalar_tensor_tensor(out=A[:, :, :], in0=modT[:, sc:sc + 8, :], scalar=1.0,
                                                in1=par[:, l, g_:g_ + 8].unsqueeze(2).to_broadcast([P, 8, 2]),
                                                op0=ALU.add, op1=ALU.mult))

            mix_scale, ff_scale = (A1, 8, PB_G1), (A2, 32, PB_G2)

            def inv_rms(l, i, width, c1):
                v.wait_ge(ss_ready.sem, ss_ready.at(l, i))
                v.tensor_scalar(rms[:, 0:c1], ps[0 if i != 3 else 1][:, 0:c1], 1.0 / width, EPS, ALU.mult, ALU.add).then_inc(ms_ready.sem, 1)
                v.wait_ge(rt_ready.sem, rt_ready.at(l, i))
                link(v.reciprocal(rms[:, 0:c1], rms[:, 0:c1]))

            v.memset(zrow[:, :], 0.0).then_inc(init_done, 1)

            for l in range(DEPTH):
                c1 = full[l][1]
                ns = len(streams[l])
                if l == 0:
                    v.wait_ge(con_loaded, 16)
                    v.wait_ge(loaded, 32)
                v.memset(pu[:, :, :, :], 0.0).then_inc(pad_done, 1)
                v.memset(v1[:, :, :, MD:MD + 1], 1.0)
                link(v.memset(ones8, 1.0))
                inv_rms(l, 1, D, COLS)
                for k in range(KC):
                    v.tensor_tensor(hT[:, k, :], xT[:, k, :], rms[:, :], ALU.mult).then_inc(hx_ready.sem, 1)
                if l == 0:
                    v.wait_ge(ada_tr.sem, ada_tr.at(0, ADA_FIRST))
                    modulation(0, 0, 16, ps[3], [mix_scale])
                    v.sem_inc(mod_ready.sem, 1)

                v.wait_ge(lnf_ready.sem, lnf_ready.at(l, 1))
                link(v.scalar_tensor_tensor(out=lf, in0=gf, scalar=0.0, in1=gt, op0=ALU.min, op1=ALU.subtract))
                xs, cs = slice(0, SEQ), slice(SEQ, COLS)
                v.tensor_tensor_scan(BB[:, ::-1], ones8[:, ::-1], lf[:, ::-1], 0.0, ALU.mult, ALU.add)
                link(v.tensor_tensor_scan(BF[:, cs], ones8[:, cs], lf[:, cs], 0.0, ALU.mult, ALU.add))
                link(v.tensor_tensor_scan(BF[:, xs], ones8[:, xs], lf[:, xs], BF[:, COLS - 1:COLS], ALU.mult, ALU.add))
                v.tensor_tensor(cB, gi, BB, ALU.subtract)
                link(v.tensor_tensor(cF, gi, BF, ALU.subtract))
                v.tensor_tensor_scan(MB[:, ::-1], cB[:, ::-1], cB[:, ::-1], NEG, ALU.max, ALU.max)
                link(v.tensor_tensor_scan(MF[:, cs], cF[:, cs], cF[:, cs], NEG, ALU.max, ALU.max))
                link(v.tensor_tensor_scan(MF[:, xs], cF[:, xs], cF[:, xs], MF[:, COLS - 1:COLS], ALU.max, ALU.max))
                v.tensor_tensor(BF, BF, MF, ALU.add)
                link(v.tensor_tensor(BB, BB, MB, ALU.add))
                for j, (f_, b_) in enumerate(((cF, cB), (MF, MB), (BF, BB))):
                    link(v.tensor_scalar(gu, b_, con[0:8, C_DIR + 1:C_DIR + 2], None, ALU.mult))
                    ins = v.scalar_tensor_tensor(out=gcm[:, j, :], in0=f_, scalar=con[0:8, C_DIR:C_DIR + 1], in1=gu,
                                                 op0=ALU.mult, op1=ALU.add)
                    link(ins)
                v.sem_inc(gm_ready.sem, 1)

                inv_rms(l, 2, QRANK, c1)
                for k in range(3):
                    ins = v.scalar_tensor_tensor(out=zqT[:, k, 0:c1], in0=zqT[:, k, 0:c1], scalar=par[:, l, PB_QN + k:PB_QN + k + 1],
                                                 in1=rms[:, 0:c1], op0=ALU.mult, op1=ALU.mult).then_inc(zn_ready.sem, 1)
                v.wait_ge(zn_ready.sem, zn_ready.at(l, 3))
                inv_rms(l, 3, KVRANK, COLS)
                for k in range(2):
                    v.scalar_tensor_tensor(out=zkvT[:, k, :], in0=zkvT[:, k, :], scalar=par[:, l, PB_KVN + k:PB_KVN + k + 1],
                                           in1=rms[:, :], op0=ALU.mult, op1=ALU.mult).then_inc(zn_ready.sem, 1)

                for n in range(4):
                    b = n % 2
                    g0 = 0 if n in tiles[l] else 1
                    gn = 2 - g0
                    v.wait_ge(row_ready.sem, row_ready.at(l, n + 1))
                    if n:
                        v.wait_ge(rsq_ready.sem, rsq_ready.at(l, n))
                    link(v.tensor_reduce(rowss[:, 0, 8 * g0:16], rowsq[:, g0 * 768:1536].rearrange("p (h d) -> p h d", d=QK), AX.X, ALU.add))
                    v.tensor_scalar(rowss[:, 0, 8 * g0:16], rowss[:, 0, 8 * g0:16], 1.0 / QK, EPS, ALU.mult, ALU.add).then_inc(rss_ready.sem, 1)
                    v.wait_ge(rsq_ready.sem, rsq_ready.at(l, n + 1))
                    link(v.reciprocal(rowss[:, 2, 8 * g0:16], rowss[:, 1, 8 * g0:16]))
                    rb = rowbuf[:, b, g0:, :, :].rearrange("p g h d -> p (g h) d")
                    link(v.tensor_tensor(rb, rb, rowss[:, 2, 8 * g0:16].unsqueeze(2).to_broadcast([P, 8 * gn, QK]), ALU.mult))
                    gains = par[:, l, PB_QG + g0 * QK:PB_QG + 2 * QK].rearrange("p (g d) -> p g d", d=QK)
                    rg = rowbuf[:, b, g0:, :, :]
                    link(v.tensor_tensor(rg, rg, gains.unsqueeze(2).to_broadcast([P, gn, HEADS, QK]), ALU.mult))
                    if n < 2:
                        H = 8 * gn
                        hf = ROPE // 2
                        x1, x2 = rb[:, :, NOPE:NOPE + hf], rb[:, :, NOPE + hf:QK]
                        cc = cos[:, n, :].unsqueeze(1).to_broadcast([P, H, hf])
                        ss = sin[:, n, :].unsqueeze(1).to_broadcast([P, H, hf])
                        v.tensor_tensor(rtmp[:, 0, 0:H, :], x1, cc, ALU.mult)
                        v.tensor_tensor(rtmp[:, 1, 0:H, :], x2, ss, ALU.mult)
                        v.tensor_tensor(rtmp[:, 2, 0:H, :], x2, cc, ALU.mult)
                        link(v.tensor_tensor(rtmp[:, 3, 0:H, :], x1, ss, ALU.mult))
                        v.tensor_tensor(x1, rtmp[:, 0, 0:H, :], rtmp[:, 1, 0:H, :], ALU.subtract)
                        link(v.tensor_tensor(x2, rtmp[:, 2, 0:H, :], rtmp[:, 3, 0:H, :], ALU.add))
                    v.sem_inc(rown_ready.sem, 1)

                units = mixer_units(l)

                def unit_max(i):
                    t, h = units[i]
                    k0 = 0 if t < 2 else SEQ
                    v.wait_ge(sc_mm.sem, sc_mm.at(l, i + 1))
                    link(v.tensor_reduce(asm[:, i % 2, 0:1], ps[i % 2][:, k0:COLS], AX.X, ALU.max))
                    v.tensor_scalar(asm[:, i % 2, 1:2], asm[:, i % 2, 0:1], -SCALE, None, ALU.mult).then_inc(smax.sem, 1)

                def unit_norm(i):
                    t, h = units[i]
                    k0 = 0 if t < 2 else SEQ
                    v.wait_ge(e_done.sem, e_done.at(l, i + 1))
                    link(v.reciprocal(asm[:, i % 2, 3:4], asm[:, i % 2, 2:3]))
                    v.tensor_scalar(prob[:, i % 2, k0:COLS], prob[:, i % 2, k0:COLS], asm[:, i % 2, 3:4], None, ALU.mult).then_inc(p_ready.sem, 1)

                def pair_out(j):
                    t, h = units[2 * j]
                    v.wait_ge(pv_mm.sem, pv_mm.at(l, j + 1))
                    v.tensor_copy(hT[:, 2 + h // 2, t * P:(t + 1) * P], ps[3][:, 0:P]).then_inc(attn_out.sem, 1)

                nu = len(units)
                if l == 0:
                    v.wait_ge(pair_tr.sem, PAIRS)
                    modulation(0, 16, 48, ps[7], [ff_scale])
                    v.sem_inc(rest_ready, 1)

                mu = ml_units(l)

                def masked(i, e):
                    u = 2 * i + e
                    if e == 0:
                        v.wait_ge(st_mm.sem, st_mm.at(l, i + 1))
                    if u >= 2:
                        v.wait_ge(mE_ready.sem, mE_ready.at(l, u - 1))
                    if mu[i][0] == 0:
                        v.tensor_scalar(marg[:, e, 2, :], ps[6][:, e * 256:e * 256 + 256], -1.0, None, ALU.mult)
                    v.tensor_tensor(marg[:, e, 0:2, :], mask[:, e, :, :],
                                    ps[6][:, e * 256:e * 256 + 256].unsqueeze(1).to_broadcast([P, 2, 256]),
                                    ALU.subtract).then_inc(marg_ready.sem, 1)

                def weighted(i, e):
                    s, h = mu[i]
                    u = 2 * i + e
                    v.wait_ge(mE_ready.sem, mE_ready.at(l, u + 1))
                    if i >= 1:
                        v.wait_ge(num_mm.sem, num_mm.at(l, i))
                    for j in ((0, 1) if s == 0 else (1,)):
                        ins = v.tensor_tensor(mP[:, e, 2 * j:2 * j + 2, :], mE[:, e, 2 * j:2 * j + 2, :],
                                              ps[4 + j][:, :].rearrange("p (c q) -> p c q", c=2), ALU.mult)
                    ins.then_inc(mP_ready.sem, 1)

                def combine(n):
                    s = streams[l][n]
                    v.wait_ge(num_evac.sem, num_evac.at(l, MH * (n + 1)))
                    den = numS[:, :, :, :, MD:MD + 1].rearrange("p q e h o -> p (q e h) o")
                    md = mden[:, :, :].unsqueeze(3)
                    link(v.scalar_tensor_tensor(out=md[:, 0, :, :], in0=den, scalar=-1.0, in1=den, op0=ALU.mult, op1=ALU.max))
                    link(v.tensor_tensor(mden[:, 0, :], mden[:, 0, :], gcol[:, 1, 2 * s:2 * s + 2, :].rearrange("p t r -> p (t r)"), ALU.max))
                    link(v.reciprocal(mden[:, 1, :], mden[:, 0, :]))
                    link(v.tensor_tensor(hn.rearrange("p q e h d -> p (q e h) d"), numS[:, :, :, :, 0:MD].rearrange("p q e h d -> p (q e h) d"),
                                         mden[:, 1, :].unsqueeze(2).to_broadcast([P, 16, MD]), ALU.mult))
                    v.tensor_tensor(hs, hn[:, :, 0, :, :], hn[:, :, 1, :, :], ALU.add).then_inc(hq_ready.sem, 1)
                    v.wait_ge(hsq_ready.sem, hsq_ready.at(l, n + 1))
                    link(v.tensor_reduce(mden[:, 0, 0:8], hq.rearrange("p q h d -> p (q h) d"), AX.X, ALU.add))
                    link(v.tensor_scalar(mden[:, 0, 0:8], mden[:, 0, 0:8], 1.0 / MD, EPS, ALU.mult, ALU.add))
                    v.sem_inc(hss_ready.sem, 1)
                    v.wait_ge(hrt_ready.sem, hrt_ready.at(l, n + 1))
                    link(v.reciprocal(mden[:, 2, 0:8], mden[:, 1, 0:8]))
                    h3 = hs.rearrange("p q h d -> p (q h) d")
                    link(v.tensor_tensor(h3, h3, mden[:, 2, 0:8].unsqueeze(2).to_broadcast([P, 8, MD]), ALU.mult))
                    h2 = hs.rearrange("p q h d -> p q (h d)")
                    link(v.tensor_tensor(h2, h2, par[:, l, PB_ML:PB_ML + MH * MD].unsqueeze(1).to_broadcast([P, 2, MH * MD]), ALU.mult))
                    if n:
                        v.wait_ge(mt_mm.sem, mt_mm.at(l, n))
                    v.tensor_tensor(osig[:, 2 * s:2 * s + 2, :], osig[:, 2 * s:2 * s + 2, :], h2, ALU.mult).then_inc(ml_ready.sem, 1)

                for i in range(nu + 4):
                    u, r = i // STEPS, i % STEPS
                    if i >= 5 and i % 2 == 1:
                        pair_out((i - 5) // 2)
                    if i < nu:
                        unit_max(i)
                    if 1 <= i <= nu:
                        unit_norm(i - 1)
                    if u < len(mu):
                        if r == 0:
                            masked(u, 0)
                            masked(u, 1)
                        if r >= 2:
                            weighted(u, r - 2)
                    if r == 3 and u == MH and len(streams[l]) > 1:
                        combine(0)
                combine(len(streams[l]) - 1)

                for k in range(KC):
                    v.wait_ge(out_mm.sem, out_mm.at(l, k + 1))
                    for s in streams[l]:
                        ins = v.scalar_tensor_tensor(out=xT[:, k, s * SEQ:(s + 1) * SEQ], in0=ps[4 + k % 2][:, s * SEQ:(s + 1) * SEQ],
                                                     scalar=modT[:, 16 + k, s:s + 1], in1=xT[:, k, s * SEQ:(s + 1) * SEQ],
                                                     op0=ALU.mult, op1=ALU.add)
                    ins.then_inc(x_mid.sem, 1)
                v.wait_ge(x_mid.sem, x_mid.at(l, KC))
                inv_rms(l, 4, D, c1)
                for k in range(KC):
                    v.tensor_tensor(hT[:, k, 0:c1], xT[:, k, 0:c1], rms[:, 0:c1], ALU.mult).then_inc(hx_ready.sem, 1)

                link(v.tensor_copy(gate_f[:, :, :], modT[:, 40:48, :]))

                def top_keys(q, ts):
                    v.wait_ge(psc_mm.sem, psc_mm.at(l, q + 1))
                    for t in ts:
                        sc = ps[2 + q % 2][:, t * P:(t + 1) * P]
                        tv, ti = topv[:, t, q, :], topiu[:, t, q, :]
                        link(v.max(tv[:, 0:8], sc))
                        v.max_index(ti[:, 0:8], tv[:, 0:8], sc)
                        link(v.match_replace(s2[:, 0:P], tv[:, 0:8], sc, NEG))
                        link(v.max(tv[:, 8:16], s2[:, 0:P]))
                        link(v.max_index(ti[:, 8:16], tv[:, 8:16], s2[:, 0:P]))
                    if ts[-1] == tiles[l][-1]:
                        v.sem_inc(top_done.sem, 1)

                def choose(n, h):
                    t = tiles[l][n]
                    b = (n if l == 0 else 4 + n) % 2
                    o = h * PTOP
                    cd = cand[:, 0:256]
                    c3 = cd.rearrange("p (i j) -> p i j", i=PTOP)
                    eq = cand[:, 256:768].rearrange("p (c s j) -> p c s j", c=2, s=PTOP)
                    tf = cand[:, 768:800].rearrange("p (c k) -> p c k", c=2)
                    v.tensor_copy(tf, topiu[:, t, 2 * h:2 * h + 2, :])
                    link(v.tensor_tensor(c3, topv[:, t, 2 * h, :].unsqueeze(2).to_broadcast([P, PTOP, PTOP]),
                                         topv[:, t, 2 * h + 1, :].unsqueeze(1).to_broadcast([P, PTOP, PTOP]), ALU.add))
                    best = bv[:, b, o:o + PTOP]
                    link(v.max(best[:, 0:8], cd))
                    v.max_index(bi[:, 0:8], best[:, 0:8], cd)
                    link(v.match_replace(s2[:, :], best[:, 0:8], cd, NEG))
                    link(v.max(best[:, 8:16], s2[:, :]))
                    link(v.max_index(bi[:, 8:16], best[:, 8:16], s2[:, :]))
                    rank = cand[:, 800:832]
                    rankI = rank.bitcast(I32)
                    biI = bi[:, 0:PTOP].bitcast(I32)
                    v.tensor_scalar(rankI[:, 0:16], biI, 4, None, ALU.arith_shift_right)
                    link(v.tensor_scalar(rankI[:, 16:32], biI, 15, None, ALU.bitwise_and))
                    link(v.tensor_copy(cand[:, 832:864], rankI))
                    link(v.tensor_tensor(eq, cand[:, 832:864].rearrange("p (c s) -> p c s", c=2).unsqueeze(3).to_broadcast([P, 2, PTOP, PTOP]),
                                         iota16.unsqueeze(1).unsqueeze(1).to_broadcast([P, 2, PTOP, PTOP]), ALU.is_equal))
                    link(v.tensor_tensor(eq, eq, tf.unsqueeze(2).to_broadcast([P, 2, PTOP, PTOP]), ALU.mult))
                    link(v.tensor_reduce(cand[:, 864:896], cand[:, 256:768].rearrange("p (s j) -> p s j", j=PTOP), AX.X, ALU.add))
                    link(v.scalar_tensor_tensor(out=idx[:, b, o:o + PTOP], in0=cand[:, 864:880], scalar=float(PKEYS), in1=cand[:, 880:896],
                                                op0=ALU.mult, op1=ALU.add))
                    v.sem_inc(idx_ready.sem, 1)
                    link(v.tensor_copy(esum[:, 0, 0:1], best[:, 0:1]))
                    v.tensor_scalar(best, best, esum[:, 0, 0:1], None, ALU.subtract).then_inc(sub_ready.sem, 1)

                def gates(n, h):
                    b = (n if l == 0 else 4 + n) % 2
                    o = h * PTOP
                    v.wait_ge(ex_ready.sem, ex_ready.at(l, n * PH + h + 1))
                    link(v.tensor_reduce(esum[:, 0, 1:2], bv[:, b, o:o + PTOP], AX.X, ALU.add))
                    link(v.reciprocal(esum[:, 1, 1:2], esum[:, 0, 1:2]))
                    link(v.tensor_scalar(wts[:, b, o:o + PTOP], bv[:, b, o:o + PTOP], esum[:, 1, 1:2], None, ALU.mult))

                def group(n, h, it, f):
                    tile = n if l == 0 else 4 + n
                    at = (tile * PH + h) * PTOP
                    for s in range(GROUP * f, GROUP * (f + 1)):
                        v.wait_ge(landed[s], it * 16 + (at // RING + 1) * 16)
                        v.scalar_tensor_tensor(out=ring[:, s, 0:D], in0=ring[:, s, 0:D], scalar=1.0, in1=hrow[:, tiles[l][n], :],
                                               op0=ALU.mult, op1=ALU.mult,
                                               accum_out=araw[:, bass.ds(it * RING + (h * PTOP + s), 1)]).then_inc(dotted, 1)
                    v.wait_ge(gelu_ready, it * (RING // GROUP) + (at // GROUP + f + 1))
                    for s in range(GROUP * f, GROUP * (f + 1)):
                        v.wait_ge(v_used, it * RING + (at + s + 1 + RING - DIAGS))
                        v.tensor_scalar(diag[:, s % DIAGS, :], ident, gact[:, bass.ds(it * RING + (h * PTOP + s), 1)],
                                        wts[:, tile % 2, bass.ds(it * RING + (h * PTOP + s), 1)], ALU.mult, ALU.mult).then_inc(diag_ready, 1)

                def add_experts(n):
                    t = tiles[l][n]
                    s = t // 2
                    for f in range(2):
                        v.wait_ge(yt_mm.sem, yt_mm.at(l, 2 * n + f + 1))
                        for j in range(4):
                            k = 4 * f + j
                            ins = v.scalar_tensor_tensor(out=xT[:, k, t * P:(t + 1) * P], in0=ps[4 + f][:, j * P:(j + 1) * P],
                                                         scalar=gate_f[:, k, s:s + 1], in1=xT[:, k, t * P:(t + 1) * P],
                                                         op0=ALU.mult, op1=ALU.add)
                            link(ins)
                    v.sem_inc(x_done.sem, 1)

                nt = len(tiles[l])
                top_keys(0, tiles[l][:1])
                top_keys(1, tiles[l][:1])
                choose(0, 0)
                for q in range(2):
                    top_keys(q, tiles[l][1:])
                for q in (2, 3):
                    top_keys(q, tiles[l])
                for n in range(nt):
                    v.wait_ge(hr_ready.sem, hr_ready.at(l, 2 * n + 2))
                    for h in range(PH):
                        gates(n, h)
                        more = h < PH - 1 or n < nt - 1
                        if n == 0:
                            group(n, h, 0, 0)
                            group(n, h, 0, 1)
                            if more:
                                choose((h + 1) // PH, (h + 1) % PH)
                            group(n, h, 0, 2)
                            group(n, h, 0, 3)
                            if h < PH - 2:
                                top_keys(2 * h + 4, tiles[l])
                            group(n, h, 1, 0)
                            group(n, h, 1, 1)
                            if h < PH - 2:
                                top_keys(2 * h + 5, tiles[l])
                            group(n, h, 1, 2)
                            group(n, h, 1, 3)
                        else:
                            if more:
                                choose(n + (h + 1) // PH, (h + 1) % PH)
                            with v.Fori(0, PTOP // RING) as it:
                                for f in range(RING // GROUP):
                                    group(n, h, it, f)
                        if h == 0 and n:
                            add_experts(n - 1)
                    if l == 0 and n == 1:
                        v.wait_ge(ada_tr.sem, ada_tr.at(1, ADA_TILES))
                        modulation(1, 0, 48, ps[3], [mix_scale, ff_scale])
                        v.sem_inc(mod_ready.sem, 1)
                add_experts(nt - 1)

        @block.tensor
        def _(p):
            def tile_in(n):
                p.wait_ge(w_landed[n % WSLOTS], 16 * (n // WSLOTS + 1))
                return wring[:, n % WSLOTS, :, :]

            def ada_tiles(l, j0, j1):
                def turn(j):
                    p.wait_ge(ada_row.sem, ada_row.at(l, j + 1))
                    for b in range(2):
                        mm = p.transpose(ps[3][:, (2 * j + b) * 2:(2 * j + b) * 2 + 2], modrow[:, j % 2, b * P:(b + 1) * P], ident[0:2, 0:2])
                    mm.then_inc(ada_tr.sem, 1)

                for j in range(j0, j1):
                    wt = tile_in(l * LAYER_TILES + j)
                    if j - j0 >= 2:
                        p.wait_ge(ada_row.sem, ada_row.at(l, j - 1))
                    for k in range(KC):
                        mm = p.matmul(ps[4 + j % 2][0:2, 0:WT], cS[:, k, :], wt[:, k, :], start=(k == 0), stop=(k == KC - 1))
                    mm.then_inc(ada_mm.sem, 1)
                    if j > j0:
                        turn(j - 1)
                    p.wait_ge(ada_mm.sem, ada_mm.at(l, j + 1))
                    p.sem_inc(w_free, 1)
                turn(j1 - 1)

            sqn = [0]

            def sum_squares(l, n, bank, c1, sig):
                for k in range(n):
                    sqn[0] += 1
                    p.wait_ge(sq_ready.sem, sqn[0])
                    mm = p.matmul(ps[bank][:, 0:c1], ones, sq[:, sqn[0] % 2, 0:c1], start=(k == 0), stop=(k == n - 1)).then_inc(sq_used.sem, 1)
                p.wait_ge(sq_used.sem, sqn[0])
                p.sem_inc(ss_ready.sem, 1)

            p.sem_inc(w_free, WSLOTS)
            p.wait_ge(cs_ready, 1)
            p.wait_ge(con_loaded, 16)
            def pair_turn(q):
                p.wait_ge(pair_row.sem, q + 1)
                for b in range(4):
                    o = 2 * (2 * ADA_FIRST + 4 * q + b)
                    mm = p.transpose(ps[7][:, o:o + 2], pairrow[:, b * P:(b + 1) * P], ident[0:2, 0:2])
                mm.then_inc(pair_tr.sem, 1)

            def ada_pairs(l, q0, q1):
                if l == 0:
                    for q in range(q0, q1):
                        if q:
                            pair_turn(q - 1)
                        for f in range(2):
                            wt = tile_in(ADA_FIRST + IN_TILES + 2 * q + f)
                            for k in range(KC):
                                mm = p.matmul(ps[6][0:2, f * WT:(f + 1) * WT], cS[:, k, :], wt[:, k, :], start=(k == 0), stop=(k == KC - 1))
                        mm.then_inc(pair_mm.sem, 1)
                        p.wait_ge(pair_mm.sem, q + 1)
                        p.sem_inc(w_free, 2)

            ada_tiles(0, 0, ADA_FIRST // 2)
            sum_squares(0, KC, 0, COLS, 1)
            ada_tiles(0, ADA_FIRST // 2, ADA_FIRST)
            for l in range(DEPTH):
                c1 = full[l][1]
                ns = len(streams[l])
                base = ADA_FIRST if l == 0 else LAYER_TILES + ADA_TILES
                out_base = l * LAYER_TILES + ADA_TILES + IN_TILES
                query_base = out_base + OUT_TILES
                if l:
                    sum_squares(l, KC, 0, COLS, 1)

                g = [0]

                def group():
                    g[0] += 1
                    if g[0] > 2:
                        p.wait_ge(in_evac.sem, in_evac.at(l, g[0] - 2))
                    return ps[2 + g[0] % 2]

                for b in range(12):
                    if b % 2 == 0:
                        wt = tile_in(base + b // 2)
                    dst = group()
                    n = c1 if (b < 5 or 7 <= b < 9) else COLS
                    m = P if b < 11 else 64 + ROPE
                    o = (b % 2) * P
                    for k in range(KC):
                        if b == 0:
                            p.wait_ge(h_ready.sem, h_ready.at(l, k + 1))
                        mm = p.matmul(dst[0:m, 0:n], wt[:, k, o:o + m], hT[:, k, 0:n], start=(k == 0), stop=(k == KC - 1))
                    mm.then_inc(in_mm.sem, 1)
                    if b % 2 == 1:
                        p.wait_ge(in_mm.sem, in_mm.at(l, g[0]))
                        p.sem_inc(w_free, 1)
                for j in range(2):
                    wt = tile_in(base + 6 + j)
                    for t in (range(4) if j == 0 else tiles[l]):
                        dst = group()
                        for k in range(KC):
                            mm = p.matmul(dst[:, 0:WT], hT[:, k, t * P:(t + 1) * P], wt[:, k, :], start=(k == 0), stop=(k == KC - 1))
                        mm.then_inc(in_mm.sem, 1)
                    if j == 0:
                        sum_squares(l, 3, 0, c1, 2)
                        sum_squares(l, 2, 1, COLS, 3)
                        dst = group()
                        for t in range(4):
                            mm = p.transpose(dst[:, t * ROPE:(t + 1) * ROPE], zkc[64:64 + ROPE, t * P:(t + 1) * P], ident[64:64 + ROPE, 64:64 + ROPE])
                        mm.then_inc(in_mm.sem, 1)
                    p.wait_ge(in_mm.sem, in_mm.at(l, g[0]))
                    p.sem_inc(w_free, 1)

                ada_pairs(l, 0, 1)

                p.wait_ge(gm_ready.sem, gm_ready.at(l, 1))
                p.wait_ge(em_ready.sem, em_ready.at(l, 1))
                p.wait_ge(ms_ready.sem, ms_ready.at(l, 2))
                for q, j in ((0, 0), (1, 2)):
                    for t in range(4):
                        mm = p.transpose(ps[0][:, q * 32 + t * 8:q * 32 + t * 8 + 8], gcm[:, j, t * P:(t + 1) * P], ident[0:8, 0:8])
                mm.then_inc(gt_mm.sem, 1)

                p.wait_ge(mixw, 48 * (l + 1))
                p.wait_ge(pool_ready.sem, pool_ready.at(l, 1))
                if l == 0:
                    p.wait_ge(mod_ready.sem, 1)
                for c in range(2):
                    for f in range(2):
                        mm = p.matmul(ps[4 + c][64 * f:64 * f + 64, 0:c1], poolw[64 * f:64 * f + 64, c, :],
                                      pa_[64 * f:64 * f + 64, c, 0:ns, PAD:PAD + SEQ], start=True, stop=True)
                    mm.then_inc(pool_mm.sem, 1)

                def trs(n):
                    at = sum(4 if m in tiles[l] else 2 for m in range(n))
                    return [tr_mm.at(l, at + j + 1) for j in range(4 if n in tiles[l] else 2)]

                def qk_rows(n):
                    if n == 0:
                        p.wait_ge(zn_ready.sem, zn_ready.at(l, 5))
                        p.wait_ge(gc_ready.sem, gc_ready.at(l, 1))
                        p.wait_ge(in_evac.sem, in_evac.at(l, 21 if l == 0 else 19))
                    else:
                        p.wait_ge(row_ready.sem, row_ready.at(l, n))
                    if n in tiles[l]:
                        for f in range(2):
                            for k in range(3):
                                p.matmul(ps[f][:, 0:384], zqT[:, k, n * P:(n + 1) * P], uqw[:, k, f * 384:(f + 1) * 384], start=(k == 0), stop=(k == 2))
                    for f in range(2):
                        for k in range(2):
                            mm = p.matmul(ps[2 + f][:, :], zkvT[:, k, n * P:(n + 1) * P], ukvw[:, k, f * 512:(f + 1) * 512], start=(k == 0), stop=(k == 1))
                    mm.then_inc(qk_mm.sem, 1)

                def row_transposes(n):
                    p.wait_ge(rown_ready.sem, rown_ready.at(l, n + 1))
                    if n == 0:
                        p.wait_ge(pool_out.sem, pool_out.at(l, 2))
                    what = [(1, f) for f in range(2)]
                    if n in tiles[l]:
                        what = [(0, f) for f in range(2)] + what
                    for (g_, f), val in zip(what, trs(n)):
                        if val - 2 > tr_mm.start[l]:
                            p.wait_ge(tr_evac.sem, val - 2)
                        for j in range(4):
                            mm = p.transpose(ps[4 + (val - 1) % 2][0:QK, j * P:(j + 1) * P], rowbuf[:, n % 2, g_, 4 * f + j, :], ident)
                        mm.then_inc(tr_mm.sem, 1)

                for n in range(4):
                    qk_rows(n)
                    if n:
                        row_transposes(n - 1)
                    ada_pairs(l, PAIRS_AT[n], PAIRS_AT[n + 1])
                row_transposes(3)
                if l == 0:
                    pair_turn(PAIRS - 1)

                units = mixer_units(l)
                nu = len(units)

                def scores(i):
                    t, h = units[i]
                    k0 = 0 if t < 2 else SEQ
                    if i == 0:
                        p.wait_ge(tr_evac.sem, trs(3)[-1])
                    if i >= 2:
                        p.wait_ge(e_done.sem, e_done.at(l, i - 1))
                    p.matmul(ps[i % 2][:, k0:COLS], qT[0:QK, h, t * P:(t + 1) * P], kT[0:QK, h, k0:COLS], start=True, stop=True).then_inc(sc_mm.sem, 1)

                def prob_transposes(i):
                    t, h = units[i]
                    p.wait_ge(p_ready.sem, p_ready.at(l, i + 1))
                    if i >= 1:
                        p.wait_ge(pt_ready.sem, pt_ready.at(l, i))
                    for j in range(0 if t < 2 else 2, 4):
                        mm = p.transpose(ps[2][:, j * P:(j + 1) * P], prob[:, i % 2, j * P:(j + 1) * P], ident)
                    mm.then_inc(pt_mm.sem, 1)

                def outputs(i):
                    t, h = units[i]
                    j_ = i // 2
                    p.wait_ge(pt_ready.sem, pt_ready.at(l, i + 1))
                    if i % 2 == 0 and j_ >= 1:
                        p.wait_ge(attn_out.sem, attn_out.at(l, j_))
                    f = h % 2
                    js = range(0 if t < 2 else 2, 4)
                    for j in js:
                        mm = p.matmul(ps[3][64 * f:64 * f + 64, 0:P], vrow[:, j, h * VD:(h + 1) * VD], pt[:, i % 2, j, :],
                                      start=(j == js[0]), stop=(j == 3))
                    if f:
                        mm.then_inc(pv_mm.sem, 1)

                mu = ml_units(l)

                def state_scores(i):
                    s, h = mu[i]
                    f, c = h % 2, h // 2
                    if i:
                        p.wait_ge(mP_ready.sem, mP_ready.at(l, 2 * i))
                    for kc in (range(4) if s == 0 else (2, 3)):
                        p.matmul(ps[4 + kc // 2][:, (kc % 2) * 256:(kc % 2) * 256 + 256],
                                 mkT[64 * f:64 * f + 64, c, kc * P:(kc + 1) * P], mqT[64 * f:64 * f + 64, c, s * SEQ:(s + 1) * SEQ],
                                 start=True, stop=True)
                    for e in range(DIRS):
                        r = e * MH + h
                        mm = p.matmul(ps[6][:, e * 256:e * 256 + 256], ident[0:8, r:r + 1].to_broadcast([8, P]),
                                      gcm[:, 1, s * SEQ:(s + 1) * SEQ], start=True, stop=True)
                    mm.then_inc(st_mm.sem, 1)

                def numerators(i):
                    s, h = mu[i]
                    if l == 0 and i == 0:
                        p.wait_ge(rest_ready, 1)
                    p.wait_ge(mP_ready.sem, mP_ready.at(l, 2 * i + 2))
                    if i:
                        p.wait_ge(num_evac.sem, num_evac.at(l, i))
                    for e in range(DIRS):
                        for q in range(2):
                            o = (q * 2 + e) * (MD + 1)
                            kcs = [c for c in range(2 * s, 4) if c != 2 * s + 1 - e or q != e]
                            for kc in kcs:
                                mm = p.matmul(ps[7][:, o:o + MD + 1], mP[:, e, kc, q * P:(q + 1) * P], v1[:, kc, h, :],
                                              start=(kc == kcs[0]), stop=(kc == kcs[-1]))
                    mm.then_inc(num_mm.sem, 1)

                def ml_transposes(n):
                    s = streams[l][n]
                    p.wait_ge(ml_ready.sem, ml_ready.at(l, n + 1))
                    if n:
                        p.wait_ge(mt_evac.sem, mt_evac.at(l, n))
                    for c in range(2):
                        for q in range(2):
                            mm = p.transpose(ps[3][:, c * SEQ + q * P:c * SEQ + (q + 1) * P], osig[:, 2 * s + q, c * P:(c + 1) * P], ident)
                    mm.then_inc(mt_mm.sem, 1)

                for i in range(nu + 4):
                    u = i // STEPS
                    if i < nu:
                        scores(i)
                    if 2 <= i < nu + 2:
                        prob_transposes(i - 2)
                    if 3 <= i < nu + 3:
                        outputs(i - 3)
                    if i % STEPS == 0:
                        if u:
                            numerators(u - 1)
                        if u < len(mu):
                            state_scores(u)
                p.wait_ge(attn_out.sem, attn_out.at(l, nu // 2))
                for n in range(len(streams[l])):
                    ml_transposes(n)

                for b in range(8):
                    if b % 2 == 0:
                        wt = tile_in(out_base + b // 2)
                    if b == 0:
                        p.wait_ge(mt_evac.sem, mt_evac.at(l, len(streams[l])))
                        p.wait_ge(marg_ready.sem, marg_ready.at(l, 2 * len(mu)))
                    if b >= 2:
                        p.wait_ge(x_mid.sem, x_mid.at(l, b - 1))
                    for k in range(KC):
                        mm = p.matmul(ps[4 + b % 2][:, 0:c1], wt[:, k, (b % 2) * P:(b % 2 + 1) * P], hT[:, k, 0:c1], start=(k == 0), stop=(k == KC - 1))
                    mm.then_inc(out_mm.sem, 1)
                    if b % 2:
                        p.wait_ge(out_mm.sem, out_mm.at(l, b + 1))
                        p.sem_inc(w_free, 1)
                sum_squares(l, KC, 0, c1, 4)

                def query(q):
                    if q % 2 == 0:
                        tile_in(query_base + q // 2)
                    wt = wring[:, (query_base + q // 2) % WSLOTS, :, :]
                    if q == 0:
                        p.wait_ge(ms_ready.sem, ms_ready.at(l, 4))
                    if q >= 2:
                        p.wait_ge(pq_ready.sem, pq_ready.at(l, q - 1))
                    for k in range(KC):
                        if q == 0:
                            p.wait_ge(h_ready.sem, h_ready.at(l, KC + k + 1))
                        mm = p.matmul(ps[q % 2][:, 0:c1], wt[:, k, (q % 2) * P:(q % 2 + 1) * P], hT[:, k, 0:c1], start=(k == 0), stop=(k == KC - 1))
                    mm.then_inc(pq_mm.sem, 1)
                    if q % 2:
                        p.wait_ge(pq_mm.sem, pq_mm.at(l, q + 1))
                        p.sem_inc(w_free, 1)

                def key_scores(q):
                    p.wait_ge(pq_ready.sem, pq_ready.at(l, q + 1))
                    if q == 0:
                        p.wait_ge(skw, 16 * (l + 1))
                    if q >= 2:
                        p.wait_ge(top_done.sem, top_done.at(l, q - 1))
                    for t in tiles[l]:
                        mm = p.matmul(ps[2 + q % 2][:, t * P:(t + 1) * P], pq[:, q % 2, t * P:(t + 1) * P], subk[:, q, :], start=True, stop=True)
                    mm.then_inc(psc_mm.sem, 1)

                nt = len(tiles[l])

                def turn_sums(n):
                    p.wait_ge(y_ready.sem, y_ready.at(l, n + 1))
                    if n:
                        p.wait_ge(x_done.sem, x_done.at(l, n))
                    for f in range(2):
                        for j in range(4):
                            mm = p.transpose(ps[4 + f][:, j * P:(j + 1) * P], yrow[:, (4 * f + j) * P:(4 * f + j + 1) * P], ident)
                        mm.then_inc(yt_mm.sem, 1)

                def sums(tile, h, it, f0, f1):
                    at = (tile * PH + h) * PTOP
                    for s in range(f0 * GROUP, f1 * GROUP):
                        p.wait_ge(diag_ready, it * RING + (at + s + 1))
                        for f in range(2):
                            mm = p.matmul(acc[:, f * 512:f * 512 + 512], diag[:, s % DIAGS, :], ring[:, s, D + f * 512:D + f * 512 + 512],
                                          start=False, stop=False, skip_group_check=True)
                        mm.then_inc(v_used, 1)

                query(0)
                query(1)
                key_scores(0)
                key_scores(1)
                for j in range(2 * len(tiles[l])):
                    t, f = j // 2, j % 2
                    if j < 2:
                        p.wait_ge(x_mid.sem, x_mid.at(l, KC))
                        p.wait_ge(h_ready.sem, h_ready.at(l, 2 * KC))
                    else:
                        p.wait_ge(hr_ready.sem, hr_ready.at(l, j - 1))
                    for k in range(4):
                        mm = p.transpose(ps[4 + j % 2][:, k * P:(k + 1) * P], hT[:, 4 * f + k, t * P:(t + 1) * P], ident)
                    mm.then_inc(hr_mm.sem, 1)

                query(2)
                query(3)
                key_scores(2)
                key_scores(3)
                query(4)
                query(5)
                for n in range(nt):
                    tile = n if l == 0 else 4 + n
                    if n:
                        turn_sums(n - 1)
                    if tile == 0:
                        p.wait_ge(init_done, 1)
                    for f in range(2):
                        p.matmul(acc[:, f * 512:f * 512 + 512], zrow[0:1, :], con[0:1, 0:512], start=True, stop=False, skip_group_check=True)
                    for h in range(PH):
                        if n == 0:
                            if h < PH - 2:
                                key_scores(2 * h + 4)
                                key_scores(2 * h + 5)
                            sums(tile, h, 0, 0, 2)
                            if h < PH - 3:
                                query(2 * h + 6)
                            sums(tile, h, 0, 2, 4)
                            sums(tile, h, 1, 0, 2)
                            if h < PH - 3:
                                query(2 * h + 7)
                            sums(tile, h, 1, 2, 4)
                        else:
                            with p.Fori(0, PTOP // RING) as it:
                                sums(tile, h, it, 0, RING // GROUP)
                        if l == 0 and n == 1:
                            if h == 0:
                                p.wait_ge(x_done.sem, x_done.at(l, 1))
                            ada_tiles(1, 3 * h, 3 * h + 3)
                    for f in range(2):
                        mm = p.matmul(acc[:, f * 512:f * 512 + 512], zrow[0:1, :], con[0:1, 0:512], start=False, stop=True, skip_group_check=True)
                    mm.then_inc(acc_done.sem, 1)
                turn_sums(nt - 1)


def constants():
    con = np.zeros((P, CB), np.float32)
    con[:, C_ID:C_ID + P] = np.eye(P)
    con[:, C_ONE:C_ONE + P] = 1.0
    key = np.arange(256)[:, None]
    query = np.arange(256)[None, :]
    allowed = (query >= key, query <= key)
    for e in range(2):
        m = np.where(allowed[e], 0.0, NEG)
        for k in range(2):
            o = C_MASK + (e * 2 + k) * 256
            con[:, o:o + 256] = m[k * P:(k + 1) * P]
    t = np.arange(SEQ)
    for g, w in enumerate(WINDOWS):
        n = np.clip(t + w // 2, 0, SEQ) - np.clip(t - w // 2, 0, SEQ)
        o = C_INV + (g // 2) * 256
        con[(g % 2) * 64:(g % 2) * 64 + 64, o:o + 256] = 1.0 / n
    per = ROPE // 2
    freqs = np.float32(ROPE_BASE) ** (-np.arange(0, per, 2, dtype=np.float32) / np.float32(per))
    row = (t // GRID_W).astype(np.float32)
    col = (t % GRID_W).astype(np.float32)
    ang = np.concatenate([row[:, None] * freqs, col[:, None] * freqs], axis=-1)
    con[:, C_COS:C_COS + 32] = np.cos(ang).reshape(2, P, 16).transpose(1, 0, 2).reshape(P, 32)
    con[:, C_SIN:C_SIN + 32] = np.sin(ang).reshape(2, P, 16).transpose(1, 0, 2).reshape(P, 32)
    con[0:4, C_DIR] = 1.0
    con[4:8, C_DIR + 1] = 1.0
    con[:, C_IOTA:C_IOTA + 16] = np.arange(16)
    return con


def kernel(**inputs):
    import concourse.bacc as _bacc
    from concourse.bass_utils import run_bass_kernel_spmd as _run

    i = {k: np.asarray(v) for k, v in inputs.items()}
    f32 = np.float32

    def chan(a, n):
        return a.reshape(n, P).T

    x_in = np.concatenate([i["x"][0], i["ctx"][0]], axis=0).T.reshape(KC, P, COLS).transpose(1, 0, 2)
    c_in = np.stack([i["c"][0], i["c_ctx"]], axis=-1).reshape(KC, P, 2).transpose(1, 0, 2)
    par = np.zeros((P, DEPTH, PB), f32)
    tiles = np.zeros((DEPTH, LAYER_TILES, P, KC, WT), f32)
    for l in range(DEPTH):
        par[:, l, PB_ADA:PB_ADA + 48] = chan(i["b_ada"][l], 48)
        par[:, l, PB_G1:PB_G1 + 8] = chan(i["norm1_gain"][l], 8)
        par[:, l, PB_G2:PB_G2 + 8] = chan(i["norm2_gain"][l], 8)
        par[:, l, PB_PS:PB_PS + 2] = chan(i["pool_scale"][l], 2)
        par[:, l, PB_QN:PB_QN + 3] = chan(i["mla_q_norm"][l], 3)
        par[:, l, PB_KVN:PB_KVN + 2] = chan(i["mla_kv_norm"][l], 2)
        gb = i["ml_gate_bias"][l].reshape(4, MH)
        par[0:4, l, PB_GI], par[4:8, l, PB_GI] = gb[0], gb[2]
        par[0:4, l, PB_GF], par[4:8, l, PB_GF] = gb[1], gb[3]
        par[:, l, PB_QG:PB_QG + QK] = i["q_norm"][l]
        par[:, l, PB_KG:PB_KG + QK] = i["k_norm"][l]
        par[:, l, PB_ML:PB_ML + MH * MD] = i["ml_out_norm"][l].reshape(-1)
        w = i["w_in"][l]
        wi = np.zeros((D, IN_TILES * WT), f32)
        wi[:, 0:896] = w[:, 0:896]
        wi[:, 896:1408] = w[:, 928:1440]
        g = w[:, 1952:1968].reshape(D, 4, MH)
        wi[:, 1408:1412], wi[:, 1412:1416] = g[:, 0], g[:, 2]
        wi[:, 1440:1444], wi[:, 1444:1448] = g[:, 1], g[:, 3]
        wi[:, 1472:1504] = w[:, 896:928]
        wi[:, 1536:2048] = w[:, 1440:1952]
        at = 0
        ada, c = i["w_ada"][l], ADA_FIRST * WT
        for m in ((ada[:, :c], wi, ada[:, c:]) if l == 0 else (ada, wi)) + (i["w_out"][l], i["peer_wq"][l]):
            n = m.shape[1] // WT
            tiles[l, at:at + n] = m.reshape(KC, P, n, WT).transpose(2, 1, 0, 3)
            at += n
    uq = i["w_uq"].reshape(DEPTH, 3, P, 768).transpose(0, 2, 1, 3)
    ukv = i["w_ukv"].reshape(DEPTH, 2, P, 1024).transpose(0, 2, 1, 3)
    pw = i["pool_w"].reshape(DEPTH, 2, 2 * PGROUP, PGROUP).transpose(0, 2, 1, 3)
    sk = i["peer_subkeys"].reshape(DEPTH, HC, PKEYS, PDK).transpose(0, 3, 1, 2)

    nc = _bacc.Bacc("TRN2", target_bir_lowering=False, num_devices=1)
    arrays = {}

    def put(name, a):
        a = np.ascontiguousarray(a)
        arrays[name + "_dram"] = a
        return nc.dram_tensor(name + "_dram", a.shape, mybir.dt.from_np(a.dtype), kind="ExternalInput").ap()

    args = [put("x", x_in), put("c", c_in), put("par", par), put("con", constants()),
            put("w", tiles.reshape(DEPTH * LAYER_TILES, P, KC * WT)), put("uq", uq), put("ukv", ukv), put("pw", pw), put("sk", sk)]
    args.append([put(f"uv{l}", np.concatenate([i["peer_u"][l], i["peer_v"][l]], axis=1)) for l in range(DEPTH)])
    args.append(nc.dram_tensor("out_dram", (P, KC, SEQ), F32, kind="ExternalOutput").ap())
    build(nc, *args)
    r = _run(nc, [arrays], core_ids=[0])
    return np.ascontiguousarray(r.results[0]["out_dram"].transpose(2, 1, 0)).reshape(1, SEQ, D)
```
